# Optimizing a Trainium2 kernel written in Bass

```python
import jax, jax.numpy as jnp
from jax import lax
import numpy as np

D_MODEL = 2048
BATCH = 1
SEQ = 256
DEPTH = 1

PLE_DIM = 256
MIX_WIDTH = D_MODEL // 2
CHUNK = 64
EPS = 1e-6
GLA_HEADS = 4
GLA_DK = MIX_WIDTH // 8
GLA_DV = MIX_WIDTH // GLA_HEADS
GLA_LORA = 16
GLA_GATE_NORMALIZER = 16.0
RWKV_HEAD = 64
RWKV_HEADS = MIX_WIDTH // RWKV_HEAD
RWKV_W_LORA = 64
RWKV_A_LORA = 64
RWKV_V_LORA = 32
RWKV_G_LORA = 160
RWKV_GN_EPS = 64e-5
RET_HEADS = 4
RET_DK = MIX_WIDTH // 8
RET_DV = MIX_WIDTH // RET_HEADS
ROPE_BASE = 10000.0
D_FF = 5504
CONV_W = 3

GLA_QK = GLA_HEADS * GLA_DK
GLA_SPLITS = (GLA_QK, 2 * GLA_QK, 2 * GLA_QK + MIX_WIDTH, 2 * GLA_QK + 2 * MIX_WIDTH)
GLA_COLS = 2 * GLA_QK + 2 * MIX_WIDTH + GLA_LORA
RWKV_SPLITS = (MIX_WIDTH, 2 * MIX_WIDTH, 3 * MIX_WIDTH, 3 * MIX_WIDTH + RWKV_W_LORA,
               3 * MIX_WIDTH + RWKV_W_LORA + RWKV_A_LORA)
RWKV_COLS = 3 * MIX_WIDTH + RWKV_W_LORA + RWKV_A_LORA + RWKV_G_LORA
RET_QK = RET_HEADS * RET_DK
RET_SPLITS = (RET_QK, 2 * RET_QK, 2 * RET_QK + MIX_WIDTH)
RET_COLS = 2 * RET_QK + 2 * MIX_WIDTH
GATE_COLS = 3 * D_MODEL
IN_SPLITS = (GLA_COLS, GLA_COLS + RWKV_COLS, GLA_COLS + RWKV_COLS + RET_COLS)
N_IN = GLA_COLS + RWKV_COLS + RET_COLS + GATE_COLS

kernel_name = "hybrid_gla_rwkv7_retnet_gated_block"

def rmsnorm(x, gain, eps=EPS):
    xf = x.astype(jnp.float32)
    y = xf * lax.rsqrt(jnp.mean(xf * xf, axis=-1, keepdims=True) + eps)
    return (y * gain.astype(jnp.float32)).astype(x.dtype)

def head_rmsnorm(x, eps=EPS):
    return x * lax.rsqrt(jnp.mean(x * x, axis=-1, keepdims=True) + eps)

def to_chunks(t):
    b, t_len, h, d = t.shape
    return t.reshape(b, t_len // CHUNK, CHUNK, h, d).transpose(1, 0, 3, 2, 4)

def from_chunks(t):
    n, b, h, c, d = t.shape
    return t.transpose(1, 0, 3, 2, 4).reshape(b, n * c, h, d)

def token_shift(u, mu):
    prev = jnp.pad(u, ((0, 0), (1, 0), (0, 0)))[:, :-1]
    return u + (prev - u) * mu

def rotary(x, positions):
    d = x.shape[-1]
    inv_freq = ROPE_BASE ** (-jnp.arange(0, d, 2, dtype=jnp.float32) / d)
    ang = positions.astype(jnp.float32)[:, :, None, None] * inv_freq
    cos, sin = jnp.cos(ang), jnp.sin(ang)
    x1, x2 = jnp.split(x, 2, axis=-1)
    return jnp.concatenate([x1 * cos - x2 * sin, x1 * sin + x2 * cos], axis=-1)

def gla_chunked(q, k, v, log_a):
    b_, _, h_, dk = q.shape
    dv = v.shape[-1]
    qc, kc, vc, gc = map(to_chunks, (q, k, v, log_a))
    cum = jnp.cumsum(gc, axis=3)
    cum_last = cum[:, :, :, -1:, :]
    q_in = qc * jnp.exp(cum)
    k_in = kc * jnp.exp(-cum)
    k_st = kc * jnp.exp(cum_last - cum)
    causal = jnp.tril(jnp.ones((CHUNK, CHUNK), dtype=bool))
    scores = jnp.where(causal, jnp.einsum('nbhid,nbhjd->nbhij', q_in, k_in), 0.0)
    o_intra = jnp.einsum('nbhij,nbhjv->nbhiv', scores, vc)

    def step(state, xs):
        q_c, k_c, v_c, dec_c = xs
        o = jnp.einsum('bhid,bhdv->bhiv', q_c, state)
        state = state * dec_c[:, :, 0, :, None] + jnp.einsum('bhjd,bhjv->bhdv', k_c, v_c)
        return state, o

    s0 = jnp.zeros((b_, h_, dk, dv), jnp.float32)
    _, o_inter = lax.scan(step, s0, (q_in, k_st, vc, jnp.exp(cum_last)))
    return from_chunks(o_intra + o_inter)

def rwkv7_scan(r, w, k, v, a, b):
    b_, _, h_, n_ = r.shape

    def step(state, xs):
        r_t, w_t, k_t, v_t, a_t, b_t = xs
        sa = jnp.einsum('bhvk,bhk->bhv', state, a_t)
        state = (state * w_t[:, :, None, :] + sa[..., None] * b_t[:, :, None, :]
                 + v_t[..., None] * k_t[:, :, None, :])
        return state, jnp.einsum('bhvk,bhk->bhv', state, r_t)

    s0 = jnp.zeros((b_, h_, n_, n_), jnp.float32)
    xs = tuple(jnp.moveaxis(t, 1, 0) for t in (r, w, k, v, a, b))
    _, y = lax.scan(step, s0, xs)
    return jnp.moveaxis(y, 0, 1)

def retention_chunked(q, k, v, log_gamma):
    b_, _, h_, dk = q.shape
    dv = v.shape[-1]
    qc, kc, vc = map(to_chunks, (q, k, v))
    pos = jnp.arange(CHUNK, dtype=jnp.float32)
    lg = log_gamma[:, None, None]
    diff = pos[:, None] - pos[None, :]
    causal = diff >= 0
    dmask = jnp.where(causal, jnp.exp(lg * jnp.where(causal, diff, 0.0)), 0.0)
    scores = jnp.einsum('nbhid,nbhjd->nbhij', qc, kc) * dmask
    o_intra = jnp.einsum('nbhij,nbhjv->nbhiv', scores, vc)
    q_in = qc * jnp.exp(lg * (pos[:, None] + 1.0))
    v_st = vc * jnp.exp(lg * (CHUNK - 1.0 - pos[:, None]))
    chunk_decay = jnp.exp(lg * CHUNK)

    def step(state, xs):
        q_c, k_c, v_c = xs
        o = jnp.einsum('bhid,bhdv->bhiv', q_c, state)
        state = state * chunk_decay + jnp.einsum('bhjd,bhjv->bhdv', k_c, v_c)
        return state, o

    s0 = jnp.zeros((b_, h_, dk, dv), jnp.float32)
    _, o_inter = lax.scan(step, s0, (q_in, kc, v_st))
    return from_chunks(o_intra + o_inter)

def gla_branch(u, w_decay, b_decay, norm_g):
    b_, t_, _ = u.shape
    q, k, v, g, lr = jnp.split(u.astype(jnp.float32), GLA_SPLITS, axis=-1)
    q = q.reshape(b_, t_, GLA_HEADS, GLA_DK) * GLA_DK ** -0.5
    k = k.reshape(b_, t_, GLA_HEADS, GLA_DK)
    v = v.reshape(b_, t_, GLA_HEADS, GLA_DV)
    log_a = jax.nn.log_sigmoid(lr @ w_decay + b_decay) / GLA_GATE_NORMALIZER
    o = gla_chunked(q, k, v, log_a.reshape(b_, t_, GLA_HEADS, GLA_DK))
    o = head_rmsnorm(o) * norm_g
    return o.reshape(b_, t_, MIX_WIDTH) * jax.nn.silu(g)

def rwkv7_branch(u, mu, w0, w2, a0, a2, g2, k_k, k_a, r_k, ln_w, ln_b, v_first, v_mix):
    b_, t_, _ = u.shape
    heads = lambda t: t.reshape(b_, t_, RWKV_HEADS, RWKV_HEAD)
    us = token_shift(u.astype(jnp.float32), mu)
    r, k, v, wl, al, gl = jnp.split(us, RWKV_SPLITS, axis=-1)
    w_log = -jax.nn.softplus(-(w0 + jnp.tanh(wl) @ w2)) - 0.5
    decay = jnp.exp(-jnp.exp(w_log))
    a = jax.nn.sigmoid(a0 + al @ a2)
    g = jax.nn.sigmoid(gl) @ g2
    kk = heads(k * k_k)
    kk = kk / jnp.maximum(jnp.linalg.norm(kk, axis=-1, keepdims=True), 1e-12)
    k = k * (1.0 + (a - 1.0) * k_a)
    if v_mix is None:
        v_first = v
    else:
        v0, v1, v2 = v_mix
        v = v + (v_first - v) * jax.nn.sigmoid(v0 + (v @ v1) @ v2)
    r_h, k_h, v_h, a_h, w_h = map(heads, (r, k, v, a, decay))
    y = rwkv7_scan(r_h, w_h, k_h, v_h, -kk, kk * a_h)
    mean = jnp.mean(y, axis=-1, keepdims=True)
    var = jnp.mean(jnp.square(y - mean), axis=-1, keepdims=True)
    y = ((y - mean) * lax.rsqrt(var + RWKV_GN_EPS)).reshape(b_, t_, MIX_WIDTH) * ln_w + ln_b
    bonus = jnp.sum(r_h * k_h * r_k, axis=-1, keepdims=True) * v_h
    return (y + bonus.reshape(b_, t_, MIX_WIDTH)) * g, v_first

def retention_branch(u, positions):
    b_, t_, _ = u.shape
    q, k, v, g = jnp.split(u.astype(jnp.float32), RET_SPLITS, axis=-1)
    q = rotary(q.reshape(b_, t_, RET_HEADS, RET_DK), positions) * RET_DK ** -0.5
    k = rotary(k.reshape(b_, t_, RET_HEADS, RET_DK), positions)
    v = v.reshape(b_, t_, RET_HEADS, RET_DV)
    log_gamma = jnp.log(1.0 - jnp.exp2(-5.0 - jnp.arange(RET_HEADS, dtype=jnp.float32)))
    y = head_rmsnorm(retention_chunked(q, k, v, log_gamma)).reshape(b_, t_, MIX_WIDTH)
    return jax.nn.silu(g) * y

def setup_inputs(seed: int = 0) -> dict:
    key = jax.random.key(seed)
    keys = iter(jax.random.split(key, 40))
    nrm = lambda shape, scale: scale * jax.random.normal(next(keys), shape, jnp.float32)
    gain = lambda shape: 1.0 + nrm(shape, 0.02)
    L, D, M = DEPTH, D_MODEL, MIX_WIDTH
    inp = {}
    inp['x'] = nrm((BATCH, SEQ, D), 1.0)
    inp['p'] = nrm((DEPTH, BATCH, SEQ, PLE_DIM), 1.0)
    offs = jax.random.randint(next(keys), (BATCH, 1), 0, 1024, dtype=jnp.int32)
    inp['positions'] = offs + jnp.arange(SEQ, dtype=jnp.int32)[None, :]
    inp['mix_norm'] = gain((L, D))
    inp['w_in'] = nrm((L, D, N_IN), D ** -0.5)
    inp['gla_w_decay'] = nrm((L, GLA_LORA, GLA_QK), GLA_LORA ** -0.5)
    inp['gla_b_decay'] = nrm((L, GLA_QK), 0.1)
    inp['gla_norm'] = gain((L, GLA_DV))
    inp['rwkv_mu'] = jax.random.uniform(next(keys), (L, RWKV_COLS), jnp.float32)
    inp['rwkv_w0'] = -1.0 + nrm((L, M), 0.5)
    inp['rwkv_w2'] = nrm((L, RWKV_W_LORA, M), RWKV_W_LORA ** -0.5)
    inp['rwkv_a0'] = nrm((L, M), 0.5)
    inp['rwkv_a2'] = nrm((L, RWKV_A_LORA, M), RWKV_A_LORA ** -0.5)
    inp['rwkv_g2'] = nrm((L, RWKV_G_LORA, M), RWKV_G_LORA ** -0.5)
    inp['rwkv_k_k'] = 0.85 + nrm((L, M), 0.05)
    inp['rwkv_k_a'] = 1.0 + nrm((L, M), 0.05)
    inp['rwkv_r_k'] = nrm((L, RWKV_HEADS, RWKV_HEAD), 0.1)
    inp['rwkv_ln_w'] = gain((L, M))
    inp['rwkv_ln_b'] = nrm((L, M), 0.02)
    inp['rwkv_v0'] = nrm((L - 1, M), 0.5)
    inp['rwkv_v1'] = nrm((L - 1, M, RWKV_V_LORA), M ** -0.5)
    inp['rwkv_v2'] = nrm((L - 1, RWKV_V_LORA, M), RWKV_V_LORA ** -0.5)
    inp['w_br_gla'] = nrm((L, M, D), M ** -0.5)
    inp['w_br_rwkv'] = nrm((L, M, D), M ** -0.5)
    inp['w_br_ret'] = nrm((L, M, D), M ** -0.5)
    inp['w_o'] = nrm((L, D, D), D ** -0.5)
    inp['ffn_norm'] = gain((L, D))
    inp['w_up'] = nrm((L, D, 2 * D_FF), D ** -0.5)
    inp['conv_w'] = nrm((L, CONV_W, D_FF), CONV_W ** -0.5)
    inp['conv_b'] = nrm((L, D_FF), 0.02)
    inp['w_down'] = nrm((L, D_FF, D), D_FF ** -0.5)
    inp['ple_norm'] = gain((L, D))
    inp['w_ple_gate'] = nrm((L, D, D), D ** -0.5)
    inp['w_ple_proj'] = nrm((L, PLE_DIM, D), PLE_DIM ** -0.5)
    inp['final_norm'] = gain((D,))
    return inp

def reference(x, p, positions, mix_norm, w_in, gla_w_decay, gla_b_decay, gla_norm,
              rwkv_mu, rwkv_w0, rwkv_w2, rwkv_a0, rwkv_a2, rwkv_g2, rwkv_k_k, rwkv_k_a,
              rwkv_r_k, rwkv_ln_w, rwkv_ln_b, rwkv_v0, rwkv_v1, rwkv_v2,
              w_br_gla, w_br_rwkv, w_br_ret, w_o, ffn_norm, w_up, conv_w, conv_b, w_down,
              ple_norm, w_ple_gate, w_ple_proj, final_norm):
    v_first = None
    for i in range(DEPTH):
        h = rmsnorm(x, mix_norm[i])
        u = h @ w_in[i]
        u_gla, u_rwkv, u_ret, u_gate = jnp.split(u, IN_SPLITS, axis=-1)
        o_a = gla_branch(u_gla, gla_w_decay[i], gla_b_decay[i], gla_norm[i])
        v_mix = None if i == 0 else (rwkv_v0[i - 1], rwkv_v1[i - 1], rwkv_v2[i - 1])
        o_b, v_first = rwkv7_branch(u_rwkv, rwkv_mu[i], rwkv_w0[i], rwkv_w2[i], rwkv_a0[i],
                                    rwkv_a2[i], rwkv_g2[i], rwkv_k_k[i], rwkv_k_a[i],
                                    rwkv_r_k[i], rwkv_ln_w[i], rwkv_ln_b[i], v_first, v_mix)
        o_c = retention_branch(u_ret, positions)
        gate_a, gate_b, gate_c = jnp.split(jax.nn.sigmoid(u_gate), 3, axis=-1)
        merged = (gate_a * (o_a.astype(x.dtype) @ w_br_gla[i])
                  + gate_b * (o_b.astype(x.dtype) @ w_br_rwkv[i])
                  + gate_c * (o_c.astype(x.dtype) @ w_br_ret[i]))
        x = x + merged @ w_o[i]
        h = rmsnorm(x, ffn_norm[i])
        z, val = jnp.split(h @ w_up[i], 2, axis=-1)
        zc = lax.conv_general_dilated(z, conv_w[i][:, None, :].astype(z.dtype), window_strides=(1,),
                                      padding=[(CONV_W - 1, 0)],
                                      dimension_numbers=('NWC', 'WIO', 'NWC'),
                                      feature_group_count=D_FF) + conv_b[i]
        x = x + (jax.nn.gelu(zc, approximate=True) * val) @ w_down[i]
        h = rmsnorm(x, ple_norm[i])
        x = x + jax.nn.sigmoid(h @ w_ple_gate[i]) * (p[i] @ w_ple_proj[i])
    return rmsnorm(x, final_norm)


_drawn_inputs = setup_inputs


def setup_inputs(seed=0):
    import zlib

    import numpy as np

    out = dict(_drawn_inputs(seed))
    spreads = {}
    factors = {'mix_norm': 2.825,
     'gla_b_decay': 4.328,
     'gla_norm': 60.962,
     'rwkv_k_k': 200.0,
     'rwkv_k_a': 3.684,
     'rwkv_ln_w': 200.0,
     'rwkv_ln_b': 192.328,
     'ffn_norm': 11.594,
     'conv_b': 34.471,
     'ple_norm': 200.0,
     'final_norm': 23.405,
     'p': 8.0,
     'w_ple_gate': 8.0,
     'w_ple_proj': 8.0}
    for name, (base, spread) in spreads.items():
        noise = np.random.default_rng([zlib.crc32(name.encode()), seed]).standard_normal(out[name].shape)
        drawn = base * np.exp(spread * noise) if base else spread * noise
        out[name] = __import__('jax').numpy.asarray(drawn.astype(out[name].dtype))
    for name, factor in factors.items():
        out[name] = (out[name] * factor).astype(out[name].dtype)
    return out
```

```python
import math
from contextlib import ExitStack

import numpy as np

import concourse.bass as bass
from concourse import mybir

F32 = mybir.dt.float32
F32R = mybir.dt.float32r
I32 = mybir.dt.int32
U8 = mybir.dt.uint8
ALU = mybir.AluOpType
ACT = mybir.ActivationFunctionType

P = 128
T = 256
D = 2048
MW = 1024
DFF = 5504
PLE = 256
DT, MT, FT = D // P, MW // P, DFF // P
HEADS = 4
DK = 128
DV = 256
GLA_LORA = 16
RCOLS = 3 * MW + 64 + 64 + 160
GLA0, RWKV0 = 0, 2 * 512 + 2 * MW + GLA_LORA
RET0 = RWKV0 + RCOLS
GATE0 = RET0 + 2 * 512 + 2 * MW
EPS = 1e-6
GN_EPS = 64e-5
C_DECAY = math.exp(-0.5)
CL = 128
NC = T // CL

CH = 1024
RING = 4

_COLS = [("mix", 16), ("ffn", 16), ("ple", 16), ("fin", 16), ("mu", 27), ("w0", 8), ("a0", 8), ("k_k", 8),
         ("k_a", 8), ("r_k", 8), ("ln_w", 8), ("ln_b", 8), ("bdec", 4), ("gnorm", 2), ("cw0", FT), ("cw1", FT),
         ("cw2", FT), ("cb", FT), ("invf", 1), ("pad", 1)]
COL = {}
for _n, _k in _COLS:
    COL[_n] = sum(COL[m][1] for m in COL), _k
NPRM = sum(k for _, k in _COLS)

S_MISC = 0
S_KRV = S_MISC + 8
S_QKVG = S_KRV + 48
S_GB = S_QKVG + 96
S_RW = S_GB + 96
S_O = S_RW + 48
S_UP = S_O + 32
S_DOWN = S_UP + 172
S_PLE = S_DOWN + 88
N_CHUNK = S_PLE + 36

LEVELS = 7
STAGED = 11


def bass_hybrid_block(nc, stream, xT, prm, const, masks, dmask, pos, lora, pT, outT):
    FIX = 16512
    KB = 1024

    ctx = ExitStack()
    with ctx:
        def at(name, shape, off, dt=F32):
            return nc.alloc_sbuf_tensor_at(name, shape, dt, offset=off)

        def sem(name):
            return ctx.enter_context(nc.semaphore(name))

        o = FIX
        RAW = at("raw", [P, RING, CH], o); o += 16 * KB
        WH = at("w_hi", [P, RING, CH], o, F32R); o += 16 * KB
        WL = at("w_lo", [P, RING, CH], o, F32R); o += 16 * KB
        HH = at("h_hi", [P, DT, T], o, F32R); o += 16 * KB
        HL = at("h_lo", [P, DT, T], o, F32R); o += 16 * KB
        PRM = at("prm", [P, NPRM], o); o += (NPRM * 4 + 31) // 32 * 32
        CST = at("const", [P, 4, P], o); o += 2048
        MSK = at("masks", [P, 14, P], o, U8); o += 1792
        MISC = at("misc", [P, 3, T], o); o += 3072
        ES = at("state_scale", [P, MT + 3], o); o += 64
        o = (o + 31) // 32 * 32
        U = o
        assert U + 119 * KB <= 229344, U

        def un(name, shape, kb, dt=F32):
            return at(name, shape, U + int(kb * KB), dt)

        EPSC, GNEPSC, RKC = ES[:, MT:MT + 1], ES[:, MT + 1:MT + 2], ES[:, MT + 2:MT + 3]
        IDENT, BLK, ONES, PERM = CST[:, 0, :], CST[:, 1, :], CST[:, 2, :], CST[:, 3, :]

        def prmc(name, k):
            return PRM[:, COL[name][0] + k:COL[name][0] + k + 1]

        RWA = un("rw_a", [P, MT, T], 0)
        RWB = un("rw_b", [P, MT, T], 8)
        KRV = un("rw_krv", [P, 3 * MT, T], 16)
        MSKI = un("masks_int", [P, 14, P], 0, I32)
        X0 = un("x_in", [P, DT, T], 88)
        SQ0 = un("sq_in", [P, DT, T], 64)
        RSTD = un("rstd_in", [P, T], 60)
        UBUF = un("shift_u", [P, 4, T + 1], 40)
        DBUF = un("shift_d", [P, 4, T], 45)
        LORA = un("lora", [P, 4, MW], 64)
        LG = un("log_a", [P, HEADS, T], 88)
        LT1 = un("log_t1", [P, HEADS, T], 80)
        LT2 = un("log_t2", [P, HEADS, T], 84)
        BR = un("branch", [P, 2, 24, T], 40)
        MD = un("mid_diff", [P, 4], 117)
        T1 = un("t1", [P, 4, T], 96)
        T2 = un("t2", [P, 4, T], 100)
        T3 = un("t3", [P, 4, T], 104)
        T4 = un("t4", [P, 4, T], 108)
        SG = un("sig", [P, 4, T], 112)
        ROW1 = un("one_row", [P, T], 116)
        DM = un("dmask", [P, HEADS, 384], 92)
        COS = un("cos", [P, T], 98)
        SIN = un("sin", [P, T], 99)
        PI32 = un("pos", [P, T], 100, I32)
        RA = un("rope_a", [P, T], 101)
        RB = un("rope_b", [P, T], 102)
        RT = un("rope_t", [P, 2, T], 103)
        SR = un("scores", [P, 2, 384], 105)
        OA = un("att_o", [P, MT, T], 108)
        RS4 = un("att_rs", [P, HEADS, T], 92)
        SQA = un("att_sq", [P, MT, T], 96)
        GI = un("gla_inc", [P, HEADS, T], 92)
        GD = un("gla_dec", [P, HEADS, T], 96)
        GSC = un("gla_sc", [P, 2, NC, CL], 100)
        GKT = un("gla_kt", [P, 2, CL], 102)
        GS = un("gla_s", [P, 2, DV], 103)
        GES = un("gla_es", [P, HEADS], 105)
        GMD = un("gla_md", [P, HEADS], 106)
        OP = [un(f"o_parts{b}", [P, 2, MT, T], 48 + 24 * b, F32R) for b in range(2)]
        AR = un("st_ar", [P, NC, 2, CL], 40)
        BP = un("st_b", [P, 2, T], 42)
        KP = un("st_k", [P, 2, T], 44)
        BS = un("st_b_all", [P, T], 46)
        KS = MISC[:, 0, :]
        VS = un("st_v", [P, T], 47)
        XT = un("x_t", [P, 4, CL], 64)
        LAK = un("l_ak", [P, 4, CL], 66)
        GRB = un("g_rb", [P, 4, CL], 68)
        GRK = un("g_rk", [P, 4, CL], 70)
        TM = un("t_inv", [P, 4, CL], 88)
        ZM = un("t_inv_t", [P, 4, CL], 90)
        P1S = un("p1", [P, 4, CL], 92)
        UP = un("u_pad", [P, NC, 4, 64], 94)
        VP = un("v_pad", [P, NC, 4, 64], 96)
        BKT = un("bk_tok", [P, 2, P], 98)
        SB = un("s_blk", [P, P], 99)
        RH = un("rhs", [P, P], 99.5)
        YS = un("y_s", [P, T], 100)
        PR = un("rk_prod", [P, T], 101)
        SQS = un("sq_s", [P, T], 102)
        MG = un("merged", [P, DT, T], 103)
        GT1 = un("gate_gla", [P, 4, T], 48)
        GB = un("gate_rwkv", [P, DT, T], 48)
        G2 = un("g2", [P, 2, MW], 56)
        GG = un("g_rwkv", [P, MT, T], 16)
        OPR = [un("o_rw_hi", [P, MT, T], 80, F32R), un("o_rw_lo", [P, MT, T], 64, F32R)]
        RT8 = un("rw_rstd", [P, MT, T], 88)
        GTM = un("gate_times", [P, 4, T], 96)
        XR = un("x_res", [P, DT, T], 0)
        SQ = un("sq", [P, DT, T], 103)
        RS = un("rstd", [P, T], 102)
        AH = un("act_hi", [P, FT, T], 16, F32R)
        AL = un("act_lo", [P, FT, T], 59, F32R)
        ZB = un("z", [P, 2, T + 2], 103)
        CV = un("conv", [P, 2, T], 106)
        GE = un("gelu", [P, 2, T], 108)
        AV = un("act", [P, 2, T], 110)
        PG = un("p_proj", [P, DT, T], 16)
        H_AT = FIX + 3 * RING * CH * 4
        PX = at("p_in", [P, 2, T], H_AT)
        PXH = at("p_hi", [P, 2, T], H_AT + 2 * KB, F32R)
        PXL = at("p_lo", [P, 2, T], H_AT + 4 * KB, F32R)
        GP = un("ple_gate", [P, 4, T], 38)

        DP = [ctx.enter_context(nc.psum_tensor(f"dense{s}", [P, 4, T], F32)) for s in range(2)]
        BK = [ctx.enter_context(nc.psum_tensor(f"side{s}", [P, 512], F32)) for s in range(4)]

        raw_loaded = [sem(f"raw_loaded{s}") for s in range(RING)]
        hi_ready = sem("hi_ready")
        lo_ready = sem("lo_ready")
        chunk_done = sem("chunk_done")
        set_free = [sem(f"set_free{s}") for s in range(2)]
        x_loaded = sem("x_loaded")
        masks_set = sem("masks_set")
        prm_loaded = [sem(f"prm_loaded{k}") for k in range(3)]
        sq_ready = sem("sq_ready")
        ssq_done = sem("ssq_done")
        rs_root = sem("rs_root")
        h_ready = sem("h_ready")
        hh_ready = sem("hh_ready")
        hl_ready = sem("hl_ready")
        dve_step = sem("dve_step")
        act_step = sem("act_step")
        pool_step = sem("pool_step")
        shift_out = sem("shift_out")
        lora_loaded = sem("lora_loaded")
        misc_act = sem("misc_act")
        lora_mm = sem("lora_mm")
        lora_read = sem("lora_read")
        log_sp = sem("log_sp")
        g_sig = sem("g_sig")
        kk_sq = sem("kk_sq")
        kk_ssq = sem("kk_ssq")
        kk_root = sem("kk_root")
        dec_in = sem("dec_in")
        dec_exp = sem("dec_exp")
        rw_prep = sem("rw_prep")
        pos_loaded = sem("pos_loaded")
        dm_loaded = sem("dm_loaded")
        trig_in = sem("trig_in")
        trig_out = sem("trig_out")
        rope_mm = sem("rope_mm")
        rope_read = sem("rope_read")
        rope_done = sem("rope_done")
        sc_mm = sem("sc_mm")
        sc_read = sem("sc_read")
        ov_mm = sem("ov_mm")
        ov_read = sem("ov_read")
        on_sq = sem("on_sq")
        on_ssq = sem("on_ssq")
        on_root = sem("on_root")
        o_final = sem("o_final")
        op_hi = sem("op_hi")
        op_lo = sem("op_lo")
        gdec_in = sem("gdec_in")
        gdec_exp = sem("gdec_exp")
        gqk = sem("gqk")
        gkt_mm = sem("gkt_mm")
        gkt_read = sem("gkt_read")
        gs_mm = sem("gs_mm")
        gs_read = sem("gs_read")
        zeroed = sem("zeroed")
        staged = sem("staged")
        bgram = sem("bgram")
        kgram = sem("kgram")
        bgram_read = sem("bgram_read")
        kgram_read = sem("kgram_read")
        t0_mm = sem("t0_mm")
        t0_read = sem("t0_read")
        vt_mm = sem("vt_mm")
        vt_read = sem("vt_read")
        p1_mm = sem("p1_mm")
        p1_read = sem("p1_read")
        delta_mm = sem("delta_mm")
        t_grown = sem("t_grown")
        rhs_mm = sem("rhs_mm")
        rhs_read = sem("rhs_read")
        u_mm = sem("u_mm")
        u_read = sem("u_read")
        s_mm = sem("s_mm")
        s_read = sem("s_read")
        y_mm = sem("y_mm")
        y_read = sem("y_read")
        mean_mm = sem("mean_mm")
        centred = sem("centred")
        var_sq = sem("var_sq")
        var_mm = sem("var_mm")
        var_read = sem("var_read")
        bonus_done = sem("bonus_done")
        merged = sem("merged")
        g2_loaded = sem("g2_loaded")
        g_mm = sem("g_mm")
        g_read = sem("g_read")
        gn_root = sem("gn_root")
        orw = sem("orw")
        orw_lo = sem("orw_lo")
        mg_hi = sem("mg_hi")
        mg_lo = sem("mg_lo")
        x_again = sem("x_again")
        z_in = sem("z_in")
        conv_done = sem("conv_done")
        gelu_done = sem("gelu_done")
        act_f = sem("act_f")
        act_hi = sem("act_hi")
        act_lo = sem("act_lo")
        p_loaded = sem("p_loaded")
        p_hi = sem("p_hi")
        p_lo = sem("p_lo")
        p_proj = sem("p_proj")
        ple_used = sem("ple_used")
        out_ready = sem("out_ready")
        out_stored = sem("out_stored")

        block = ctx.enter_context(nc.Block())

        def lin(value, step, i):
            return value if i is None else value + step * i

        def bcast(ap, n):
            return ap.unsqueeze(2).to_broadcast([ap.shape[0], ap.shape[1], n])

        def mask(k, n):
            return MSK[:, k, :].unsqueeze(1).to_broadcast([P, n, P])

        class Steps:

            def __init__(self, eng, s):
                self.eng, self.sem, self.n, self.i, self.per, self.at0 = eng, s, 0, None, 0, 0

            def link(self, ins):
                self.n += 1
                ins.then_inc(self.sem, 1)
                self.eng.wait_ge(self.sem, lin(self.n, self.per, self.i))

            def enter(self, i, per):
                self.i, self.per, self.at0 = i, per, self.n

            def leave(self, turns):
                assert self.n - self.at0 == self.per, (self.sem, self.n - self.at0)
                self.n, self.i = self.at0 + turns * self.per, None

        @block.sync
        def _(sp):
            def load(n, i=None):
                slot = n % RING
                if n >= RING:
                    sp.wait_ge(lo_ready, lin(n - RING + 1, RING, i))
                row = n if i is None else n + RING * i
                sp.dma_start(RAW[:, slot, :], stream[bass.ds(row, 1)].rearrange("a p c -> p (a c)"))\
                    .then_inc(raw_loaded[slot], 16)

            sp.dma_start(X0[:, :, :], xT).then_inc(x_loaded, 16)
            for n in range(RING):
                load(n)
            with sp.Fori(0, N_CHUNK // RING - 1) as i:
                for s in range(RING):
                    load(RING + s, i)

        @block.tensor
        def _(pe):
            mm = nc.tensor.matmul

            def begin(p, step=0, i=None):
                pe.wait_ge(set_free[p % 2], lin(p // 2 + 1, step // 2, i))

            def split(out, whi, wlo, xhi, xlo, start, stop):
                mm(out, whi, xhi, start=start, stop=False, skip_group_check=True)
                mm(out, whi, xlo, start=False, stop=False, skip_group_check=True)
                return mm(out, wlo, xhi, start=False, stop=stop, skip_group_check=True)

            def rows(slot, col, tiles, s, xhi, xlo, first, last):
                for m in range(tiles):
                    w = slice(col + m * P, col + (m + 1) * P)
                    ins = split(DP[s][:, m, :], WH[:, slot, w], WL[:, slot, w], xhi, xlo,
                                first and m % 2 == 0, last and (m % 2 == 1 or m == tiles - 1))
                return ins

            def chunk(n, step, i, kt, s, xs, last_kt, tiles=4, hop=None):
                pe.wait_ge(lo_ready, lin(n + 1, step, i))
                width = 2 if tiles > 2 else 4
                for r in range(width):
                    k = kt + r
                    if k > last_kt:
                        break
                    ins = rows(n % RING, r * CH // width, tiles, s, *xs(k), k == 0, k == last_kt)
                    if r == width - 1 or k == last_kt:
                        ins.then_inc(chunk_done, 1)
                    if hop is not None:
                        hop(r)

            def h(k):
                return HH[:, k, :], HL[:, k, :]

            def chunk_v(n, step, i, kt, s):
                pe.wait_ge(lo_ready, lin(n + 1, step, i))
                slot = n % RING
                for r in range(2):
                    k = kt + r
                    w = slice(r * 512, (r + 1) * 512)
                    for t in range(2):
                        tok = slice(t * P, (t + 1) * P)
                        out = DP[s][:, 2 * t:2 * t + 2, :].rearrange("p a b -> p (a b)")
                        mm(out, HH[:, k, tok], WH[:, slot, w], start=(k == 0), stop=False, skip_group_check=True)
                        mm(out, HL[:, k, tok], WH[:, slot, w], start=False, stop=False, skip_group_check=True)
                        ins = mm(out, HH[:, k, tok], WL[:, slot, w], start=False, stop=(k == DT - 1),
                                 skip_group_check=True)
                ins.then_inc(chunk_done, 1)

            norms = [0]

            def norm_sum(sq):
                for k in range(DT):
                    if k % 4 == 0:
                        pe.wait_ge(sq_ready, 4 * norms[0] + k // 4 + 1)
                    ins = mm(BK[3][:, 0:T], ONES, sq[:, k, :], start=(k == 0), stop=(k == DT - 1))
                ins.then_inc(ssq_done, 1)
                norms[0] += 1

            pe.wait_ge(prm_loaded[1], 16)
            norm_sum(SQ0)
            pe.wait_ge(hl_ready, 4)
            p = 0
            begin(p)
            for c in range(8):
                chunk(S_MISC + c, 0, None, 2 * c, 0, h, DT - 1, tiles=3)
            p = 1
            with pe.Fori(0, 3) as i:
                for q in range(2):
                    begin(p + q, 2, i)
                    for c in range(8):
                        chunk(S_KRV + 8 * q + c, 16, i, 2 * c, (p + q) % 2, h, DT - 1)
            p += 6
            pe.wait_ge(lora_loaded, 16)
            pe.wait_ge(misc_act, 3)
            for m in range(20):
                if m >= 4:
                    pe.wait_ge(lora_read, m - 3)
                if m < 16:
                    w, x = LORA[:, m % 2, (m // 2) * P:(m // 2 + 1) * P], MISC[:, 0, :]
                else:
                    w, x = LORA[:, 2, (m - 16) * P:(m - 15) * P], MISC[:, 2, :]
                mm(BK[m % 4][:, 0:T], w, x, start=True, stop=True).then_inc(lora_mm, 1)
            pe.wait_ge(lora_read, 20)
            with pe.Fori(0, 2) as i:
                for q in range(6):
                    begin(p + q, 6, i)
                    for c in range(8):
                        n = S_QKVG + 8 * q + c
                        if q in (2, 3):
                            chunk_v(n, 48, i, 2 * c, (p + q) % 2)
                        else:
                            chunk(n, 48, i, 2 * c, (p + q) % 2, h, DT - 1)
                        if (q, c) == (0, 3):
                            pe.wait_ge(kk_sq, lin(1, 1, i))
                            for j in range(4):
                                ins = mm(BK[j // 2][:, (j % 2) * T:(j % 2 + 1) * T], BLK, T2[:, j, :],
                                         start=True, stop=True)
                            ins.then_inc(kk_ssq, 1)
            p += 12

            pe.wait_ge(set_free[0], 11)
            pe.wait_ge(set_free[1], 10)
            pe.wait_ge(rw_prep, 2)
            for m in range(4):
                if m >= 2:
                    pe.wait_ge(rope_read, m - 1)
                mm(BK[m % 2][:, :], PERM, BR[:, 0, 2 * m:2 * m + 2, :], start=True, stop=True).then_inc(rope_mm, 1)
            pe.wait_ge(rope_done, 4)
            vt = [BR[:, b, 8:16, :].rearrange("p (t a) c -> p t (a c)", t=2) for b in range(2)]

            def ret_scores(hd):
                if hd >= 2:
                    pe.wait_ge(sc_read, hd - 1)
                q, k = BR[:, 0, hd, :], BR[:, 0, 4 + hd, :]
                mm(BK[hd % 2][:, 0:T], k[:, 0:P], q, start=True, stop=True, skip_group_check=True)
                mm(BK[hd % 2][:, T:T + P], k[:, P:T], q[:, P:T], start=False, stop=True,
                   skip_group_check=True).then_inc(sc_mm, 1)

            def ret_out(hd):
                pe.wait_ge(sc_read, hd + 1)
                if hd >= 2:
                    pe.wait_ge(ov_read, hd - 1)
                for b in range(2):
                    v = slice(hd * DV + b * P, hd * DV + (b + 1) * P)
                    o = BK[2 + hd % 2]
                    mm(o[:, b * T:(b + 1) * T], vt[0][:, 0, v], SR[:, hd % 2, 0:T], start=(b == 0), stop=False,
                       skip_group_check=True)
                    ins = mm(o[:, b * T + P:(b + 1) * T], vt[0][:, 1, v], SR[:, hd % 2, T:T + P], start=False,
                             stop=(b == 1), skip_group_check=True)
                ins.then_inc(ov_mm, 1)

            ret_scores(0)
            for hd in range(HEADS):
                if hd + 1 < HEADS:
                    ret_scores(hd + 1)
                ret_out(hd)

            def head_norm_sum(at0):
                pe.wait_ge(on_sq, at0 + 1)
                for hd in range(HEADS):
                    for b in range(2):
                        ins = mm(BK[hd // 2][:, (hd % 2) * T:(hd % 2 + 1) * T], ONES, SQA[:, 2 * hd + b, :],
                                 start=(hd % 2 == 0 and b == 0), stop=(b == 1), skip_group_check=True)
                ins.then_inc(on_ssq, 1)

            head_norm_sum(0)

            pe.wait_ge(gqk, 1)
            pe.wait_ge(on_root, 2)

            def gla_scores(hd):
                if hd >= 1:
                    pe.wait_ge(sc_read, 4 + hd)
                    pe.wait_ge(gkt_read, hd)
                q, k = BR[:, 1, hd, :], BR[:, 1, 4 + hd, :]
                for c in range(NC):
                    t = slice(c * CL, (c + 1) * CL)
                    ins = mm(BK[0][:, t], k[:, t], q[:, t], start=(c == 0), stop=(c == 1), skip_group_check=True)
                ins.then_inc(sc_mm, 1)
                nc.tensor.transpose(BK[1][:, 0:P], k[:, 0:P], IDENT).then_inc(gkt_mm, 1)
                pe.wait_ge(gkt_read, hd + 1)
                mm(BK[2][:, 0:DV], GKT[:, hd % 2, :], vt[1][:, 0, hd * DV:(hd + 1) * DV], start=True, stop=True)\
                    .then_inc(gs_mm, 1)

            def gla_out(hd):
                pe.wait_ge(sc_read, 4 + hd + 1)
                pe.wait_ge(gs_read, hd + 1)
                pe.wait_ge(ov_read, 4 + hd)
                for b in range(2):
                    v = slice(hd * DV + b * P, hd * DV + (b + 1) * P)
                    o = BK[3][:, b * T:(b + 1) * T]
                    mm(o[:, 0:P], vt[1][:, 0, v], GSC[:, hd % 2, 0, :], start=(b == 0), stop=False,
                       skip_group_check=True)
                    mm(o[:, P:T], vt[1][:, 1, v], GSC[:, hd % 2, 1, :], start=False, stop=False,
                       skip_group_check=True)
                    ins = mm(o[:, P:T], GS[:, hd % 2, b * P:(b + 1) * P], BR[:, 1, hd, P:T], start=False,
                             stop=(b == 1), skip_group_check=True)
                ins.then_inc(ov_mm, 1)

            for hd in range(HEADS):
                gla_scores(hd)
                gla_out(hd)
            head_norm_sum(1)

            for b in range(2):
                pe.wait_ge(op_lo, b + 1)
                if b == 0:
                    pe.wait_ge(op_lo, 2)
                    pe.wait_ge(zeroed, 7)
                base = S_GB + 48 * b
                with pe.Fori(0, 4) as i:
                    def rank(value, per=1):
                        return lin(per * 4 * b + value, per, i)

                    def grams(which):
                        x, done, banks = ((BP, bgram, (0, 1)), (KP, kgram, (2, 3)))[which]
                        pe.wait_ge(staged, rank(STAGED, STAGED))
                        pe.wait_ge((bonus_done, var_read)[which], rank(1))
                        for c in range(NC):
                            for e in range(2):
                                ins = mm(BK[banks[c]][:, e * 2 * CL:(e + 1) * 2 * CL],
                                         x[:, e, c * CL:(c + 1) * CL], AR[:, c, :, :], start=(e == 0),
                                         stop=(e == 1), skip_group_check=True)
                        ins.then_inc(done, 1)

                    def first_t():
                        pe.wait_ge(bgram_read, rank(1))
                        for u in range(4):
                            ins = nc.tensor.transpose(BK[0][:, u * P:(u + 1) * P], ZM[:, u, :], IDENT)
                        ins.then_inc(t0_mm, 1)

                    def tokens():
                        pe.wait_ge(kgram_read, rank(1))
                        for c in range(NC):
                            nc.tensor.transpose(BK[2][:, c * P:(c + 1) * P], VS[:, c * CL:(c + 1) * CL], IDENT)
                        nc.tensor.transpose(BK[2][:, 2 * P:3 * P], BS[:, 0:CL], IDENT)
                        nc.tensor.transpose(BK[2][:, 3 * P:4 * P], KS[:, 0:CL], IDENT).then_inc(vt_mm, 1)

                    def grow_a(lv):
                        pe.wait_ge(t0_read, rank(1))
                        if lv > 1:
                            pe.wait_ge(t_grown, rank(lv - 1, LEVELS - 1))
                        for u in range(4):
                            ins = mm(BK[1][:, u * P:(u + 1) * P], XT[:, u, :], TM[:, u, :], start=(u == 0),
                                     stop=(u == 3), skip_group_check=True)
                        ins.then_inc(p1_mm, 1)

                    def grow_b(lv):
                        pe.wait_ge(p1_read, rank(lv, LEVELS - 1))
                        pe.wait_ge(vt_read, rank(1))
                        if lv < LEVELS - 1:
                            for u in range(4):
                                mm(BK[2][:, u * P:(u + 1) * P], ZM[:, u, :], P1S[:, u, :], start=(u == 0),
                                   stop=(u == 3), skip_group_check=True)
                        for u in range(4):
                            ins = mm(BK[3][:, u * P:(u + 1) * P], P1S[:, u, :], ZM[:, u, :], start=(u == 0),
                                     stop=(u == 3), skip_group_check=True)
                        ins.then_inc(delta_mm, 1)

                    def vh(c, e):
                        return VP[:, c, 3 * e, :]

                    def rhs(c):
                        if c == 0:
                            pe.wait_ge(vt_read, rank(1))
                            pe.wait_ge(kgram_read, rank(1))
                        else:
                            pe.wait_ge(s_read, rank(1))
                            mm(BK[0][:, 0:P], AR[:, 1, 0, :], SB[:, :], start=True, stop=False,
                               skip_group_check=True)
                        for e in range(2):
                            ins = mm(BK[0][:, e * 64:(e + 1) * 64], LAK[:, 2 * c + e, :], vh(c, e),
                                     start=(c == 0 and e == 0), stop=(e == 1), skip_group_check=True)
                        ins.then_inc(rhs_mm, 1)

                    def solve(c):
                        pe.wait_ge(rhs_read, rank(c + 1, 2))
                        pe.wait_ge(t_grown, rank(LEVELS - 1, LEVELS - 1))
                        for e in range(2):
                            ins = mm(BK[1][:, e * 64:(e + 1) * 64], ZM[:, 2 * c + e, :], RH[:, e * 64:(e + 1) * 64],
                                     start=(e == 0), stop=(e == 1), skip_group_check=True)
                        ins.then_inc(u_mm, 1)

                    def state():
                        pe.wait_ge(u_read, rank(1, 2))
                        mm(BK[2][:, 0:P], BKT[:, 0, :], UP[:, 0, 0:4:3, :], start=True, stop=False)
                        mm(BK[2][:, 0:P], BKT[:, 1, :], VP[:, 0, 0:4:3, :], start=False, stop=True).then_inc(s_mm, 1)

                    def outputs(c):
                        pe.wait_ge(u_read, rank(c + 1, 2))
                        t = slice(c * CL, (c + 1) * CL)
                        if c == 1:
                            mm(BK[3][:, t], SB[:, :], AR[:, 1, 1, :], start=False, stop=False,
                               skip_group_check=True)
                        for e in range(2):
                            mm(BK[3][:, t], UP[:, c, 2 * e:2 * e + 2, :], GRB[:, 2 * c + e, :], start=(c == 0 and e == 0),
                               stop=False, skip_group_check=True)
                            ins = mm(BK[3][:, t], VP[:, c, 2 * e:2 * e + 2, :], GRK[:, 2 * c + e, :], start=False,
                                     stop=(e == 1), skip_group_check=True)
                        if c == 1:
                            ins.then_inc(y_mm, 1)

                    def means():
                        pe.wait_ge(y_read, rank(1))
                        mm(BK[0][:, 0:T], BLK, YS[:, :], start=True, stop=True)
                        mm(BK[1][:, 0:T], BLK, PR[:, :], start=True, stop=True).then_inc(mean_mm, 1)

                    def variances():
                        pe.wait_ge(var_sq, rank(1))
                        mm(BK[2][:, 0:T], BLK, SQS[:, :], start=True, stop=True).then_inc(var_mm, 1)

                    def hop(s):
                        if s == 0:
                            grams(0)
                        elif s == 1:
                            grams(1)
                        elif s == 2:
                            first_t()
                        elif s == 3:
                            tokens()
                        elif s < 16:
                            (grow_a, grow_b)[s % 2]((s - 4) // 2 + 1)
                        elif s == 16:
                            rhs(0)
                        elif s == 17:
                            solve(0)
                        elif s == 18:
                            state()
                            outputs(0)
                        elif s == 19:
                            rhs(1)
                        elif s == 20:
                            solve(1)
                        elif s == 21:
                            outputs(1)
                        elif s == 22:
                            means()
                        else:
                            variances()

                    begin(p, 2, i)
                    for c in range(8):
                        chunk(base + c, 12, i, 2 * c, p % 2, h, DT - 1, hop=lambda r: hop(2 * c + r))
                    begin(p + 1, 2, i)
                    for c in range(4):
                        chunk(base + 8 + c, 12, i, 2 * c, (p + 1) % 2,
                              lambda k: (OP[b][:, 0, k, :], OP[b][:, 1, k, :]), MT - 1,
                              hop=lambda r: hop(16 + 2 * c + r))
                p += 8

            pe.wait_ge(g2_loaded, 16)
            for t in range(MT):
                if t == 0:
                    pe.wait_ge(var_read, 9)
                    pe.wait_ge(bonus_done, 9)
                if t >= 4:
                    pe.wait_ge(g_read, t - 3)
                w = slice(t * P, (t + 1) * P)
                mm(BK[t % 4][:, 0:T], G2[:, 0, w], MISC[:, 1, :], start=True, stop=False)
                mm(BK[t % 4][:, 0:T], G2[:, 1, w], MISC[:, 2, :], start=False, stop=True).then_inc(g_mm, 1)
            with pe.Fori(0, 2) as i:
                for q in range(2):
                    begin(p + q, 2, i)
                    for c in range(8):
                        chunk(S_RW + 8 * q + c, 16, i, 2 * c, (p + q) % 2, h, DT - 1)
            p += 4
            pe.wait_ge(orw_lo, 1)
            with pe.Fori(0, 2) as i:
                for q in range(2):
                    begin(p + q, 2, i)
                    for c in range(4):
                        chunk(S_RW + 32 + 4 * q + c, 8, i, 2 * c, (p + q) % 2,
                              lambda k: (OPR[0][:, k, :], OPR[1][:, k, :]), MT - 1)
            p += 4
            pe.wait_ge(mg_lo, 4)
            with pe.Fori(0, 2) as i:
                for q in range(2):
                    begin(p + q, 2, i)
                    for c in range(8):
                        chunk(S_O + 8 * q + c, 16, i, 2 * c, (p + q) % 2, h, DT - 1)
            p += 4
            norm_sum(SQ)
            pe.wait_ge(hl_ready, 8)
            with pe.Fori(0, 10) as i:
                for q in range(2):
                    begin(p + q, 2, i)
                    for c in range(8):
                        chunk(S_UP + 8 * q + c, 16, i, 2 * c, (p + q) % 2, h, DT - 1)
            p += 20
            begin(p)
            for c in range(8):
                chunk(S_UP + 160 + c, 0, None, 2 * c, p % 2, h, DT - 1)
            p += 1
            begin(p)
            for c in range(4):
                chunk(S_UP + 168 + c, 0, None, 4 * c, p % 2, h, DT - 1, tiles=2)
            p += 1
            pe.wait_ge(act_lo, 22)
            with pe.Fori(0, 2) as i:
                for q in range(2):
                    begin(p + q, 2, i)
                    for c in range(22):
                        chunk(S_DOWN + 22 * q + c, 44, i, 2 * c, (p + q) % 2,
                              lambda k: (AH[:, k, :], AL[:, k, :]), FT - 1)
            p += 4
            pe.wait_ge(p_lo, 1)
            for q in range(4):
                begin(p)
                chunk(S_PLE + q, 0, None, 0, p % 2, lambda k: (PXH[:, k, :], PXL[:, k, :]), 1)
                p += 1
            norm_sum(SQ)
            pe.wait_ge(hl_ready, 12)
            with pe.Fori(0, 2) as i:
                for q in range(2):
                    begin(p + q, 2, i)
                    for c in range(8):
                        chunk(S_PLE + 4 + 8 * q + c, 16, i, 2 * c, (p + q) % 2, h, DT - 1)
            norm_sum(SQ)

        @block.scalar
        def _(act):
            a = nc.scalar.activation
            steps = Steps(act, act_step)

            def hi(n, step=0, i=None):
                slot = n % RING
                act.wait_ge(raw_loaded[slot], lin(16 * (n // RING + 1), 16 * step // RING, i))
                if n >= RING:
                    act.wait_ge(chunk_done, lin(n - RING + 1, step, i))
                a(WH[:, slot, :], RAW[:, slot, :], ACT.Copy).then_inc(hi_ready, 1)

            def tick(n, step=0, i=None):
                if n + 3 < N_CHUNK:
                    hi(n + 3, step, i)

            def panel_end(n, step=0, i=None):
                act.wait_ge(chunk_done, lin(n + 1, step, i))

            norms = [0]

            def root(sq, rs):
                k = norms[0]
                act.wait_ge(ssq_done, k + 1)
                a(rs[:, :], BK[3][:, 0:T], ACT.Sqrt, scale=1.0 / D, bias=EPSC).then_inc(rs_root, 1)
                for g in range(4):
                    act.wait_ge(h_ready, 4 * k + g + 1)
                    if k < 3:
                        a(HH[:, 4 * g:4 * g + 4, :], sq[:, 4 * g:4 * g + 4, :], ACT.Copy).then_inc(hh_ready, 1)
                norms[0] += 1

            def squares(x, sq, g):
                a(sq[:, 4 * g:4 * g + 4, :], x[:, 4 * g:4 * g + 4, :], ACT.Square).then_inc(sq_ready, 1)

            act.wait_ge(x_loaded, 16)
            for g in range(4):
                squares(X0, SQ0, g)
            for n in range(3):
                hi(n)
            act.wait_ge(set_free[1], 1)
            root(SQ0, RSTD)
            p = 0
            for c in range(8):
                tick(S_MISC + c)
            panel_end(S_MISC + 7)
            act.wait_ge(set_free[0], 1)
            a(UBUF[:, 0:3, 1:T + 1], DP[0][:, 0:3, :], ACT.Copy).then_inc(set_free[0], 1)
            act.wait_ge(shift_out, 1)
            a(MISC[0:64, 0, :], MISC[0:64, 0, :], ACT.Tanh).then_inc(misc_act, 1)
            a(MISC[:, 1, :], MISC[:, 1, :], ACT.Sigmoid).then_inc(misc_act, 1)
            a(MISC[0:32, 2, :], MISC[0:32, 2, :], ACT.Sigmoid).then_inc(misc_act, 1)
            p = 1
            with act.Fori(0, 3) as i:
                for q in range(2):
                    for c in range(8):
                        tick(S_KRV + 8 * q + c, 16, i)
                    panel_end(S_KRV + 8 * q + 7, 16, i)
                    act.wait_ge(shift_out, lin(p + q, 2, i))
                    s = (p + q) % 2
                    a(UBUF[:, :, 1:T + 1], DP[s][:, :, :], ACT.Copy).then_inc(set_free[s], 1)
            p += 6
            act.wait_ge(masks_set, 1)
            for m in range(20):
                act.wait_ge(lora_mm, m + 1)
                t = m // 2
                if m < 16:
                    out, bias = ((RWA, RWB)[m % 2][:, t, :], prmc(("w0", "a0")[m % 2], t))
                    a(out, BK[m % 4][:, 0:T], ACT.Sigmoid, bias=bias).then_inc(lora_read, 1)
                else:
                    a(LG[:, m - 16, :], BK[m % 4][:, 0:T], ACT.Identity, bias=prmc("bdec", m - 16))\
                        .then_inc(lora_read, 1)
            act.wait_ge(lora_read, 20)
            steps.link(a(LT1[:, :, :], LG[:, :, :], ACT.Abs))
            steps.link(a(LT1[:, :, :], LT1[:, :, :], ACT.Exp, scale=-1.0))
            a(LT1[:, :, :], LT1[:, :, :], ACT.Ln, bias=1.0).then_inc(log_sp, 1)
            with act.Fori(0, 2) as i:
                for q in range(6):
                    s = (p + q) % 2
                    for c in range(8):
                        tick(S_QKVG + 8 * q + c, 48, i)
                        if (q, c) == (0, 4):
                            act.wait_ge(kk_ssq, lin(1, 1, i))
                            for j in range(2):
                                a(T2[:, 2 * j:2 * j + 2, :].rearrange("p a b -> p (a b)"), BK[j][:, :], ACT.Sqrt)\
                                    .then_inc(kk_root, 1)
                        if (q, c) == (1, 2):
                            act.wait_ge(dec_in, lin(1, 1, i))
                            a(T4[:, :, :], T4[:, :, :], ACT.Exp, scale=-C_DECAY).then_inc(dec_exp, 1)
                            a(RWA[:, bass.ds(4 * i, 4), :], T2[:, :, :], ACT.Exp, scale=-C_DECAY)\
                                .then_inc(dec_exp, 1)
                            a(T2[:, :, :], T2[:, :, :], ACT.Exp, scale=C_DECAY).then_inc(dec_exp, 1)
                            a(ES[:, bass.ds(4 * i, 4)], MD[:, :], ACT.Exp, scale=-C_DECAY).then_inc(dec_exp, 1)
                    panel_end(S_QKVG + 8 * q + 7, 48, i)
                    if q < 2:
                        a(BR[:, bass.ds(i, 1), 4 * q:4 * q + 4, :].rearrange("p o a b -> p (o a) b"),
                          DP[s][:, :, :], ACT.Copy).then_inc(set_free[s], 1)
                    elif q < 4:
                        for t in range(2):
                            lo_t = 8 + 4 * t + 2 * (q - 2)
                            ins = a(BR[:, bass.ds(i, 1), lo_t:lo_t + 2, :].rearrange("p o a b -> p (o a) b"),
                                    DP[s][:, 2 * t:2 * t + 2, :], ACT.Copy)
                        ins.then_inc(set_free[s], 1)
                    else:
                        if q == 5:
                            act.wait_ge(set_free[1 - s], lin((p + 4) // 2 + 2, 3, i))
                        a(SG[:, :, :], DP[s][:, :, :], ACT.Sigmoid).then_inc(g_sig, 1)
            p += 12
            act.wait_ge(trig_in, 2)
            a(SIN[:, :], SIN[:, :], ACT.Sin).then_inc(trig_out, 1)
            a(COS[:, :], COS[:, :], ACT.Sin).then_inc(trig_out, 1)

            def o_read(k, bank, hd):
                act.wait_ge(ov_mm, k + 1)
                a(OA[:, 2 * hd:2 * hd + 2, :].rearrange("p a b -> p (a b)"), BK[bank][:, :], ACT.Copy)\
                    .then_inc(ov_read, 1)

            def head_norm(b):
                act.wait_ge(ov_read, 4 * b + 4)
                a(SQA[:, :, :], OA[:, :, :], ACT.Square).then_inc(on_sq, 1)
                act.wait_ge(on_ssq, b + 1)
                for j in range(2):
                    a(RS4[:, 2 * j:2 * j + 2, :].rearrange("p a b -> p (a b)"), BK[j][:, :], ACT.Sqrt,
                      scale=1.0 / DV, bias=EPSC).then_inc(on_root, 1)

            for hd in range(HEADS):
                o_read(hd, 2 + hd % 2, hd)
            head_norm(0)
            act.wait_ge(gdec_in, 1)
            a(GI[:, :, :], GD[:, :, :], ACT.Exp, scale=1.0 / 16).then_inc(gdec_exp, 1)
            a(GD[:, :, :], GD[:, :, :], ACT.Exp, scale=-1.0 / 16).then_inc(gdec_exp, 1)
            a(GES[:, :], GMD[:, :], ACT.Exp, scale=1.0 / 16).then_inc(gdec_exp, 1)
            act.wait_ge(gdec_exp, 3)
            act.wait_ge(o_final, 1)
            for hd in range(HEADS):
                act.wait_ge(gkt_mm, hd + 1)
                a(GKT[:, hd % 2, :], BK[1][:, 0:P], ACT.Copy).then_inc(gkt_read, 1)
                act.wait_ge(gs_mm, hd + 1)
                a(GS[:, hd % 2, :], BK[2][:, 0:DV], ACT.Copy, scale=GES[:, hd:hd + 1]).then_inc(gs_read, 1)
                o_read(4 + hd, 3, hd)
            head_norm(1)
            for b in range(2):
                act.wait_ge(o_final, b + 1)
                a(OP[b][:, 0, :, :], BR[:, b, 0:8, :], ACT.Copy).then_inc(op_hi, 1)
            for b in range(2):
                base = S_GB + 48 * b
                with act.Fori(0, 4) as i:
                    def rank(value, per=1):
                        return lin(per * 4 * b + value, per, i)

                    for k in range(12):
                        tick(base + k, 12, i)
                        if k == 1:
                            act.wait_ge(t0_mm, rank(1))
                            a(TM[:, :, :].rearrange("p a b -> p (a b)"), BK[0][:, :], ACT.Copy).then_inc(t0_read, 1)
                            act.wait_ge(vt_mm, rank(2))
                            a(VP[:, :, 0:4:3, :], BK[2][:, 0:2 * P].rearrange("p (c e q) -> p c e q", c=2, e=2),
                              ACT.Copy)
                            a(BKT[:, :, :].rearrange("p a b -> p (a b)"), BK[2][:, 2 * P:], ACT.Copy)\
                                .then_inc(vt_read, 1)
                        elif 2 <= k < 8:
                            act.wait_ge(p1_mm, rank(k - 1, LEVELS - 1))
                            a(P1S[:, :, :].rearrange("p a b -> p (a b)"), BK[1][:, :], ACT.Copy).then_inc(p1_read, 1)
                        elif k in (8, 9):
                            act.wait_ge(rhs_mm, rank(k - 7, 2))
                            a(RH[:, :], BK[0][:, 0:P], ACT.Copy).then_inc(rhs_read, 1)
                        if k in (8, 10):
                            c = (k - 8) // 2
                            act.wait_ge(u_mm, rank(c + 1, 2))
                            a(UP[:, c, 0:4:3, :], BK[1][:, 0:P].rearrange("p (e q) -> p e q", e=2), ACT.Copy)\
                                .then_inc(u_read, 1)
                        if k == 10:
                            act.wait_ge(y_mm, rank(2))
                            a(YS[:, :], BK[3][:, 0:T], ACT.Copy).then_inc(y_read, 1)
                        if k == 11:
                            act.wait_ge(centred, rank(1))
                            a(SQS[:, :], KRV[:, bass.ds(MT + 4 * b + i, 1), :].rearrange("p a b -> p (a b)"),
                              ACT.Square).then_inc(var_sq, 1)
                            act.wait_ge(var_mm, rank(1))
                            a(RWA[:, bass.ds(4 * b + i, 1), :].rearrange("p a b -> p (a b)"), BK[2][:, 0:T],
                              ACT.Copy).then_inc(var_read, 1)
                        if k == 7:
                            panel_end(base + 7, 12, i)
                            if b == 0:
                                a(MG[:, bass.ds(4 * i, 4), :], DP[p % 2][:, :, :], ACT.Sigmoid)\
                                    .then_inc(set_free[p % 2], 1)
                            else:
                                act.wait_ge(merged, lin(1, 1, i))
                                a(GT1[:, :, :], DP[p % 2][:, :, :], ACT.Sigmoid).then_inc(set_free[p % 2], 1)
                p += 8
            act.wait_ge(var_read, 9)
            a(RT8[:, :, :], RWA[:, :, :], ACT.Sqrt, scale=1.0 / 64, bias=GNEPSC).then_inc(gn_root, 1)
            for t in range(MT):
                act.wait_ge(g_mm, t + 1)
                a(GG[:, t, :], BK[t % 4][:, 0:T], ACT.Copy).then_inc(g_read, 1)
            act.wait_ge(merged, 5)
            for q in range(4):
                for c in range(8):
                    tick(S_RW + 8 * q + c)
                panel_end(S_RW + 8 * q + 7)
                a(GB[:, 4 * q:4 * q + 4, :], DP[p % 2][:, :, :], ACT.Sigmoid).then_inc(set_free[p % 2], 1)
                p += 1
            act.wait_ge(orw, 1)
            a(OPR[0][:, :, :], KRV[:, MT:2 * MT, :], ACT.Copy).then_inc(orw, 1)
            for q in range(4):
                for c in range(4):
                    tick(S_RW + 32 + 4 * q + c)
                act.wait_ge(merged, 6 + q)
                a(HH[:, 4 * q:4 * q + 4, :], MG[:, 4 * q:4 * q + 4, :], ACT.Copy).then_inc(mg_hi, 1)
                p += 1
            for q in range(4):
                for c in range(8):
                    tick(S_O + 8 * q + c)
                act.wait_ge(set_free[p % 2], p // 2 + 2)
                squares(XR, SQ, q)
                p += 1
            root(SQ, RS)

            act.wait_ge(conv_done, 1)

            def ffn(w, n, step, i, s, pc, tiles=2):
                panel_end(n, step, i)
                a(ZB[:, 0:tiles, 2:], DP[s][:, 0:tiles, :], ACT.Copy).then_inc(z_in, 1)
                act.wait_ge(conv_done, lin(w + 2, 2, i))
                a(GE[:, 0:tiles, :], CV[:, 0:tiles, :], ACT.Gelu_apprx_tanh).then_inc(gelu_done, 1)
                act.wait_ge(set_free[s], lin(pc // 2 + 2, 1, i))
                tile = 2 * w if i is None else 2 * w + 4 * i
                a(AH[:, bass.ds(tile, tiles), :], AV[:, 0:tiles, :], ACT.Copy).then_inc(act_hi, 1)

            with act.Fori(0, 10) as i:
                for q in range(2):
                    for c in range(8):
                        tick(S_UP + 8 * q + c, 16, i)
                    ffn(q, S_UP + 8 * q + 7, 16, i, (p + q) % 2, p + q)
            p += 20
            for c in range(8):
                tick(S_UP + 160 + c)
            ffn(20, S_UP + 167, 0, None, p % 2, p)
            p += 1
            for c in range(4):
                tick(S_UP + 168 + c)
            ffn(21, S_UP + 171, 0, None, p % 2, p, 1)
            p += 1
            with act.Fori(0, 2) as i:
                for c in range(44):
                    tick(S_DOWN + c, 44, i)
            p += 4
            act.wait_ge(p_loaded, 16)
            a(PXH[:, :, :], PX[:, :, :], ACT.Copy).then_inc(p_hi, 1)
            act.wait_ge(act_lo, 22)
            for g in range(4):
                act.wait_ge(set_free[(p - 4 + g) % 2], (p - 4 + g) // 2 + 2)
                squares(XR, SQ, g)
            for q in range(4):
                tick(S_PLE + q)
                panel_end(S_PLE + q)
                a(PG[:, 4 * q:4 * q + 4, :], DP[p % 2][:, :, :], ACT.Copy).then_inc(set_free[p % 2], 1)
                p += 1
            root(SQ, RS)
            for q in range(4):
                for c in range(8):
                    tick(S_PLE + 4 + 8 * q + c)
                panel_end(S_PLE + 11 + 8 * q)
                if q:
                    act.wait_ge(ple_used, q)
                a(GP[:, :, :], DP[p % 2][:, :, :], ACT.Sigmoid).then_inc(set_free[p % 2], 1)
                act.wait_ge(ple_used, q + 1)
                squares(XR, SQ, q)
                p += 1
            root(SQ, RS)

        @block.vector
        def _(dve):
            v = nc.vector
            steps = Steps(dve, dve_step)
            link = steps.link

            def lo(n, step=0, i=None):
                slot = n % RING
                dve.wait_ge(hi_ready, lin(n + 1, step, i))
                v.tensor_tensor(WL[:, slot, :], RAW[:, slot, :], WH[:, slot, :].bitcast(F32), ALU.subtract)\
                    .then_inc(lo_ready, 1)

            def tick(n, step=0, i=None):
                if n + 3 < N_CHUNK:
                    lo(n + 3, step, i)

            norms = [0]

            def normalise(x, sq, rs, gain):
                k = norms[0]
                dve.wait_ge(rs_root, k + 1)
                link(v.reciprocal(rs[:, :], rs[:, :]))
                for t in range(DT):
                    ins = v.scalar_tensor_tensor(out=sq[:, t, :], in0=x[:, t, :], scalar=prmc(gain, t), in1=rs[:, :],
                                                 op0=ALU.mult, op1=ALU.mult)
                    if t % 4 == 3:
                        ins.then_inc(h_ready, 1)
                if k < 3:
                    for g in range(4):
                        dve.wait_ge(hh_ready, 4 * k + g + 1)
                        t = slice(4 * g, 4 * g + 4)
                        v.tensor_tensor(HL[:, t, :], sq[:, t, :], HH[:, t, :].bitcast(F32), ALU.subtract)\
                            .then_inc(hl_ready, 1)
                norms[0] += 1

            v.memset(EPSC, EPS)
            v.memset(GNEPSC, GN_EPS)
            link(v.memset(ROW1[:, :], 1.0))
            v.memset(UBUF[:, :, 0:1], 0.0).then_inc(set_free[0], 1)
            v.memset(DBUF[:, :, 0:1], 0.0).then_inc(set_free[1], 1)
            for n in range(3):
                lo(n)
            dve.wait_ge(prm_loaded[0], 16)
            normalise(X0, SQ0, RSTD, "mix")
            p = 0

            def shift(pv, s, dest, mu, step=0, i=None, tiles=4):
                dve.wait_ge(set_free[s], lin(pv // 2 + 2, step // 2, i))
                link(v.tensor_tensor(DBUF[:, 0:tiles, :], UBUF[:, 0:tiles, 0:T], UBUF[:, 0:tiles, 1:T + 1],
                                     ALU.subtract))
                for m in range(tiles):
                    ins = v.scalar_tensor_tensor(out=dest(m), in0=DBUF[:, m, :], scalar=mu(m),
                                                 in1=UBUF[:, m, 1:T + 1], op0=ALU.mult, op1=ALU.add)
                ins.then_inc(shift_out, 1)

            for c in range(8):
                tick(S_MISC + c)
            shift(0, 0, lambda m: MISC[:, m, :], lambda m: prmc("mu", 24 + m), tiles=3)
            p = 1
            with dve.Fori(0, 3) as i:
                steps.enter(i, 2)
                for q in range(2):
                    for c in range(8):
                        tick(S_KRV + 8 * q + c, 16, i)
                    shift(p + q, (p + q) % 2,
                          lambda m: KRV[:, bass.ds(8 * i + 4 * q + m, 1), :].rearrange("p a b -> p (a b)"),
                          lambda m: PRM[:, bass.ds(8 * i + 4 * q + m + COL["mu"][0], 1)], 2, i)
            steps.leave(3)
            p += 6
            dve.wait_ge(lora_read, 20)
            link(v.tensor_scalar(LT2[:, :, :], LG[:, :, :], 0.0, None, ALU.min))
            dve.wait_ge(log_sp, 1)
            link(v.tensor_tensor(LG[:, :, :], LT2[:, :, :], LT1[:, :, :], ALU.subtract))
            dve.wait_ge(shift_out, 7)
            with dve.Fori(0, 2) as i:
                steps.enter(i, 12)
                kx, rx = KRV[:, bass.ds(4 * i, 4), :], KRV[:, bass.ds(4 * i + MT, 4), :]
                ax, bx = RWA[:, bass.ds(4 * i, 4), :], RWB[:, bass.ds(4 * i, 4), :]

                def chan(name):
                    return bcast(PRM[:, bass.ds(4 * i + COL[name][0], 4)], T)

                for q in range(6):
                    s = (p + q) % 2
                    for c in range(8):
                        tick(S_QKVG + 8 * q + c, 48, i)
                        if (q, c) == (0, 1):
                            link(v.tensor_tensor(T1[:, :, :], kx, chan("k_k"), ALU.mult))
                            v.tensor_tensor(T2[:, :, :], T1[:, :, :], T1[:, :, :], ALU.mult).then_inc(kk_sq, 1)
                        elif (q, c) == (0, 5):
                            dve.wait_ge(kk_root, lin(2, 2, i))
                            link(v.tensor_scalar(T2[:, :, :], T2[:, :, :], 1e-12, None, ALU.max))
                            link(v.reciprocal(T2[:, :, :], T2[:, :, :]))
                            link(v.tensor_tensor(T1[:, :, :], T1[:, :, :], T2[:, :, :], ALU.mult))
                        elif (q, c) == (0, 6):
                            link(v.scalar_tensor_tensor(out=T2[:, :, :], in0=bx, scalar=-1.0, in1=chan("k_a"),
                                                        op0=ALU.add, op1=ALU.mult))
                            link(v.scalar_tensor_tensor(out=kx, in0=T2[:, :, :], scalar=1.0, in1=kx,
                                                        op0=ALU.add, op1=ALU.mult))
                        elif (q, c) == (0, 7):
                            v.scalar_tensor_tensor(out=T3[:, :, :], in0=T1[:, :, :], scalar=-1.0, in1=bx,
                                                   op0=ALU.mult, op1=ALU.mult)
                            for m in range(4):
                                ins = v.tensor_tensor_scan(
                                    T4[:, m, :], ROW1[:, :],
                                    RWA[:, bass.ds(4 * i + m, 1), :].rearrange("p a b -> p (a b)"),
                                    0.0, ALU.mult, ALU.add)
                            link(ins)
                        elif (q, c) == (1, 0):
                            mid = T4[:, :, :].rearrange("p m (c t) -> p (m c) t", c=NC)[:, :, 63:64]
                            link(v.tensor_tensor(T2[:, :, :].rearrange("p m (c t) -> p (m c) t", c=NC),
                                                 T4[:, :, :].rearrange("p m (c t) -> p (m c) t", c=NC),
                                                 mid.to_broadcast([P, 4 * NC, CL]), ALU.subtract))
                            link(v.tensor_tensor(MD[:, :], T4[:, :, 191:192].rearrange("p a b -> p (a b)"),
                                                 T4[:, :, 63:64].rearrange("p a b -> p (a b)"), ALU.subtract))
                            v.tensor_tensor(T4[:, :, :], T2[:, :, :], ax, ALU.subtract).then_inc(dec_in, 1)
                        elif (q, c) == (1, 4):
                            dve.wait_ge(dec_exp, lin(4, 4, i))
                            link(v.tensor_tensor(rx, rx, ax, ALU.mult))
                            link(v.tensor_tensor(ax, T1[:, :, :], T4[:, :, :], ALU.mult))
                        elif (q, c) == (1, 5):
                            link(v.tensor_tensor(kx, kx, T2[:, :, :], ALU.mult))
                            v.tensor_tensor(bx, T3[:, :, :], T2[:, :, :], ALU.mult).then_inc(rw_prep, 1)
                    if q >= 4:
                        dve.wait_ge(g_sig, lin(q - 3, 2, i))
                        v.tensor_tensor(BR[:, bass.ds(i, 1), 4 * q:4 * q + 4, :].rearrange("p o a b -> p (o a) b"),
                                        DP[s][:, :, :], SG[:, :, :], ALU.mult).then_inc(set_free[s], 1)
            steps.leave(2)
            p += 12
            two_pi = 2 * math.pi
            magic = 1.5 * 2 ** 23
            c1 = 6.28125
            c2 = float(np.float32(two_pi - c1) - np.float32(two_pi - c1) % np.float32(2.0 ** -19))
            c3 = two_pi - c1 - c2
            lim = 3.1415925
            dve.wait_ge(pos_loaded, 16)
            link(v.tensor_copy(RA[:, :], PI32[:, :]))
            link(v.tensor_scalar(RA[:, :], RA[:, :], prmc("invf", 0), None, ALU.mult))
            link(v.tensor_scalar(RB[:, :], RA[:, :], 1 / two_pi, magic, ALU.mult, ALU.add))
            link(v.tensor_scalar(RB[:, :], RB[:, :], -magic, None, ALU.add))
            for ck in (c1, c2, c3):
                link(v.scalar_tensor_tensor(out=RA[:, :], in0=RB[:, :], scalar=-ck, in1=RA[:, :], op0=ALU.mult,
                                            op1=ALU.add))
            v.tensor_scalar(SIN[:, :], RA[:, :], lim, -lim, ALU.min, ALU.max).then_inc(trig_in, 1)
            link(v.tensor_scalar(RB[:, :], RA[:, :], math.pi / 2, None, ALU.add))
            link(v.tensor_scalar(RT[:, 0, :], RB[:, :], math.pi, -two_pi, ALU.is_gt, ALU.mult))
            link(v.tensor_tensor(RB[:, :], RB[:, :], RT[:, 0, :], ALU.add))
            v.tensor_scalar(COS[:, :], RB[:, :], lim, -lim, ALU.min, ALU.max).then_inc(trig_in, 1)
            dve.wait_ge(trig_out, 2)
            sin2 = SIN[:, :].unsqueeze(1).to_broadcast([P, 2, T])
            cos2 = COS[:, :].unsqueeze(1).to_broadcast([P, 2, T])
            for m in range(4):
                x = BR[:, 0, 2 * m:2 * m + 2, :]
                dve.wait_ge(rope_mm, m + 1)
                v.tensor_tensor(RT[:, :, :], BK[m % 2][:, :].rearrange("p (a b) -> p a b", a=2), sin2, ALU.mult)\
                    .then_inc(rope_read, 1)
                link(v.tensor_tensor(x, x, cos2, ALU.mult))
                dve.wait_ge(rope_read, m + 1)
                v.tensor_tensor(x, x, RT[:, :, :], ALU.add).then_inc(rope_done, 1)
                dve.wait_ge(rope_done, m + 1)
            dve.wait_ge(dm_loaded, 16)
            for hd in range(HEADS):
                dve.wait_ge(sc_mm, hd + 1)
                if hd >= 2:
                    dve.wait_ge(ov_mm, hd - 1)
                v.tensor_tensor(SR[:, hd % 2, :], BK[hd % 2][:, 0:384], DM[:, hd, :], ALU.mult).then_inc(sc_read, 1)

            def head_scale(b):
                dve.wait_ge(on_root, 2 * b + 2)
                link(v.reciprocal(RS4[:, :, :], RS4[:, :, :]))
                o4 = OA[:, :, :].rearrange("p (h e) t -> p h e t", h=HEADS)
                for e in range(2):
                    if b == 0:
                        ins = v.tensor_tensor(o4[:, :, e, :], o4[:, :, e, :], RS4[:, :, :], ALU.mult)
                    else:
                        ins = v.scalar_tensor_tensor(out=o4[:, :, e, :], in0=o4[:, :, e, :], scalar=prmc("gnorm", e),
                                                     in1=RS4[:, :, :], op0=ALU.mult, op1=ALU.mult)
                link(ins)
                v.tensor_tensor(BR[:, b, 0:8, :], OA[:, :, :], BR[:, b, 16:24, :], ALU.mult).then_inc(o_final, 1)

            head_scale(0)
            for hd in range(HEADS):
                ins = v.tensor_tensor_scan(GI[:, hd, :], ROW1[:, :], LG[:, hd, :], 0.0, ALU.mult, ALU.add)
            link(ins)
            gi = GI[:, :, :].rearrange("p m (c t) -> p (m c) t", c=NC)
            v.tensor_tensor(GD[:, :, :].rearrange("p m (c t) -> p (m c) t", c=NC), gi,
                            gi[:, :, 63:64].to_broadcast([P, HEADS * NC, CL]), ALU.subtract)
            v.tensor_tensor(GMD[:, :], GI[:, :, 191:192].rearrange("p a b -> p (a b)"),
                            GI[:, :, 63:64].rearrange("p a b -> p (a b)"), ALU.subtract).then_inc(gdec_in, 1)
            v.memset(GSC[:, :, :, :], 0.0)
            dve.wait_ge(gdec_exp, 3)
            v.scalar_tensor_tensor(out=BR[:, 1, 0:4, :], in0=BR[:, 1, 0:4, :], scalar=DK ** -0.5, in1=GI[:, :, :],
                                   op0=ALU.mult, op1=ALU.mult)
            v.tensor_tensor(BR[:, 1, 4:8, :], BR[:, 1, 4:8, :], GD[:, :, :], ALU.mult).then_inc(gqk, 1)
            dve.wait_ge(gqk, 1)
            dve.wait_ge(masks_set, 1)
            for hd in range(HEADS):
                dve.wait_ge(sc_mm, 4 + hd + 1)
                if hd >= 2:
                    dve.wait_ge(ov_mm, 4 + hd - 1)
                v.copy_predicated(GSC[:, hd % 2, :, :], mask(1, 2), BK[0][:, 0:T].rearrange("p (c t) -> p c t", c=2))\
                    .then_inc(sc_read, 1)
            head_scale(1)
            for b in range(2):
                dve.wait_ge(op_hi, b + 1)
                v.tensor_tensor(OP[b][:, 1, :, :], BR[:, b, 0:8, :], OP[b][:, 0, :, :].bitcast(F32), ALU.subtract)\
                    .then_inc(op_lo, 1)
            count_reg = dve.alloc_register("count")
            for b in range(2):
                base = S_GB + 48 * b
                with dve.Fori(0, 4) as i:
                    steps.enter(i, 0)

                    def rank(value, per=1):
                        return lin(per * 4 * b + value, per, i)

                    def pair(x, k0):
                        return x[:, bass.ds(k0 + 4 * b + i, 1), :].rearrange("p a b -> p (a b)")

                    def masked_wait(s, count):
                        dve.reg_mov(count_reg, count)
                        dve.wait_ge(masks_set, 1)
                        dve.wait_ge(s, count_reg)

                    for k in range(12):
                        if k == 0:
                            masked_wait(bgram, rank(1))
                            for c in range(NC):
                                g = BK[c][:, :].rearrange("p (e x t) -> p e x t", e=2, x=2)
                                u = slice(2 * c, 2 * c + 2)
                                v.copy_predicated(XT[:, u, :], mask(0, 2), g[:, :, 0, :])
                                v.copy_predicated(ZM[:, u, :], mask(2, 2), g[:, :, 0, :])
                                ins = v.copy_predicated(GRB[:, u, :], mask(1, 2), g[:, :, 1, :])
                            ins.then_inc(bgram_read, 1)
                        if 2 <= k < 8:
                            lv = k - 1
                            masked_wait(delta_mm, rank(lv, LEVELS - 1))
                            if lv < LEVELS - 1:
                                v.copy_predicated(TM[:, :, :], mask(8 + lv, 4),
                                                  BK[2][:, :].rearrange("p (u t) -> p u t", u=4))
                            v.copy_predicated(ZM[:, :, :], mask(2 + lv, 4),
                                              BK[3][:, :].rearrange("p (u t) -> p u t", u=4)).then_inc(t_grown, 1)
                        if k == 9:
                            dve.wait_ge(s_mm, rank(1))
                            for e in range(2):
                                w = slice(64 * e, 64 * e + 64)
                                ins = v.tensor_scalar(SB[w, w], BK[2][w, w], ES[w, bass.ds(4 * b + i, 1)], None,
                                                      ALU.mult)
                            ins.then_inc(s_read, 1)
                        tick(base + k, 12, i)
                        if k == 0:
                            masked_wait(kgram, rank(1))
                            for c in range(NC):
                                g = BK[2 + c][:, :].rearrange("p (e x t) -> p e x t", e=2, x=2)
                                u = slice(2 * c, 2 * c + 2)
                                v.copy_predicated(LAK[:, u, :], mask(0, 2), g[:, :, 0, :])
                                ins = v.copy_predicated(GRK[:, u, :], mask(1, 2), g[:, :, 1, :])
                            ins.then_inc(kgram_read, 1)
                        if k == 11:
                            dve.wait_ge(mean_mm, rank(2))
                            v.scalar_tensor_tensor(out=pair(KRV, MT), in0=BK[0][:, 0:T], scalar=-1.0 / 64,
                                                   in1=YS[:, :], op0=ALU.mult, op1=ALU.add).then_inc(centred, 1)
                            v.tensor_tensor(pair(KRV, 2 * MT), BK[1][:, 0:T], pair(KRV, 2 * MT), ALU.mult)\
                                .then_inc(bonus_done, 1)
                            s = (p + 1) % 2
                            dve.wait_ge(chunk_done, lin(base + 12, 12, i))
                            mg = MG[:, bass.ds(4 * i, 4), :]
                            if b == 0:
                                v.tensor_tensor(mg, DP[s][:, :, :], mg, ALU.mult).then_inc(set_free[s], 1)
                            else:
                                v.tensor_tensor(GT1[:, :, :], DP[s][:, :, :], GT1[:, :, :], ALU.mult)\
                                    .then_inc(set_free[s], 1)
                                dve.wait_ge(set_free[s], lin((p + 1) // 2 + 2, 1, i))
                                v.tensor_tensor(mg, mg, GT1[:, :, :], ALU.add).then_inc(merged, 1)
                steps.leave(4)
                p += 8
            y = KRV[:, MT:2 * MT, :]
            for q in range(4):
                for c in range(8):
                    tick(S_RW + 8 * q + c)
                    if (q, c) == (0, 0):
                        dve.wait_ge(gn_root, 1)
                        link(v.reciprocal(RT8[:, :, :], RT8[:, :, :]))
                    elif (q, c) == (0, 2):
                        link(v.tensor_tensor(y, y, RT8[:, :, :], ALU.mult))
                    elif (q, c) == (0, 4):
                        for t in range(MT):
                            ins = v.tensor_scalar(KRV[:, MT + t, :], KRV[:, MT + t, :], prmc("ln_w", t),
                                                  prmc("ln_b", t), ALU.mult, ALU.add)
                        link(ins)
                    elif (q, c) == (0, 6):
                        link(v.tensor_tensor(y, y, KRV[:, 2 * MT:3 * MT, :], ALU.add))
                    elif (q, c) == (1, 0):
                        dve.wait_ge(g_read, 8)
                        v.tensor_tensor(y, y, GG[:, :, :], ALU.mult).then_inc(orw, 1)
                p += 1
            dve.wait_ge(orw, 2)
            v.tensor_tensor(OPR[1][:, :, :], y, OPR[0][:, :, :].bitcast(F32), ALU.subtract).then_inc(orw_lo, 1)
            for q in range(4):
                t = slice(4 * q, 4 * q + 4)
                for c in range(4):
                    tick(S_RW + 32 + 4 * q + c)
                dve.wait_ge(chunk_done, S_RW + 32 + 4 * q + 4)
                v.tensor_tensor(GTM[:, :, :], DP[p % 2][:, :, :], GB[:, t, :], ALU.mult).then_inc(set_free[p % 2], 1)
                dve.wait_ge(set_free[p % 2], p // 2 + 2)
                v.tensor_tensor(MG[:, t, :], MG[:, t, :], GTM[:, :, :], ALU.add).then_inc(merged, 1)
                dve.wait_ge(mg_hi, q + 1)
                v.tensor_tensor(HL[:, t, :], MG[:, t, :], HH[:, t, :].bitcast(F32), ALU.subtract).then_inc(mg_lo, 1)
                p += 1
            dve.wait_ge(x_again, 16)
            for q in range(4):
                t = slice(4 * q, 4 * q + 4)
                for c in range(8):
                    tick(S_O + 8 * q + c)
                dve.wait_ge(chunk_done, S_O + 8 * q + 8)
                v.tensor_tensor(XR[:, t, :], DP[p % 2][:, :, :], XR[:, t, :], ALU.add).then_inc(set_free[p % 2], 1)
                p += 1
            normalise(XR, SQ, RS, "ffn")
            dve.wait_ge(hl_ready, 8)
            link(v.memset(ZB[:, :, 0:2], 0.0))

            def ffn(w, s, i, vtile=2, tiles=2):
                def par(name, m):
                    return PRM[:, bass.ds((0 if i is None else 4 * i) + 2 * w + m + COL[name][0], 1)]

                dve.wait_ge(z_in, lin(w + 1, 2, i))
                for m in range(tiles):
                    ins = v.tensor_scalar(CV[:, m, :], ZB[:, m, 2:T + 2], par("cw2", m), par("cb", m), ALU.mult,
                                          ALU.add)
                link(ins)
                for j in (1, 0):
                    for m in range(tiles):
                        ins = v.scalar_tensor_tensor(out=CV[:, m, :], in0=ZB[:, m, j:T + j], scalar=par(f"cw{j}", m),
                                                     in1=CV[:, m, :], op0=ALU.mult, op1=ALU.add)
                    if j == 1:
                        link(ins)
                ins.then_inc(conv_done, 1)
                dve.wait_ge(gelu_done, lin(w + 1, 2, i))
                v.tensor_tensor(AV[:, 0:tiles, :], DP[s][:, vtile:vtile + tiles, :], GE[:, 0:tiles, :], ALU.mult)\
                    .then_inc(set_free[s], 1)
                dve.wait_ge(act_hi, lin(w + 1, 2, i))
                tile = 2 * w if i is None else 2 * w + 4 * i
                v.tensor_tensor(AL[:, bass.ds(tile, tiles), :], AV[:, 0:tiles, :],
                                AH[:, bass.ds(tile, tiles), :].bitcast(F32), ALU.subtract).then_inc(act_lo, 1)

            v.memset(CV[:, :, :], 0.0).then_inc(conv_done, 1)
            with dve.Fori(0, 10) as i:
                steps.enter(i, 4)
                for q in range(2):
                    for c in range(8):
                        tick(S_UP + 8 * q + c, 16, i)
                    ffn(q, (p + q) % 2, i)
            steps.leave(10)
            p += 20
            for c in range(8):
                tick(S_UP + 160 + c)
            ffn(20, p % 2, None)
            p += 1
            for c in range(4):
                tick(S_UP + 168 + c)
            ffn(21, p % 2, None, vtile=1, tiles=1)
            p += 1
            with dve.Fori(0, 2) as i:
                for q in range(2):
                    for c in range(22):
                        tick(S_DOWN + 22 * q + c, 44, i)
                    s = (p + q) % 2
                    dve.wait_ge(chunk_done, lin(S_DOWN + 22 * q + 22, 44, i))
                    xr = XR[:, bass.ds(8 * i + 4 * q, 4), :]
                    v.tensor_tensor(xr, DP[s][:, :, :], xr, ALU.add).then_inc(set_free[s], 1)
            p += 4
            dve.wait_ge(p_hi, 1)
            v.tensor_tensor(PXL[:, :, :], PX[:, :, :], PXH[:, :, :].bitcast(F32), ALU.subtract).then_inc(p_lo, 1)
            for q in range(4):
                tick(S_PLE + q)
                p += 1
            normalise(XR, SQ, RS, "ple")
            for q in range(4):
                t = slice(4 * q, 4 * q + 4)
                for c in range(8):
                    tick(S_PLE + 4 + 8 * q + c)
                dve.wait_ge(set_free[p % 2], p // 2 + 2)
                link(v.tensor_tensor(GP[:, :, :], GP[:, :, :], PG[:, t, :], ALU.mult))
                v.tensor_tensor(XR[:, t, :], XR[:, t, :], GP[:, :, :], ALU.add).then_inc(ple_used, 1)
                p += 1
            normalise(XR, SQ, RS, "fin")

        @block.gpsimd
        def _(pool):
            g = nc.gpsimd
            pool.dma_start(CST[:, :, :], const).then_inc(prm_loaded[1], 16)
            pool.dma_start(PRM[:, :], prm).then_inc(prm_loaded[0], 16)
            pool.dma_start(MSKI[:, :, :], masks).then_inc(prm_loaded[2], 16)
            pool.wait_ge(prm_loaded[2], 16)
            g.tensor_copy(MSK[:, :, :], MSKI[:, :, :]).then_inc(masks_set, 1)
            pool.wait_ge(hl_ready, 4)
            pool.dma_start(LORA[:, 0:3, :], lora[:, 0:3, :]).then_inc(lora_loaded, 16)
            pool.wait_ge(rw_prep, 2)
            pool.wait_ge(set_free[1], 10)
            pool.wait_ge(set_free[0], 11)
            pool.dma_start(PI32[:, :], pos).then_inc(pos_loaded, 16)
            pool.dma_start(DM[:, :, :], dmask).then_inc(dm_loaded, 16)
            pool.wait_ge(op_lo, 2)
            for x, s in ((XT, zeroed), (LAK, zeroed), (GRB, zeroed), (GRK, zeroed),
                         (UP, zeroed), (VP, zeroed), (SB, zeroed), (BS, vt_mm), (AR, y_mm), (PR, mean_mm),
                         (YS, bonus_done), (SQS, var_read), (RH, merged)):
                g.memset(x[tuple(slice(None) for _ in x.shape)], 0.0).then_inc(s, 1)
            pool.wait_ge(zeroed, 7)
            for b in range(2):
                with pool.Fori(0, 4) as i:
                    def rank(value, per=1):
                        return lin(per * 4 * b + value, per, i)

                    def pair(x, k0, rows=slice(None), cols=slice(None)):
                        return x[rows, bass.ds(k0 + 4 * b + i, 1), cols].rearrange("p a b -> p (a b)")

                    pool.wait_ge(vt_mm, rank(1))
                    g.tensor_copy(BS[:, :], pair(RWB, 0)).then_inc(staged, 1)
                    g.tensor_copy(KS[:, :], pair(KRV, 0)).then_inc(staged, 1)
                    g.tensor_copy(VS[:, :], pair(KRV, 2 * MT)).then_inc(staged, 1)
                    pool.wait_ge(y_mm, rank(1))
                    g.tensor_copy(AR[:, :, 0, :], pair(RWA, 0).rearrange("p (c t) -> p c t", c=NC)).then_inc(staged, 1)
                    g.tensor_copy(AR[:, :, 1, :], pair(KRV, MT).rearrange("p (c t) -> p c t", c=NC))\
                        .then_inc(staged, 1)
                    g.tensor_copy(ZM[:, :, :], IDENT.unsqueeze(1).to_broadcast([P, 4, P])).then_inc(staged, 1)
                    pool.wait_ge(mean_mm, rank(1))
                    g.tensor_copy(RKC, PRM[:, bass.ds(COL["r_k"][0] + 4 * b + i, 1)]).then_inc(staged, 1)
                    pool.wait_ge(staged, rank(7, STAGED))
                    half = BLK[:, 0:P:64].unsqueeze(2).to_broadcast([P, 2, T])
                    for x, src in ((BP, BS), (KP, KS)):
                        g.tensor_tensor(x[:, :, :], src[:, :].unsqueeze(1).to_broadcast([P, 2, T]), half, ALU.mult)\
                            .then_inc(staged, 1)
                    g.tensor_tensor(PR[:, :].rearrange("p (c t) -> p c t", c=NC), AR[:, :, 1, :],
                                    KS[:, :].rearrange("p (c t) -> p c t", c=NC), ALU.mult)\
                        .then_inc(staged, 1)
                    pool.wait_ge(staged, rank(STAGED - 1, STAGED))
                    g.tensor_tensor(PR[:, :], PR[:, :], RKC.to_broadcast([P, T]), ALU.mult).then_inc(staged, 1)
            pool.wait_ge(chunk_done, S_GB + 48)
            pool.dma_start(G2[:, :, :], lora[:, 3:5, :]).then_inc(g2_loaded, 16)
            pool.wait_ge(gn_root, 1)
            pool.dma_start(XR[:, :, :], xT).then_inc(x_again, 16)
            pool.wait_ge(chunk_done, S_DOWN)
            pool.dma_start(PX[:, :, :], pT).then_inc(p_loaded, 16)
            for k in range(4):
                pool.wait_ge(h_ready, 12 + k + 1)
                pool.dma_start(outT[:, 4 * k:4 * k + 4, :], SQ[:, 4 * k:4 * k + 4, :]).then_inc(out_stored, 16)
            pool.wait_ge(out_stored, 64)


def _layout(inputs):
    f = lambda k: np.asarray(inputs[k])[0]

    def rows(w, cols):
        w = w[:, cols]
        kt = -(-w.shape[0] // (2 * P)) * 2
        full = np.zeros((kt * P, 512), np.float32)
        full[:w.shape[0], :w.shape[1]] = w
        return full.reshape(kt // 2, 2, P, 512).transpose(0, 2, 1, 3).reshape(kt // 2, P, CH)

    def sl(a, n):
        return slice(a, a + n)

    w = f("w_in")
    up, down, wo = f("w_up"), f("w_down"), f("w_o")
    parts = [rows(np.concatenate([w[:, sl(RWKV0 + 3 * MW, 288)], w[:, sl(RWKV0 - GLA_LORA, GLA_LORA)]], 1),
                  slice(None))]
    for base in (RWKV0 + MW, RWKV0, RWKV0 + 2 * MW):
        parts += [rows(w, sl(base + 512 * j, 512)) for j in range(2)]
    for base in (RET0, GLA0):
        parts += [rows(w, sl(base + 512 * j, 512)) for j in range(6)]
    for gate, br in ((2, "w_br_ret"), (0, "w_br_gla")):
        for j in range(4):
            parts += [rows(w, sl(GATE0 + gate * D + 512 * j, 512)), rows(f(br), sl(512 * j, 512))]
    parts += [rows(w, sl(GATE0 + D + 512 * j, 512)) for j in range(4)]
    parts += [rows(f("w_br_rwkv"), sl(512 * j, 512)) for j in range(4)]
    parts += [rows(wo, sl(512 * j, 512)) for j in range(4)]
    for j in range(21):
        parts.append(rows(np.concatenate([up[:, sl(256 * j, 256)], up[:, sl(DFF + 256 * j, 256)]], 1), slice(None)))
    last = np.concatenate([up[:, sl(256 * 21, P)], up[:, sl(DFF + 256 * 21, P)]], 1)
    parts.append(last.reshape(4, 4, P, 256).transpose(0, 2, 1, 3).reshape(4, P, CH))
    parts += [rows(down, sl(512 * j, 512)) for j in range(4)]
    parts += [rows(f("w_ple_proj"), sl(512 * j, 512)) for j in range(4)]
    parts += [rows(f("w_ple_gate"), sl(512 * j, 512)) for j in range(4)]
    stream = np.concatenate(parts, 0)

    def col(x, n):
        x = np.asarray(x).reshape(-1)
        full = np.zeros(n * P, np.float32)
        full[:x.size] = x
        return full.reshape(n, P).T

    mu = f("rwkv_mu")
    mu = np.concatenate([mu[MW:2 * MW], mu[:MW], mu[2 * MW:]])
    invf = (np.float32(10000.0) ** (-np.arange(0, DK, 2, dtype=np.float32) / np.float32(DK))).astype(np.float32)
    cw = f("conv_w")
    cols = dict(mix=f("mix_norm"), ffn=f("ffn_norm"), ple=f("ple_norm"), fin=inputs["final_norm"], mu=mu,
                w0=f("rwkv_w0"), a0=f("rwkv_a0"), k_k=f("rwkv_k_k"), k_a=f("rwkv_k_a"), r_k=f("rwkv_r_k"),
                ln_w=f("rwkv_ln_w"), ln_b=f("rwkv_ln_b"), bdec=f("gla_b_decay"), gnorm=f("gla_norm"), cw0=cw[0],
                cw1=cw[1], cw2=cw[2], cb=f("conv_b"), invf=np.concatenate([invf, invf]), pad=np.zeros(1, np.float32))
    prm = np.concatenate([col(cols[n], k) for n, k in _COLS], 1)

    lora = np.zeros((P, 5, MW), np.float32)
    lora[0:64, 0] = f("rwkv_w2")
    lora[64:128, 1] = f("rwkv_a2")
    lora[32:48, 2, 0:512] = f("gla_w_decay")
    g2 = f("rwkv_g2")
    lora[:, 3] = g2[0:P]
    lora[0:32, 4] = g2[P:]

    a, b = np.arange(P)[:, None], np.arange(P)[None, :]
    const = np.zeros((P, 4, P), np.float32)
    const[:, 0] = a == b
    const[:, 1] = a // 64 == b // 64
    const[:, 2] = 1.0
    const[:, 3] = np.where(a == (b + 64) % P, np.where(b < 64, -1.0, 1.0), 0.0)
    masks = np.zeros((P, 14, P), np.int32)
    masks[:, 0] = a < b
    masks[:, 1] = a <= b
    for lv in range(LEVELS):
        m = 2 ** lv
        same = a // (2 * m) == b // (2 * m)
        masks[:, 2 + lv] = same & (a % (2 * m) < m) & (b % (2 * m) >= m)
        if 1 <= lv < LEVELS - 1:
            masks[:, 8 + lv] = same & (a % (2 * m) >= m) & (b % (2 * m) < m)
    gamma = 1.0 - 2.0 ** (-5.0 - np.arange(HEADS))
    diff = np.arange(T)[None, :] - a
    dm = np.stack([np.where(diff >= 0, gm ** np.maximum(diff, 0), 0.0) * DK ** -0.5 for gm in gamma], 1)
    dmask = np.concatenate([dm, dm[:, :, 0:P]], 2).astype(np.float32)

    def chan(x, n):
        return np.asarray(x).T.reshape(n, P, T).transpose(1, 0, 2)

    return dict(stream=stream, xT=chan(inputs["x"][0], DT), prm=prm, const=const, masks=masks, dmask=dmask,
                pos=np.broadcast_to(np.asarray(inputs["positions"]).reshape(1, T), (P, T)), lora=lora,
                pT=chan(f("p")[0], 2))


def kernel(**inputs):
    import concourse.bacc as bacc
    from concourse.bass_utils import run_bass_kernel_spmd

    nc = bacc.Bacc("TRN2", target_bir_lowering=False, num_devices=1)
    arrays, args = {}, []
    for name, x in _layout(inputs).items():
        x = np.ascontiguousarray(x)
        arrays[f"in_{name}"] = x
        args.append(nc.dram_tensor(f"in_{name}", x.shape, mybir.dt.from_np(x.dtype), kind="ExternalInput").ap())
    out = nc.dram_tensor("out", (P, DT, T), F32, kind="ExternalOutput").ap()
    bass_hybrid_block(nc, *args, out)
    got = run_bass_kernel_spmd(nc, [arrays], core_ids=[0]).results[0]["out"]
    return np.ascontiguousarray(got.transpose(2, 1, 0).reshape(1, T, D))
```

```python
import math
from contextlib import ExitStack

import numpy as np

import concourse.bass as bass
from concourse import mybir

F32 = mybir.dt.float32
F32R = mybir.dt.float32r
I32 = mybir.dt.int32
U8 = mybir.dt.uint8
ALU = mybir.AluOpType
ACT = mybir.ActivationFunctionType

P = 128
T = 256
D = 2048
MW = 1024
DFF = 5504
PLE = 256
DT, MT, FT = D // P, MW // P, DFF // P
HEADS = 4
DK = 128
DV = 256
GLA_LORA = 16
RCOLS = 3 * MW + 64 + 64 + 160
GLA0, RWKV0 = 0, 2 * 512 + 2 * MW + GLA_LORA
RET0 = RWKV0 + RCOLS
GATE0 = RET0 + 2 * 512 + 2 * MW
EPS = 1e-6
GN_EPS = 64e-5
C_DECAY = math.exp(-0.5)
CL = 128
NC = T // CL

CH = 1024
RING = 4

_COLS = [("mix", 16), ("ffn", 16), ("ple", 16), ("fin", 16), ("mu", 27), ("w0", 8), ("a0", 8), ("k_k", 8),
         ("k_a", 8), ("r_k", 8), ("ln_w", 8), ("ln_b", 8), ("bdec", 4), ("gnorm", 2), ("cw0", FT), ("cw1", FT),
         ("cw2", FT), ("cb", FT), ("invf", 1), ("pad", 1)]
COL = {}
for _n, _k in _COLS:
    COL[_n] = sum(COL[m][1] for m in COL), _k
NPRM = sum(k for _, k in _COLS)

S_MISC = 0
S_KR = S_MISC + 8
S_QKVG = S_KR + 32
S_V = S_QKVG + 96
S_GB = S_V + 16
S_RW = S_GB + 96
S_O = S_RW + 48
S_UP = S_O + 32
S_DOWN = S_UP + 172
S_PLE = S_DOWN + 88
N_CHUNK = S_PLE + 36

LEVELS = 7
IN_SQUARE = 4
STAGED = 8


def bass_hybrid_block(nc, stream, xT, prm, const, masks, dmask, pos, lora, pT, outT):
    FIX = 16512
    KB = 1024

    ctx = ExitStack()
    with ctx:
        def at(name, shape, off, dt=F32):
            return nc.alloc_sbuf_tensor_at(name, shape, dt, offset=off)

        def sem(name):
            return ctx.enter_context(nc.semaphore(name))

        o = FIX
        RAW = at("raw", [P, RING, CH], o); o += 16 * KB
        WH = at("w_hi", [P, RING, CH], o, F32R); o += 16 * KB
        WL = at("w_lo", [P, RING, CH], o, F32R); o += 16 * KB
        HH = at("h_hi", [P, DT, T], o, F32R); o += 16 * KB
        HL = at("h_lo", [P, DT, T], o, F32R); o += 16 * KB
        PRM = at("prm", [P, NPRM], o); o += (NPRM * 4 + 31) // 32 * 32
        CST = at("const", [P, 4, P], o); o += 2048
        MSK_AT = o
        MSK = at("masks", [P, 10, P], o, U8); o += 10 * P
        MISC = at("misc", [P, 3, T], o); o += 3072
        ES = at("state_scale", [P, MT + 3], o); o += 64
        o = (o + 31) // 32 * 32
        U = o
        assert U + 119 * KB <= 229344, U

        def un(name, shape, kb, dt=F32):
            return at(name, shape, U + int(kb * KB), dt)

        EPSC, GNEPSC, RKC = ES[:, MT:MT + 1], ES[:, MT + 1:MT + 2], ES[:, MT + 2:MT + 3]
        IDENT, BLK, ONES, PERM = CST[:, 0, :], CST[:, 1, :], CST[:, 2, :], CST[:, 3, :]

        def prmc(name, k):
            return PRM[:, COL[name][0] + k:COL[name][0] + k + 1]

        RWA = un("rw_a", [P, MT, T], 0)
        RWB = un("rw_b", [P, MT, T], 8)
        KRV = un("rw_krv", [P, 3 * MT, T], 16)
        MSKI = un("masks_int", [P, 10, P], 0, I32)
        X0 = un("x_in", [P, DT, T], 88)
        SQ0 = un("sq_in", [P, DT, T], 64)
        RSTD = un("rstd_in", [P, T], 60)
        UBUF = un("shift_u", [P, 4, T + 1], 112)
        DBUF = un("shift_d", [P, 4, T], 107)
        LORA = un("lora", [P, 4, MW], 64)
        LG = un("log_a", [P, HEADS, T], 88)
        LT1 = un("log_t1", [P, HEADS, T], 80)
        LT2 = un("log_t2", [P, HEADS, T], 84)
        BR = un("branch", [P, 2, 24, T], 40)
        MD = un("mid_diff", [P, 4], 117)
        T1 = un("t1", [P, 4, T], 96)
        T2 = un("t2", [P, 4, T], 100)
        T3 = un("t3", [P, 4, T], 104)
        T4 = un("t4", [P, 4, T], 108)
        SG = un("sig", [P, 4, T], 112)
        ROW1 = un("one_row", [P, T], 118)
        COS = un("cos", [P, T], 92)
        SIN = un("sin", [P, T], 93)
        RT = un("rope_t", [P, 2, T], 94)
        PI32 = un("pos", [P, T], 104, I32)
        RA = un("angle", [P, T], 105)
        RB = un("angle_b", [P, T], 106)
        RC = un("angle_c", [P, T], 107)
        DM = un("dmask", [P, HEADS, 384], 96)
        SR = un("scores", [P, 2, 384], 102)
        RS4 = un("att_rs", [P, HEADS, T], 92)
        GI = un("gla_inc", [P, HEADS, T], 92)
        GD = un("gla_dec", [P, HEADS, T], 96)
        GSC = un("gla_sc", [P, 2, NC, CL], 100)
        GKT = un("gla_kt", [P, 2, CL], 102)
        GS = un("gla_s", [P, 2, DV], 103)
        GES = un("gla_es", [P, HEADS], 105)
        GMD = un("gla_md", [P, HEADS], 106)
        OP = [un(f"o_parts{b}", [P, 2, MT, T], 48 + 24 * b, F32R) for b in range(2)]
        AR = un("st_ar", [P, NC, 2, CL], 40)
        BP = un("st_b", [P, 2, T], 42)
        KP = un("st_k", [P, 2, T], 44)
        BS = un("st_b_all", [P, T], 46)
        KS = MISC[:, 0, :]
        VS = un("st_v", [P, T], 47)
        XT = un("x_t", [P, 4, CL], 64)
        LAK = un("l_ak", [P, 4, CL], 66)
        GRB = un("g_rb", [P, 4, CL], 68)
        GRK = un("g_rk", [P, 4, CL], 70)
        TM = un("t_inv", [P, 4, CL], 88)
        ZM = un("t_inv_t", [P, 4, CL], 90)
        P1S = un("p1", [P, 4, CL], 92)
        UP = un("u_pad", [P, NC, 4, 64], 94)
        VP = un("v_pad", [P, NC, 4, 64], 96)
        BKT = un("bk_tok", [P, 2, P], 98)
        SB = un("s_blk", [P, P], 99)
        RH = un("rhs", [P, P], 99.5)
        YS = un("y_s", [P, T], 100)
        PR = un("rk_prod", [P, T], 101)
        SQS = un("sq_s", [P, T], 102)
        MG = un("merged", [P, DT, T], 103)
        GT1 = un("gate_gla", [P, 4, T], 48)
        GB = un("gate_rwkv", [P, DT, T], 48)
        G2 = un("g2", [P, 2, MW], 56)
        GG = un("g_rwkv", [P, MT, T], 16)
        OPR = [un("o_rw_hi", [P, MT, T], 80, F32R), un("o_rw_lo", [P, MT, T], 64, F32R)]
        RT8 = un("rw_rstd", [P, MT, T], 88)
        GTM = un("gate_times", [P, 4, T], 96)
        XR = un("x_res", [P, DT, T], 0)
        SQ = un("sq", [P, DT, T], 103)
        RS = un("rstd", [P, T], 102)
        AH = un("act_hi", [P, FT, T], 16, F32R)
        AL = un("act_lo", [P, FT, T], 59, F32R)
        ZB = un("z", [P, 2, T + 2], 103)
        CV = un("conv", [P, 2, T], 106)
        GE = un("gelu", [P, 2, T], 108)
        AV = un("act", [P, 2, T], 110)
        PG = un("p_proj", [P, DT, T], 16)
        PX = un("p_in", [P, 2, T], 103)
        PXH = at("p_hi", [P, 2, T], MSK_AT, F32R)
        PXL = at("p_lo", [P, 2, T], MSK_AT + 2 * KB, F32R)
        GP = un("ple_gate", [P, 4, T], 38)

        DP = [ctx.enter_context(nc.psum_tensor(f"dense{s}", [P, 4, T], F32)) for s in range(2)]
        BK = [ctx.enter_context(nc.psum_tensor(f"side{s}", [P, 512], F32)) for s in range(4)]

        raw_loaded = [sem(f"raw_loaded{s}") for s in range(RING)]
        hi_ready = sem("hi_ready")
        lo_ready = sem("lo_ready")
        chunk_done = sem("chunk_done")
        set_free = [sem(f"set_free{s}") for s in range(2)]
        x_loaded = [sem(f"x_loaded{g}") for g in range(4)]
        masks_set = sem("masks_set")
        prm_loaded = [sem(f"prm_loaded{k}") for k in range(3)]
        sq_ready = sem("sq_ready")
        ssq_done = sem("ssq_done")
        rs_root = sem("rs_root")
        h_ready = sem("h_ready")
        hh_ready = sem("hh_ready")
        hl_ready = sem("hl_ready")
        dve_step = sem("dve_step")
        act_step = sem("act_step")
        pool_step = sem("pool_step")
        shift_out = sem("shift_out")
        lora_loaded = sem("lora_loaded")
        misc_act = sem("misc_act")
        lora_mm = sem("lora_mm")
        lora_read = sem("lora_read")
        log_sp = sem("log_sp")
        g_sig = sem("g_sig")
        kk_sq = sem("kk_sq")
        kk_ssq = sem("kk_ssq")
        kk_root = sem("kk_root")
        dec_in = sem("dec_in")
        dec_exp = sem("dec_exp")
        rw_prep = sem("rw_prep")
        pos_loaded = sem("pos_loaded")
        dm_loaded = sem("dm_loaded")
        trig_in = sem("trig_in")
        trig_out = sem("trig_out")
        rope_mm = sem("rope_mm")
        rope_read = sem("rope_read")
        rope_done = sem("rope_done")
        sc_mm = sem("sc_mm")
        sc_read = sem("sc_read")
        ov_mm = sem("ov_mm")
        ov_read = sem("ov_read")
        on_sq = sem("on_sq")
        on_ssq = sem("on_ssq")
        on_root = sem("on_root")
        o_final = sem("o_final")
        op_hi = sem("op_hi")
        op_lo = sem("op_lo")
        gdec_in = sem("gdec_in")
        gdec_exp = sem("gdec_exp")
        gqk = sem("gqk")
        gkt_mm = sem("gkt_mm")
        gkt_read = sem("gkt_read")
        gs_mm = sem("gs_mm")
        gs_read = sem("gs_read")
        zeroed = sem("zeroed")
        staged = sem("staged")
        rk_staged = sem("rk_staged")
        bgram = sem("bgram")
        kgram = sem("kgram")
        bgram_read = sem("bgram_read")
        kgram_read = sem("kgram_read")
        t_start = sem("t_start")
        vt_mm = sem("vt_mm")
        vt_read = sem("vt_read")
        p1_mm = sem("p1_mm")
        p1_read = sem("p1_read")
        delta_mm = sem("delta_mm")
        t_grown = sem("t_grown")
        rhs_mm = sem("rhs_mm")
        rhs_read = sem("rhs_read")
        u_mm = sem("u_mm")
        u_read = sem("u_read")
        s_mm = sem("s_mm")
        s_read = sem("s_read")
        y_mm = sem("y_mm")
        y_read = sem("y_read")
        mean_mm = sem("mean_mm")
        centred = sem("centred")
        var_sq = sem("var_sq")
        var_mm = sem("var_mm")
        var_read = sem("var_read")
        bonus_done = sem("bonus_done")
        merged = sem("merged")
        g2_loaded = sem("g2_loaded")
        g_mm = sem("g_mm")
        g_read = sem("g_read")
        gn_root = sem("gn_root")
        orw = sem("orw")
        orw_lo = sem("orw_lo")
        mg_hi = sem("mg_hi")
        mg_lo = sem("mg_lo")
        x_again = sem("x_again")
        conv_done = sem("conv_done")
        gelu_done = sem("gelu_done")
        act_f = sem("act_f")
        act_hi = sem("act_hi")
        act_lo = sem("act_lo")
        p_loaded = sem("p_loaded")
        p_hi = sem("p_hi")
        p_lo = sem("p_lo")
        p_proj = sem("p_proj")
        ple_sig = sem("ple_sig")
        ple_used = sem("ple_used")
        out_ready = sem("out_ready")
        out_stored = sem("out_stored")

        block = ctx.enter_context(nc.Block())

        def lin(value, step, i):
            return value if i is None else value + step * i

        def bcast(ap, n):
            return ap.unsqueeze(2).to_broadcast([ap.shape[0], ap.shape[1], n])

        def mask(k, n):
            return MSK[:, k, :].unsqueeze(1).to_broadcast([P, n, P])

        def half(x, lv, h):
            names = "u " if len(x.shape) == 3 else ""
            v = x.rearrange(f"p {names}(g h m) -> p {names}g h m", h=2, m=2 ** lv)
            return v[:, :, :, h, :] if names else v[:, :, h, :]

        def packed(bank, lv, u=None):
            if u is None:
                return bank[:, 0:2 * P].rearrange("p (u g m) -> p u g m", u=4, m=2 ** lv)
            return bank[:, u * 64:(u + 1) * 64].rearrange("p (g m) -> p g m", m=2 ** lv)

        def half_mask(k, lv, h):
            x = half(MSK[:, k, :], lv, h)
            return x.unsqueeze(1).to_broadcast([P, 4, x.shape[1], x.shape[2]])

        def panel_read(eng, p):
            eng.wait_ge(set_free[p % 2], p // 2 + 2)

        class Steps:

            def __init__(self, eng, s):
                self.eng, self.sem, self.n, self.i, self.per, self.at0 = eng, s, 0, None, 0, 0

            def link(self, ins):
                self.n += 1
                ins.then_inc(self.sem, 1)
                self.eng.wait_ge(self.sem, lin(self.n, self.per, self.i))

            def enter(self, i, per):
                self.i, self.per, self.at0 = i, per, self.n

            def leave(self, turns):
                assert self.n - self.at0 == self.per, (self.sem, self.n - self.at0)
                self.n, self.i = self.at0 + turns * self.per, None

        @block.sync
        def _(sp):
            def load(n, i=None):
                slot = n % RING
                if n >= RING:
                    sp.wait_ge(lo_ready, lin(n - RING + 1, RING, i))
                row = n if i is None else n + RING * i
                sp.dma_start(RAW[:, slot, :], stream[bass.ds(row, 1)].rearrange("a p c -> p (a c)"))\
                    .then_inc(raw_loaded[slot], 16)

            for g in range(4):
                sp.dma_start(X0[:, 4 * g:4 * g + 4, :], xT[:, 4 * g:4 * g + 4, :]).then_inc(x_loaded[g], 16)
            for n in range(RING):
                load(n)
            with sp.Fori(0, N_CHUNK // RING - 1) as i:
                for s in range(RING):
                    load(RING + s, i)

        @block.tensor
        def _(pe):
            mm = nc.tensor.matmul

            def begin(p, step=0, i=None):
                pe.wait_ge(set_free[p % 2], lin(p // 2 + 1, step // 2, i))

            def split(out, whi, wlo, xhi, xlo, start, stop):
                mm(out, whi, xhi, start=start, stop=False, skip_group_check=True)
                mm(out, whi, xlo, start=False, stop=False, skip_group_check=True)
                return mm(out, wlo, xhi, start=False, stop=stop, skip_group_check=True)

            def rows(slot, col, tiles, s, xhi, xlo, first, last):
                for m in range(tiles):
                    w = slice(col + m * P, col + (m + 1) * P)
                    ins = split(DP[s][:, m, :], WH[:, slot, w], WL[:, slot, w], xhi, xlo,
                                first and m % 2 == 0, last and (m % 2 == 1 or m == tiles - 1))
                return ins

            def chunk(n, step, i, kt, s, xs, last_kt, tiles=4, hop=None):
                pe.wait_ge(lo_ready, lin(n + 1, step, i))
                width = 2 if tiles > 2 else 4
                for r in range(width):
                    k = kt + r
                    if k > last_kt:
                        break
                    ins = rows(n % RING, r * CH // width, tiles, s, *xs(k), k == 0, k == last_kt)
                    if r == width - 1 or k == last_kt:
                        ins.then_inc(chunk_done, 1)
                    if hop is not None:
                        hop(r)

            def h(k):
                return HH[:, k, :], HL[:, k, :]

            def chunk_v(n, step, i, kt, s):
                pe.wait_ge(lo_ready, lin(n + 1, step, i))
                slot = n % RING
                for r in range(2):
                    k = kt + r
                    w = slice(r * 512, (r + 1) * 512)
                    for t in range(2):
                        tok = slice(t * P, (t + 1) * P)
                        out = DP[s][:, 2 * t:2 * t + 2, :].rearrange("p a b -> p (a b)")
                        mm(out, HH[:, k, tok], WH[:, slot, w], start=(k == 0), stop=False, skip_group_check=True)
                        mm(out, HL[:, k, tok], WH[:, slot, w], start=False, stop=False, skip_group_check=True)
                        ins = mm(out, HH[:, k, tok], WL[:, slot, w], start=False, stop=(k == DT - 1),
                                 skip_group_check=True)
                ins.then_inc(chunk_done, 1)

            def norm_sum(k, g, sq):
                pe.wait_ge(sq_ready, 4 * k + g + 1)
                for t in range(4 * g, 4 * g + 4):
                    ins = mm(BK[3][:, 0:T], ONES, sq[:, t, :], start=(t == 0), stop=(t == DT - 1))
                if g == 3:
                    ins.then_inc(ssq_done, 1)

            def group(parts_ready, k, c):
                if c % 2 == 0:
                    pe.wait_ge(parts_ready, 4 * k + c // 2 + 1)

            pe.wait_ge(prm_loaded[1], 16)
            for g in range(4):
                norm_sum(0, g, SQ0)
            p = 0
            begin(p)
            for c in range(8):
                group(hl_ready, 0, c)
                chunk(S_MISC + c, 0, None, 2 * c, 0, h, DT - 1, tiles=3)
            p = 1
            with pe.Fori(0, 2) as i:
                for q in range(2):
                    begin(p + q, 2, i)
                    for c in range(8):
                        chunk(S_KR + 8 * q + c, 16, i, 2 * c, (p + q) % 2, h, DT - 1)
            p += 4

            def lora_products(c):
                if c == 0:
                    pe.wait_ge(lora_loaded, 16)
                    pe.wait_ge(misc_act, 3)
                else:
                    pe.wait_ge(lora_read, 4 * c)
                for m in range(4 * c, 4 * c + 4):
                    if m < 16:
                        w, x = LORA[:, m % 2, (m // 2) * P:(m // 2 + 1) * P], MISC[:, 0, :]
                    else:
                        w, x = LORA[:, 2, (m - 16) * P:(m - 15) * P], MISC[:, 2, :]
                    mm(BK[m % 4][:, 0:T], w, x, start=True, stop=True).then_inc(lora_mm, 1)

            def key_norms(b):
                pe.wait_ge(kk_sq, b + 1)
                for j in range(4):
                    ins = mm(BK[j // 2][:, (j % 2) * T:(j % 2 + 1) * T], BLK, T2[:, j, :], start=True, stop=True)
                ins.then_inc(kk_ssq, 1)

            def rope(m):
                if m >= 2:
                    pe.wait_ge(rope_read, m - 1)
                mm(BK[m % 2][:, :], PERM, BR[:, 0, 2 * m:2 * m + 2, :], start=True, stop=True).then_inc(rope_mm, 1)

            vt = [BR[:, b, 8:16, :].rearrange("p (t a) c -> p t (a c)", t=2) for b in range(2)]

            def ret_scores(hd):
                if hd >= 2:
                    pe.wait_ge(sc_read, hd - 1)
                q, k = BR[:, 0, hd, :], BR[:, 0, 4 + hd, :]
                mm(BK[hd % 2][:, 0:T], k[:, 0:P], q, start=True, stop=True, skip_group_check=True)
                mm(BK[hd % 2][:, T:T + P], k[:, P:T], q[:, P:T], start=False, stop=True,
                   skip_group_check=True).then_inc(sc_mm, 1)

            def ret_out(hd):
                pe.wait_ge(sc_read, hd + 1)
                if hd >= 2:
                    pe.wait_ge(ov_read, hd - 1)
                for b in range(2):
                    v = slice(hd * DV + b * P, hd * DV + (b + 1) * P)
                    o = BK[2 + hd % 2]
                    mm(o[:, b * T:(b + 1) * T], vt[0][:, 0, v], SR[:, hd % 2, 0:T], start=(b == 0), stop=False,
                       skip_group_check=True)
                    ins = mm(o[:, b * T + P:(b + 1) * T], vt[0][:, 1, v], SR[:, hd % 2, T:T + P], start=False,
                             stop=(b == 1), skip_group_check=True)
                ins.then_inc(ov_mm, 1)

            def head_norm_sum(b):
                pe.wait_ge(on_sq, b + 1)
                for hd in range(HEADS):
                    for e in range(2):
                        ins = mm(BK[hd // 2][:, (hd % 2) * T:(hd % 2 + 1) * T], ONES, BR[:, b, 8 + hd + 4 * e, :],
                                 start=(hd % 2 == 0 and e == 0), stop=(e == 1), skip_group_check=True)
                ins.then_inc(on_ssq, 1)

            def gla_scores(hd):
                if hd >= 1:
                    pe.wait_ge(sc_read, 4 + hd)
                    pe.wait_ge(gkt_read, hd)
                q, k = BR[:, 1, hd, :], BR[:, 1, 4 + hd, :]
                for c in range(NC):
                    t = slice(c * CL, (c + 1) * CL)
                    ins = mm(BK[0][:, t], k[:, t], q[:, t], start=(c == 0), stop=(c == 1), skip_group_check=True)
                ins.then_inc(sc_mm, 1)
                nc.tensor.transpose(BK[1][:, 0:P], k[:, 0:P], IDENT).then_inc(gkt_mm, 1)

            def gla_state(hd):
                pe.wait_ge(gkt_read, hd + 1)
                mm(BK[2][:, 0:DV], GKT[:, hd % 2, :], vt[1][:, 0, hd * DV:(hd + 1) * DV], start=True, stop=True)\
                    .then_inc(gs_mm, 1)

            def gla_out(hd):
                pe.wait_ge(sc_read, 4 + hd + 1)
                pe.wait_ge(gs_read, hd + 1)
                pe.wait_ge(ov_read, 4 + hd)
                for b in range(2):
                    v = slice(hd * DV + b * P, hd * DV + (b + 1) * P)
                    o = BK[3][:, b * T:(b + 1) * T]
                    mm(o[:, 0:P], vt[1][:, 0, v], GSC[:, hd % 2, 0, :], start=(b == 0), stop=False,
                       skip_group_check=True)
                    mm(o[:, P:T], vt[1][:, 1, v], GSC[:, hd % 2, 1, :], start=False, stop=False,
                       skip_group_check=True)
                    ins = mm(o[:, P:T], GS[:, hd % 2, b * P:(b + 1) * P], BR[:, 1, hd, P:T], start=False,
                             stop=(b == 1), skip_group_check=True)
                ins.then_inc(ov_mm, 1)

            def side(b, q, c):
                if b == 0:
                    if q == 0 and c < 5:
                        lora_products(c)
                    elif (q, c) == (0, 6):
                        pe.wait_ge(lora_read, 20)
                        key_norms(0)
                    elif q == 2 and 3 <= c < 7:
                        if c == 3:
                            panel_read(pe, p - 2)
                            panel_read(pe, p - 1)
                            pe.wait_ge(kk_root, 2)
                        rope(c - 3)
                    elif (q, c) in ((3, 2), (3, 4)):
                        pe.wait_ge(rope_done, 4)
                        ret_scores((c - 2) // 2)
                    elif q == 4 and c % 2:
                        if c == 1:
                            panel_read(pe, p - 2)
                            panel_read(pe, p - 1)
                        ret_out(c // 2)
                        if c < 4:
                            ret_scores(2 + c // 2)
                    elif (q, c) == (5, 3):
                        head_norm_sum(0)
                else:
                    if (q, c) == (0, 3):
                        pe.wait_ge(on_root, 2)
                        key_norms(1)
                    elif q == 4 and c % 2 == 0:
                        if c == 0:
                            pe.wait_ge(gqk, 1)
                            pe.wait_ge(kk_root, 4)
                            pe.wait_ge(ov_read, 4)
                            panel_read(pe, p - 2)
                            panel_read(pe, p - 1)
                        else:
                            gla_out(c // 2 - 1)
                        gla_scores(c // 2)
                    elif q == 4:
                        gla_state(c // 2)
                    elif (q, c) == (5, 0):
                        gla_out(HEADS - 1)
                    elif (q, c) == (5, 3):
                        head_norm_sum(1)

            for b in range(2):
                for q in range(6 + 2 * b):
                    begin(p)
                    for c in range(8):
                        n = S_QKVG + 48 * b + 8 * q + c
                        if q in (2, 3):
                            chunk_v(n, 0, None, 2 * c, p % 2)
                        else:
                            chunk(n, 0, None, 2 * c, p % 2, h, DT - 1)
                        side(b, q, c)
                    p += 1

            for b in range(2):
                pe.wait_ge(op_lo, b + 1)
                if b == 0:
                    pe.wait_ge(op_lo, 2)
                    pe.wait_ge(zeroed, 8)
                base = S_GB + 48 * b
                with pe.Fori(0, 4) as i:
                    def rank(value, per=1):
                        return lin(per * 4 * b + value, per, i)

                    def grams(which):
                        x, done, banks = ((BP, bgram, (0, 1)), (KP, kgram, (2, 3)))[which]
                        pe.wait_ge(staged, rank(STAGED, STAGED))
                        pe.wait_ge((bonus_done, var_read)[which], rank(1))
                        for c in range(NC):
                            for e in range(2):
                                ins = mm(BK[banks[c]][:, e * 2 * CL:(e + 1) * 2 * CL],
                                         x[:, e, c * CL:(c + 1) * CL], AR[:, c, :, :], start=(e == 0),
                                         stop=(e == 1), skip_group_check=True)
                        ins.then_inc(done, 1)

                    def tokens():
                        pe.wait_ge(kgram_read, rank(1))
                        for c in range(NC):
                            nc.tensor.transpose(BK[2][:, c * P:(c + 1) * P], VS[:, c * CL:(c + 1) * CL], IDENT)
                        nc.tensor.transpose(BK[2][:, 2 * P:3 * P], BS[:, 0:CL], IDENT)
                        nc.tensor.transpose(BK[2][:, 3 * P:4 * P], KS[:, 0:CL], IDENT).then_inc(vt_mm, 1)

                    def grow_a(lv):
                        pe.wait_ge(t_start, rank(1))
                        if lv > 1:
                            pe.wait_ge(t_grown, rank(lv - 1, LEVELS - 1))
                        for u in range(4):
                            ins = mm(packed(BK[1], lv, u), XT[:, u, :], half(TM[:, u, :], lv, 0), start=(u == 0),
                                     stop=(u == 3), skip_group_check=True)
                        ins.then_inc(p1_mm, 1)

                    def grow_b(lv):
                        pe.wait_ge(p1_read, rank(lv, LEVELS - 1))
                        pe.wait_ge(vt_read, rank(1))
                        if lv == IN_SQUARE + 1:
                            for u in range(4):
                                mm(packed(BK[2], lv, u), ZM[:, u, :], half(P1S[:, u, :], lv, 0), start=(u == 0),
                                   stop=(u == 3), skip_group_check=True)
                        for u in range(4):
                            ins = mm(packed(BK[3], lv, u), P1S[:, u, :], half(ZM[:, u, :], lv, 1), start=(u == 0),
                                     stop=(u == 3), skip_group_check=True)
                        ins.then_inc(delta_mm, 1)

                    def vh(c, e):
                        return VP[:, c, 3 * e, :]

                    def rhs(c):
                        if c == 0:
                            pe.wait_ge(vt_read, rank(1))
                            pe.wait_ge(kgram_read, rank(1))
                        else:
                            pe.wait_ge(s_read, rank(1))
                            mm(BK[0][:, 0:P], AR[:, 1, 0, :], SB[:, :], start=True, stop=False,
                               skip_group_check=True)
                        for e in range(2):
                            ins = mm(BK[0][:, e * 64:(e + 1) * 64], LAK[:, 2 * c + e, :], vh(c, e),
                                     start=(c == 0 and e == 0), stop=(e == 1), skip_group_check=True)
                        ins.then_inc(rhs_mm, 1)

                    def solve(c):
                        pe.wait_ge(rhs_read, rank(c + 1, 2))
                        pe.wait_ge(t_grown, rank(LEVELS - 1, LEVELS - 1))
                        for e in range(2):
                            ins = mm(BK[1][:, e * 64:(e + 1) * 64], ZM[:, 2 * c + e, :], RH[:, e * 64:(e + 1) * 64],
                                     start=(e == 0), stop=(e == 1), skip_group_check=True)
                        ins.then_inc(u_mm, 1)

                    def state():
                        pe.wait_ge(u_read, rank(1, 2))
                        mm(BK[2][:, 0:P], BKT[:, 0, :], UP[:, 0, 0:4:3, :], start=True, stop=False)
                        mm(BK[2][:, 0:P], BKT[:, 1, :], VP[:, 0, 0:4:3, :], start=False, stop=True).then_inc(s_mm, 1)

                    def outputs(c):
                        pe.wait_ge(u_read, rank(c + 1, 2))
                        t = slice(c * CL, (c + 1) * CL)
                        if c == 1:
                            mm(BK[3][:, t], SB[:, :], AR[:, 1, 1, :], start=False, stop=False,
                               skip_group_check=True)
                        for e in range(2):
                            mm(BK[3][:, t], UP[:, c, 2 * e:2 * e + 2, :], GRB[:, 2 * c + e, :], start=(c == 0 and e == 0),
                               stop=False, skip_group_check=True)
                            ins = mm(BK[3][:, t], VP[:, c, 2 * e:2 * e + 2, :], GRK[:, 2 * c + e, :], start=False,
                                     stop=(e == 1), skip_group_check=True)
                        if c == 1:
                            ins.then_inc(y_mm, 1)

                    def means():
                        pe.wait_ge(y_read, rank(1))
                        pe.wait_ge(rk_staged, rank(3, 3))
                        mm(BK[0][:, 0:T], BLK, YS[:, :], start=True, stop=True)
                        mm(BK[1][:, 0:T], BLK, PR[:, :], start=True, stop=True).then_inc(mean_mm, 1)

                    def variances():
                        pe.wait_ge(var_sq, rank(1))
                        mm(BK[2][:, 0:T], BLK, SQS[:, :], start=True, stop=True).then_inc(var_mm, 1)

                    def hop(s):
                        if s == 0:
                            grams(0)
                        elif s == 1:
                            grams(1)
                        elif s == 3:
                            tokens()
                        elif 4 <= s < 16:
                            (grow_a, grow_b)[s % 2]((s - 4) // 2 + 1)
                        elif s == 16:
                            rhs(0)
                        elif s == 17:
                            solve(0)
                        elif s == 18:
                            state()
                            outputs(0)
                        elif s == 19:
                            rhs(1)
                        elif s == 20:
                            solve(1)
                        elif s == 21:
                            outputs(1)
                        elif s == 22:
                            means()
                        elif s == 23:
                            variances()

                    begin(p, 2, i)
                    for c in range(8):
                        chunk(base + c, 12, i, 2 * c, p % 2, h, DT - 1, hop=lambda r: hop(2 * c + r))
                    begin(p + 1, 2, i)
                    for c in range(4):
                        chunk(base + 8 + c, 12, i, 2 * c, (p + 1) % 2,
                              lambda k: (OP[b][:, 0, k // 2 + 4 * (k % 2), :], OP[b][:, 1, k // 2 + 4 * (k % 2), :]), MT - 1,
                              hop=lambda r: hop(16 + 2 * c + r))
                p += 8

            pe.wait_ge(g2_loaded, 16)
            pe.wait_ge(var_read, 9)
            pe.wait_ge(bonus_done, 9)
            for q in range(4):
                begin(p)
                for c in range(8):
                    chunk(S_RW + 8 * q + c, 0, None, 2 * c, p % 2, h, DT - 1)
                    if q == 0:
                        if c >= 4:
                            pe.wait_ge(g_read, c - 3)
                        w = slice(c * P, (c + 1) * P)
                        mm(BK[c % 4][:, 0:T], G2[:, 0, w], MISC[:, 1, :], start=True, stop=False)
                        mm(BK[c % 4][:, 0:T], G2[:, 1, w], MISC[:, 2, :], start=False, stop=True).then_inc(g_mm, 1)
                p += 1
            pe.wait_ge(orw_lo, 1)
            with pe.Fori(0, 2) as i:
                for q in range(2):
                    begin(p + q, 2, i)
                    for c in range(4):
                        chunk(S_RW + 32 + 4 * q + c, 8, i, 2 * c, (p + q) % 2,
                              lambda k: (OPR[0][:, k, :], OPR[1][:, k, :]), MT - 1)
            p += 4
            with pe.Fori(0, 2) as i:
                for q in range(2):
                    begin(p + q, 2, i)
                    for c in range(8):
                        group(mg_lo, 0, c)
                        chunk(S_O + 8 * q + c, 16, i, 2 * c, (p + q) % 2, h, DT - 1)
            p += 4
            begin(p)
            for c in range(8):
                group(hl_ready, 1, c)
                chunk(S_UP + c, 0, None, 2 * c, p % 2, h, DT - 1)
                if 1 <= c < 4 or c == 7:
                    norm_sum(1, min(c - 1, 3), SQ)
            p += 1
            with pe.Fori(0, 10) as i:
                for q in range(2):
                    begin(p + q, 2, i)
                    for c in range(8):
                        chunk(S_UP + 8 + 8 * q + c, 16, i, 2 * c, (p + q) % 2, h, DT - 1)
            p += 20
            begin(p)
            for c in range(4):
                chunk(S_UP + 168 + c, 0, None, 4 * c, p % 2, h, DT - 1, tiles=2)
            p += 1
            with pe.Fori(0, 2) as i:
                for q in range(2):
                    begin(p + q, 2, i)
                    for c in range(22):
                        pe.wait_ge(act_lo, c + 1)
                        chunk(S_DOWN + 22 * q + c, 44, i, 2 * c, (p + q) % 2,
                              lambda k: (AH[:, k, :], AL[:, k, :]), FT - 1)
            p += 4
            pe.wait_ge(p_lo, 1)
            for q in range(4):
                begin(p)
                chunk(S_PLE + q, 0, None, 0, p % 2, lambda k: (PXH[:, k, :], PXL[:, k, :]), 1)
                if q < 3:
                    norm_sum(2, q, SQ)
                p += 1
            for q in range(4):
                begin(p)
                for c in range(8):
                    if q == 0:
                        group(hl_ready, 2, c)
                    chunk(S_PLE + 4 + 8 * q + c, 0, None, 2 * c, p % 2, h, DT - 1)
                    if (q, c) == (0, 7):
                        norm_sum(2, 3, SQ)
                    elif q and c == 6:
                        pe.wait_ge(rs_root, 3)
                        norm_sum(3, q - 1, SQ)
                p += 1
            norm_sum(3, 3, SQ)

        @block.scalar
        def _(act):
            a = nc.scalar.activation
            steps = Steps(act, act_step)

            def hi(n, step=0, i=None):
                slot = n % RING
                act.wait_ge(raw_loaded[slot], lin(16 * (n // RING + 1), 16 * step // RING, i))
                if n >= RING:
                    act.wait_ge(chunk_done, lin(n - RING + 1, step, i))
                a(WH[:, slot, :], RAW[:, slot, :], ACT.Copy).then_inc(hi_ready, 1)

            def tick(n, step=0, i=None):
                if n + 3 < N_CHUNK:
                    hi(n + 3, step, i)

            def panel_end(n, step=0, i=None):
                act.wait_ge(chunk_done, lin(n + 1, step, i))

            def root(k, rs):
                act.wait_ge(ssq_done, k + 1)
                a(rs[:, :], BK[3][:, 0:T], ACT.Sqrt, scale=1.0 / D, bias=EPSC).then_inc(rs_root, 1)

            def h_hi(k, g, sq):
                act.wait_ge(h_ready, 4 * k + g + 1)
                a(HH[:, 4 * g:4 * g + 4, :], sq[:, 4 * g:4 * g + 4, :], ACT.Copy).then_inc(hh_ready, 1)

            def squares(x, sq, g):
                a(sq[:, 4 * g:4 * g + 4, :], x[:, 4 * g:4 * g + 4, :], ACT.Square).then_inc(sq_ready, 1)

            for g in range(4):
                act.wait_ge(x_loaded[g], 16)
                squares(X0, SQ0, g)
            for n in range(3):
                hi(n)
            act.wait_ge(set_free[1], 1)
            root(0, RSTD)
            for g in range(4):
                h_hi(0, g, SQ0)
            p = 0
            for c in range(8):
                tick(S_MISC + c)
            panel_end(S_MISC + 7)
            act.wait_ge(set_free[0], 1)
            a(UBUF[:, 0:3, 1:T + 1], DP[0][:, 0:3, :], ACT.Copy).then_inc(set_free[0], 1)
            act.wait_ge(shift_out, 1)
            a(MISC[0:64, 0, :], MISC[0:64, 0, :], ACT.Tanh).then_inc(misc_act, 1)
            a(MISC[:, 1, :], MISC[:, 1, :], ACT.Sigmoid).then_inc(misc_act, 1)
            a(MISC[0:32, 2, :], MISC[0:32, 2, :], ACT.Sigmoid).then_inc(misc_act, 1)
            act.wait_ge(trig_in, 2)
            a(SIN[:, :], SIN[:, :], ACT.Sin).then_inc(trig_out, 1)
            a(COS[:, :], COS[:, :], ACT.Sin).then_inc(trig_out, 1)
            p = 1
            with act.Fori(0, 2) as i:
                for q in range(2):
                    for c in range(8):
                        tick(S_KR + 8 * q + c, 16, i)
                    panel_end(S_KR + 8 * q + 7, 16, i)
                    act.wait_ge(shift_out, lin(p + q, 2, i))
                    s = (p + q) % 2
                    a(UBUF[:, :, 1:T + 1], DP[s][:, :, :], ACT.Copy).then_inc(set_free[s], 1)
            p += 4

            def lora_out(c):
                if c == 0:
                    act.wait_ge(masks_set, 1)
                for m in range(4 * c, 4 * c + 4):
                    act.wait_ge(lora_mm, m + 1)
                    t = m // 2
                    if m < 16:
                        a((RWA, RWB)[m % 2][:, t, :], BK[m % 4][:, 0:T], ACT.Sigmoid,
                          bias=prmc(("w0", "a0")[m % 2], t)).then_inc(lora_read, 1)
                    else:
                        a(LG[:, m - 16, :], BK[m % 4][:, 0:T], ACT.Identity, bias=prmc("bdec", m - 16))\
                            .then_inc(lora_read, 1)

            def log_sigmoid():
                act.wait_ge(lora_read, 20)
                steps.link(a(LT1[:, :, :], LG[:, :, :], ACT.Abs))
                steps.link(a(LT1[:, :, :], LT1[:, :, :], ACT.Exp, scale=-1.0))
                a(LT1[:, :, :], LT1[:, :, :], ACT.Ln, bias=1.0).then_inc(log_sp, 1)

            def key_roots(b):
                act.wait_ge(kk_ssq, b + 1)
                for j in range(2):
                    a(T2[:, 2 * j:2 * j + 2, :].rearrange("p a b -> p (a b)"), BK[j][:, :], ACT.Sqrt)\
                        .then_inc(kk_root, 1)

            def decays(b):
                act.wait_ge(dec_in, b + 1)
                t = slice(4 * b, 4 * b + 4)
                a(T4[:, :, :], T4[:, :, :], ACT.Exp, scale=-C_DECAY).then_inc(dec_exp, 1)
                a(RWA[:, t, :], T2[:, :, :], ACT.Exp, scale=-C_DECAY).then_inc(dec_exp, 1)
                a(T2[:, :, :], T2[:, :, :], ACT.Exp, scale=C_DECAY).then_inc(dec_exp, 1)
                a(ES[:, t], MD[:, :], ACT.Exp, scale=-C_DECAY).then_inc(dec_exp, 1)

            def o_read(b, hd):
                act.wait_ge(ov_mm, 4 * b + hd + 1)
                bank = BK[3] if b else BK[2 + hd % 2]
                a(BR[:, b, hd:8:4, :], bank[:, :].rearrange("p (e t) -> p e t", e=2), ACT.Copy).then_inc(ov_read, 1)

            def head_squares(b):
                act.wait_ge(ov_read, 4 * b + 4)
                a(BR[:, b, 8:16, :], BR[:, b, 0:8, :], ACT.Square).then_inc(on_sq, 1)

            def head_roots(b):
                act.wait_ge(on_ssq, b + 1)
                for j in range(2):
                    a(RS4[:, 2 * j:2 * j + 2, :].rearrange("p a b -> p (a b)"), BK[j][:, :], ACT.Sqrt,
                      scale=1.0 / DV, bias=EPSC).then_inc(on_root, 1)

            def output_hi(b):
                act.wait_ge(o_final, b + 1)
                a(OP[b][:, 0, :, :], BR[:, b, 0:8, :], ACT.Copy).then_inc(op_hi, 1)

            def side(b, q, c):
                if b == 0:
                    if q == 0 and c < 5:
                        lora_out(c)
                    elif (q, c) == (0, 7):
                        key_roots(0)
                    elif (q, c) == (1, 5):
                        decays(0)
                    elif (q, c) == (1, 6):
                        log_sigmoid()
                    elif q == 4 and c in (2, 4, 6):
                        o_read(0, c // 2 - 1)
                    elif (q, c) == (5, 0):
                        o_read(0, 3)
                    elif (q, c) == (5, 1):
                        head_squares(0)
                    elif (q, c) == (5, 4):
                        head_roots(0)
                else:
                    if (q, c) == (0, 4):
                        key_roots(1)
                    elif (q, c) == (1, 2):
                        decays(1)
                    elif (q, c) == (1, 5):
                        output_hi(0)
                    elif (q, c) == (2, 4):
                        act.wait_ge(gdec_in, 1)
                        a(GI[:, :, :], GD[:, :, :], ACT.Exp, scale=1.0 / 16).then_inc(gdec_exp, 1)
                        a(GD[:, :, :], GD[:, :, :], ACT.Exp, scale=-1.0 / 16).then_inc(gdec_exp, 1)
                        a(GES[:, :], GMD[:, :], ACT.Exp, scale=1.0 / 16).then_inc(gdec_exp, 1)
                    elif q == 4 and c % 2 == 0:
                        hd = c // 2
                        act.wait_ge(gkt_mm, hd + 1)
                        a(GKT[:, hd % 2, :], BK[1][:, 0:P], ACT.Copy).then_inc(gkt_read, 1)
                        if hd:
                            o_read(1, hd - 1)
                    elif q == 4:
                        hd = c // 2
                        act.wait_ge(gs_mm, hd + 1)
                        act.wait_ge(gdec_exp, 3)
                        a(GS[:, hd % 2, :], BK[2][:, 0:DV], ACT.Copy, scale=GES[:, hd:hd + 1]).then_inc(gs_read, 1)
                    elif (q, c) == (5, 0):
                        o_read(1, 3)
                        head_squares(1)
                    elif (q, c) == (5, 3):
                        head_roots(1)
                    elif (q, c) == (6, 3):
                        output_hi(1)

            for b in range(2):
                for q in range(6 + 2 * b):
                    s = p % 2
                    for c in range(8):
                        tick(S_QKVG + 48 * b + 8 * q + c)
                        side(b, q, c)
                    panel_end(S_QKVG + 48 * b + 8 * q + 7)
                    if q < 2:
                        a(BR[:, b, 4 * q:4 * q + 4, :], DP[s][:, :, :], ACT.Copy).then_inc(set_free[s], 1)
                    elif q < 4:
                        for t in range(2):
                            lo_t = 8 + 4 * t + 2 * (q - 2)
                            ins = a(BR[:, b, lo_t:lo_t + 2, :], DP[s][:, 2 * t:2 * t + 2, :], ACT.Copy)
                        ins.then_inc(set_free[s], 1)
                    elif q < 6:
                        if q == 4:
                            act.wait_ge(shift_out, 5)
                        else:
                            panel_read(act, p - 1)
                        a(SG[:, :, :], DP[s][:, :, :], ACT.Sigmoid).then_inc(g_sig, 1)
                    else:
                        act.wait_ge(shift_out, q)
                        a(UBUF[:, :, 1:T + 1], DP[s][:, :, :], ACT.Copy).then_inc(set_free[s], 1)
                    p += 1
            act.wait_ge(shift_out, 8)
            for b in range(2):
                base = S_GB + 48 * b
                with act.Fori(0, 4) as i:
                    def rank(value, per=1):
                        return lin(per * 4 * b + value, per, i)

                    for k in range(12):
                        tick(base + k, 12, i)
                        if k == 1:
                            act.wait_ge(vt_mm, rank(2))
                            a(VP[:, :, 0:4:3, :], BK[2][:, 0:2 * P].rearrange("p (c e q) -> p c e q", c=2, e=2),
                              ACT.Copy)
                            a(BKT[:, :, :].rearrange("p a b -> p (a b)"), BK[2][:, 2 * P:], ACT.Copy)\
                                .then_inc(vt_read, 1)
                        elif 2 <= k < 8:
                            act.wait_ge(p1_mm, rank(k - 1, LEVELS - 1))
                            a(half(P1S[:, :, :], k - 1, 0), packed(BK[1], k - 1), ACT.Copy).then_inc(p1_read, 1)
                        elif k in (8, 9):
                            act.wait_ge(rhs_mm, rank(k - 7, 2))
                            a(RH[:, :], BK[0][:, 0:P], ACT.Copy).then_inc(rhs_read, 1)
                        if k in (8, 10):
                            c = (k - 8) // 2
                            act.wait_ge(u_mm, rank(c + 1, 2))
                            a(UP[:, c, 0:4:3, :], BK[1][:, 0:P].rearrange("p (e q) -> p e q", e=2), ACT.Copy)\
                                .then_inc(u_read, 1)
                        if k == 10:
                            act.wait_ge(y_mm, rank(2))
                            a(YS[:, :], BK[3][:, 0:T], ACT.Copy).then_inc(y_read, 1)
                        if k == 11:
                            act.wait_ge(centred, rank(1))
                            a(SQS[:, :], KRV[:, bass.ds(MT + 4 * b + i, 1), :].rearrange("p a b -> p (a b)"),
                              ACT.Square).then_inc(var_sq, 1)
                            act.wait_ge(var_mm, rank(1))
                            a(RWA[:, bass.ds(4 * b + i, 1), :].rearrange("p a b -> p (a b)"), BK[2][:, 0:T],
                              ACT.Copy).then_inc(var_read, 1)
                        if k == 7:
                            panel_end(base + 7, 12, i)
                            if b == 0:
                                a(MG[:, bass.ds(4 * i, 4), :], DP[p % 2][:, :, :], ACT.Sigmoid)\
                                    .then_inc(set_free[p % 2], 1)
                            else:
                                act.wait_ge(merged, lin(1, 1, i))
                                a(GT1[:, :, :], DP[p % 2][:, :, :], ACT.Sigmoid).then_inc(set_free[p % 2], 1)
                p += 8
            act.wait_ge(var_read, 9)
            a(RT8[:, :, :], RWA[:, :, :], ACT.Sqrt, scale=1.0 / 64, bias=GNEPSC).then_inc(gn_root, 1)
            act.wait_ge(merged, 5)
            for q in range(4):
                for c in range(8):
                    tick(S_RW + 8 * q + c)
                    if q == 0:
                        act.wait_ge(g_mm, c + 1)
                        a(GG[:, c, :], BK[c % 4][:, 0:T], ACT.Copy).then_inc(g_read, 1)
                    elif (q, c) == (1, 2):
                        act.wait_ge(orw, 1)
                        a(OPR[0][:, :, :], KRV[:, MT:2 * MT, :], ACT.Copy).then_inc(orw, 1)
                panel_end(S_RW + 8 * q + 7)
                a(GB[:, 4 * q:4 * q + 4, :], DP[p % 2][:, :, :], ACT.Sigmoid).then_inc(set_free[p % 2], 1)
                p += 1
            for q in range(4):
                for c in range(4):
                    tick(S_RW + 32 + 4 * q + c)
                act.wait_ge(merged, 6 + q)
                a(HH[:, 4 * q:4 * q + 4, :], MG[:, 4 * q:4 * q + 4, :], ACT.Copy).then_inc(mg_hi, 1)
                p += 1
            for q in range(4):
                for c in range(8):
                    tick(S_O + 8 * q + c)
                    if q == 3 and c in (2, 4, 6):
                        act.wait_ge(chunk_done, S_O + 24 + c)
                        h_hi(1, c // 2 - 1, SQ)
                    elif q == 3 and c in (3, 5, 7):
                        act.wait_ge(hl_ready, 4 + c // 2)
                        squares(XR, SQ, c // 2 - 1)
                p += 1

            def gelu(w, i):
                act.wait_ge(conv_done, lin(w + 1, 2, i))
                tiles = 1 if w == 21 else 2
                a(GE[:, 0:tiles, :], CV[:, 0:tiles, :], ACT.Gelu_apprx_tanh).then_inc(gelu_done, 1)

            def act_high(w, i, pc):
                tiles = 1 if w == 21 else 2
                act.wait_ge(set_free[pc % 2], lin(pc // 2 + 2, 1, i))
                tile = 2 * w if i is None else 2 * w + 4 * i
                a(AH[:, bass.ds(tile, tiles), :], AV[:, 0:tiles, :], ACT.Copy).then_inc(act_hi, 1)

            for c in range(8):
                tick(S_UP + c)
                if c == 0:
                    h_hi(1, 3, SQ)
                elif c == 2:
                    act.wait_ge(hl_ready, 8)
                    squares(XR, SQ, 3)
            root(1, RS)
            with act.Fori(0, 10) as i:
                for q in range(2):
                    for c in range(8):
                        tick(S_UP + 8 + 8 * q + c, 16, i)
                        if c == 1:
                            gelu(q, i)
                        elif c == 3:
                            act_high(q, i, p + q)
            p += 20
            for c in range(4):
                tick(S_UP + 168 + c)
                if c == 1:
                    gelu(20, None)
                elif c == 3:
                    act_high(20, None, p)
            p += 1
            for q in range(4):
                for c in range(22):
                    tick(S_DOWN + 22 * q + c)
                    if (q, c) == (0, 2):
                        gelu(21, None)
                    elif (q, c) == (0, 4):
                        act_high(21, None, p)
                    elif (q, c) == (0, 14):
                        act.wait_ge(p_loaded, 16)
                        a(PXH[:, :, :], PX[:, :, :], ACT.Copy).then_inc(p_hi, 1)
                    elif q and c == 2:
                        h_hi(2, q - 1, SQ)
                    elif q and c == 4:
                        act.wait_ge(hl_ready, 8 + q)
                        squares(XR, SQ, q - 1)
            p += 5
            for q in range(4):
                tick(S_PLE + q)
                if q == 0:
                    h_hi(2, 3, SQ)
                elif q == 2:
                    act.wait_ge(hl_ready, 12)
                    squares(XR, SQ, 3)
                panel_end(S_PLE + q)
                a(PG[:, 4 * q:4 * q + 4, :], DP[p % 2][:, :, :], ACT.Copy).then_inc(set_free[p % 2], 1)
                p += 1

            def ple_sigmoid(pc):
                panel_read(act, pc)
                a(GP[:, :, :], GP[:, :, :], ACT.Sigmoid).then_inc(ple_sig, 1)

            for q in range(4):
                for c in range(8):
                    tick(S_PLE + 4 + 8 * q + c)
                    if q and c == 1:
                        ple_sigmoid(p - 1)
                    elif q and c == 4:
                        act.wait_ge(ple_used, q)
                        squares(XR, SQ, q - 1)
                if q == 0:
                    root(2, RS)
                p += 1
            ple_sigmoid(p - 1)
            act.wait_ge(ple_used, 4)
            squares(XR, SQ, 3)
            root(3, RS)

        @block.vector
        def _(dve):
            v = nc.vector
            steps = Steps(dve, dve_step)
            link = steps.link

            def lo(n, step=0, i=None):
                slot = n % RING
                dve.wait_ge(hi_ready, lin(n + 1, step, i))
                v.tensor_tensor(WL[:, slot, :], RAW[:, slot, :], WH[:, slot, :].bitcast(F32), ALU.subtract)\
                    .then_inc(lo_ready, 1)

            def tick(n, step=0, i=None):
                if n + 3 < N_CHUNK:
                    lo(n + 3, step, i)

            def h_lo(g, k, sq):
                dve.wait_ge(hh_ready, 4 * k + g + 1)
                t = slice(4 * g, 4 * g + 4)
                v.tensor_tensor(HL[:, t, :], sq[:, t, :], HH[:, t, :].bitcast(F32), ALU.subtract)\
                    .then_inc(hl_ready, 1)

            def reciprocal_root(k, rs):
                dve.wait_ge(rs_root, k + 1)
                link(v.reciprocal(rs[:, :], rs[:, :]))

            def normalise(k, x, sq, rs, gain):
                reciprocal_root(k, rs)
                for g in range(4):
                    for t in range(4 * g, 4 * g + 4):
                        ins = v.scalar_tensor_tensor(out=sq[:, t, :], in0=x[:, t, :], scalar=prmc(gain, t),
                                                     in1=rs[:, :], op0=ALU.mult, op1=ALU.mult)
                    ins.then_inc(h_ready, 1)
                    if k == 0 and g:
                        h_lo(g - 1, k, sq)
                if k == 0:
                    h_lo(3, k, sq)

            def residual(p, q, gain):
                t = slice(4 * q, 4 * q + 4)
                v.tensor_tensor(XR[:, t, :], DP[p % 2][:, :, :], XR[:, t, :], ALU.add).then_inc(set_free[p % 2], 1)
                panel_read(dve, p)
                at = COL[gain][0] + 4 * q
                v.tensor_tensor(SQ[:, t, :], XR[:, t, :], bcast(PRM[:, at:at + 4], T), ALU.mult).then_inc(h_ready, 1)

            v.memset(EPSC, EPS)
            v.memset(GNEPSC, GN_EPS)
            link(v.memset(ROW1[:, :], 1.0))
            v.memset(UBUF[:, :, 0:1], 0.0).then_inc(set_free[0], 1)
            v.memset(DBUF[:, :, 0:1], 0.0).then_inc(set_free[1], 1)
            for n in range(3):
                lo(n)
            dve.wait_ge(prm_loaded[0], 16)
            normalise(0, X0, SQ0, RSTD, "mix")
            p = 0

            def shift(pv, s, dest, mu, step=0, i=None, tiles=4):
                dve.wait_ge(set_free[s], lin(pv // 2 + 2, step // 2, i))
                link(v.tensor_tensor(DBUF[:, 0:tiles, :], UBUF[:, 0:tiles, 0:T], UBUF[:, 0:tiles, 1:T + 1],
                                     ALU.subtract))
                for m in range(tiles):
                    ins = v.scalar_tensor_tensor(out=dest(m), in0=DBUF[:, m, :], scalar=mu(m),
                                                 in1=UBUF[:, m, 1:T + 1], op0=ALU.mult, op1=ALU.add)
                ins.then_inc(shift_out, 1)

            for c in range(8):
                tick(S_MISC + c)
            shift(0, 0, lambda m: MISC[:, m, :], lambda m: prmc("mu", 24 + m), tiles=3)
            two_pi = 2 * math.pi
            magic = 1.5 * 2 ** 23
            c1 = 6.28125
            c2 = float(np.float32(two_pi - c1) - np.float32(two_pi - c1) % np.float32(2.0 ** -19))
            c3 = two_pi - c1 - c2
            lim = 3.1415925
            dve.wait_ge(pos_loaded, 16)
            link(v.tensor_copy(RA[:, :], PI32[:, :]))
            link(v.tensor_scalar(RA[:, :], RA[:, :], prmc("invf", 0), None, ALU.mult))
            link(v.tensor_scalar(RB[:, :], RA[:, :], 1 / two_pi, magic, ALU.mult, ALU.add))
            link(v.tensor_scalar(RB[:, :], RB[:, :], -magic, None, ALU.add))
            for ck in (c1, c2, c3):
                link(v.scalar_tensor_tensor(out=RA[:, :], in0=RB[:, :], scalar=-ck, in1=RA[:, :], op0=ALU.mult,
                                            op1=ALU.add))
            v.tensor_scalar(SIN[:, :], RA[:, :], lim, -lim, ALU.min, ALU.max).then_inc(trig_in, 1)
            link(v.tensor_scalar(RB[:, :], RA[:, :], math.pi / 2, None, ALU.add))
            dve.wait_ge(shift_out, 1)
            link(v.tensor_scalar(RC[:, :], RB[:, :], math.pi, -two_pi, ALU.is_gt, ALU.mult))
            link(v.tensor_tensor(RB[:, :], RB[:, :], RC[:, :], ALU.add))
            v.tensor_scalar(COS[:, :], RB[:, :], lim, -lim, ALU.min, ALU.max).then_inc(trig_in, 1)
            p = 1
            with dve.Fori(0, 2) as i:
                steps.enter(i, 2)
                for q in range(2):
                    for c in range(8):
                        tick(S_KR + 8 * q + c, 16, i)
                    shift(p + q, (p + q) % 2,
                          lambda m: KRV[:, bass.ds(8 * i + 4 * q + m, 1), :].rearrange("p a b -> p (a b)"),
                          lambda m: PRM[:, bass.ds(8 * i + 4 * q + m + COL["mu"][0], 1)], 2, i)
            steps.leave(2)
            p += 4

            def prepare(b, step):
                t = slice(4 * b, 4 * b + 4)
                kx, rx, ax, bx = KRV[:, t, :], KRV[:, MT + 4 * b:MT + 4 * b + 4, :], RWA[:, t, :], RWB[:, t, :]

                def chan(name):
                    at = COL[name][0] + 4 * b
                    return bcast(PRM[:, at:at + 4], T)

                if step == 0:
                    dve.wait_ge(shift_out, 5)
                    link(v.tensor_tensor(T1[:, :, :], kx, chan("k_k"), ALU.mult))
                    v.tensor_tensor(T2[:, :, :], T1[:, :, :], T1[:, :, :], ALU.mult).then_inc(kk_sq, 1)
                elif step == 1:
                    dve.wait_ge(kk_root, 2 * b + 2)
                    link(v.tensor_scalar(T2[:, :, :], T2[:, :, :], 1e-12, None, ALU.max))
                    link(v.reciprocal(T2[:, :, :], T2[:, :, :]))
                    link(v.tensor_tensor(T1[:, :, :], T1[:, :, :], T2[:, :, :], ALU.mult))
                elif step == 2:
                    dve.wait_ge(lora_read, 20)
                    link(v.scalar_tensor_tensor(out=T2[:, :, :], in0=bx, scalar=-1.0, in1=chan("k_a"),
                                                op0=ALU.add, op1=ALU.mult))
                    link(v.scalar_tensor_tensor(out=kx, in0=T2[:, :, :], scalar=1.0, in1=kx,
                                                op0=ALU.add, op1=ALU.mult))
                elif step == 3:
                    v.scalar_tensor_tensor(out=T3[:, :, :], in0=T1[:, :, :], scalar=-1.0, in1=bx,
                                           op0=ALU.mult, op1=ALU.mult)
                    for m in range(4):
                        ins = v.tensor_tensor_scan(T4[:, m, :], ROW1[:, :], RWA[:, 4 * b + m, :], 0.0, ALU.mult,
                                                   ALU.add)
                    link(ins)
                elif step == 4:
                    t4 = T4[:, :, :].rearrange("p m (c t) -> p (m c) t", c=NC)
                    link(v.tensor_tensor(T2[:, :, :].rearrange("p m (c t) -> p (m c) t", c=NC), t4,
                                         t4[:, :, 63:64].to_broadcast([P, 4 * NC, CL]), ALU.subtract))
                    link(v.tensor_tensor(MD[:, :], T4[:, :, 191:192].rearrange("p a b -> p (a b)"),
                                         T4[:, :, 63:64].rearrange("p a b -> p (a b)"), ALU.subtract))
                    v.tensor_tensor(T4[:, :, :], T2[:, :, :], ax, ALU.subtract).then_inc(dec_in, 1)
                elif step == 5:
                    dve.wait_ge(dec_exp, 4 * b + 4)
                    link(v.tensor_tensor(rx, rx, ax, ALU.mult))
                    link(v.tensor_tensor(ax, T1[:, :, :], T4[:, :, :], ALU.mult))
                else:
                    link(v.tensor_tensor(kx, kx, T2[:, :, :], ALU.mult))
                    v.tensor_tensor(bx, T3[:, :, :], T2[:, :, :], ALU.mult).then_inc(rw_prep, 1)

            sin2 = SIN[:, :].unsqueeze(1).to_broadcast([P, 2, T])
            cos2 = COS[:, :].unsqueeze(1).to_broadcast([P, 2, T])

            def rope(m):
                x = BR[:, 0, 2 * m:2 * m + 2, :]
                dve.wait_ge(trig_out, 2)
                dve.wait_ge(rope_mm, m + 1)
                v.tensor_tensor(RT[:, :, :], BK[m % 2][:, :].rearrange("p (a b) -> p a b", a=2), sin2, ALU.mult)\
                    .then_inc(rope_read, 1)
                link(v.tensor_tensor(x, x, cos2, ALU.mult))
                dve.wait_ge(rope_read, m + 1)
                v.tensor_tensor(x, x, RT[:, :, :], ALU.add).then_inc(rope_done, 1)
                dve.wait_ge(rope_done, m + 1)

            def ret_weigh(hd):
                dve.wait_ge(dm_loaded, 16)
                dve.wait_ge(sc_mm, hd + 1)
                if hd >= 2:
                    dve.wait_ge(ov_mm, hd - 1)
                v.tensor_tensor(SR[:, hd % 2, :], BK[hd % 2][:, 0:384], DM[:, hd, :], ALU.mult).then_inc(sc_read, 1)

            def gla_mask(hd):
                dve.wait_ge(masks_set, 1)
                dve.wait_ge(sc_mm, 4 + hd + 1)
                if hd >= 2:
                    dve.wait_ge(ov_mm, 4 + hd - 1)
                v.copy_predicated(GSC[:, hd % 2, :, :], mask(1, 2), BK[0][:, 0:T].rearrange("p (c t) -> p c t", c=2))\
                    .then_inc(sc_read, 1)

            def head_recip(b):
                dve.wait_ge(on_root, 2 * b + 2)
                link(v.reciprocal(RS4[:, :, :], RS4[:, :, :]))

            def head_scale(b):
                for e in range(2):
                    o = BR[:, b, 4 * e:4 * e + 4, :]
                    if b == 0:
                        ins = v.tensor_tensor(o, o, RS4[:, :, :], ALU.mult)
                    else:
                        ins = v.scalar_tensor_tensor(out=o, in0=o, scalar=prmc("gnorm", e), in1=RS4[:, :, :],
                                                     op0=ALU.mult, op1=ALU.mult)
                link(ins)
                o = BR[:, b, 0:8, :].rearrange("p (e h) t -> p e h t", e=2)
                v.tensor_tensor(o, o, BR[:, b, 16:24, :].rearrange("p (h e) t -> p e h t", e=2), ALU.mult)\
                    .then_inc(o_final, 1)

            def output_lo(b):
                dve.wait_ge(op_hi, b + 1)
                v.tensor_tensor(OP[b][:, 1, :, :], BR[:, b, 0:8, :], OP[b][:, 0, :, :].bitcast(F32), ALU.subtract)\
                    .then_inc(op_lo, 1)

            parts = ({(0, 1): 0, (1, 0): 1, (1, 1): 2, (1, 2): 3, (1, 3): 4, (1, 7): 5, (2, 0): 6},
                     {(0, 1): 0, (0, 5): 1, (0, 6): 2, (0, 7): 3, (1, 0): 4, (1, 4): 5, (1, 5): 6})

            def side(b, q, c):
                if (q, c) in parts[b]:
                    prepare(b, parts[b][q, c])
                elif b == 0:
                    if (q, c) == (2, 1):
                        link(v.tensor_scalar(LT2[:, :, :], LG[:, :, :], 0.0, None, ALU.min))
                        dve.wait_ge(log_sp, 1)
                        link(v.tensor_tensor(LG[:, :, :], LT2[:, :, :], LT1[:, :, :], ALU.subtract))
                    elif q == 2 and 3 <= c < 7:
                        rope(c - 3)
                    elif (q, c) in ((3, 2), (3, 4)):
                        ret_weigh((c - 2) // 2)
                    elif (q, c) in ((4, 1), (4, 3)):
                        ret_weigh(2 + c // 2)
                    elif (q, c) == (5, 4):
                        head_recip(0)
                else:
                    if (q, c) == (0, 2):
                        head_scale(0)
                    elif (q, c) == (2, 0):
                        output_lo(0)
                    elif (q, c) == (2, 2):
                        for hd in range(HEADS):
                            ins = v.tensor_tensor_scan(GI[:, hd, :], ROW1[:, :], LG[:, hd, :], 0.0, ALU.mult, ALU.add)
                        link(ins)
                    elif (q, c) == (2, 3):
                        gi = GI[:, :, :].rearrange("p m (c t) -> p (m c) t", c=NC)
                        v.tensor_tensor(GD[:, :, :].rearrange("p m (c t) -> p (m c) t", c=NC), gi,
                                        gi[:, :, 63:64].to_broadcast([P, HEADS * NC, CL]), ALU.subtract)
                        v.tensor_tensor(GMD[:, :], GI[:, :, 191:192].rearrange("p a b -> p (a b)"),
                                        GI[:, :, 63:64].rearrange("p a b -> p (a b)"), ALU.subtract)\
                            .then_inc(gdec_in, 1)
                    elif (q, c) == (2, 6):
                        dve.wait_ge(gdec_exp, 3)
                        v.scalar_tensor_tensor(out=BR[:, 1, 0:4, :], in0=BR[:, 1, 0:4, :], scalar=DK ** -0.5,
                                               in1=GI[:, :, :], op0=ALU.mult, op1=ALU.mult)
                    elif (q, c) == (2, 7):
                        v.tensor_tensor(BR[:, 1, 4:8, :], BR[:, 1, 4:8, :], GD[:, :, :], ALU.mult).then_inc(gqk, 1)
                        link(v.memset(GSC[:, :, :, :], 0.0))
                    elif q == 4 and c % 2 == 0:
                        gla_mask(c // 2)
                    elif (q, c) == (5, 3):
                        head_recip(1)
                    elif (q, c) == (6, 1):
                        head_scale(1)
                    elif (q, c) == (6, 5):
                        output_lo(1)

            for b in range(2):
                for q in range(6 + 2 * b):
                    s = p % 2
                    for c in range(8):
                        tick(S_QKVG + 48 * b + 8 * q + c)
                        side(b, q, c)
                    if q in (4, 5):
                        dve.wait_ge(g_sig, 2 * b + q - 3)
                        v.tensor_tensor(BR[:, b, 4 * q:4 * q + 4, :], DP[s][:, :, :], SG[:, :, :], ALU.mult)\
                            .then_inc(set_free[s], 1)
                    if (b, q) == (1, 5):
                        panel_read(dve, p)
                        v.memset(UBUF[:, :, 0:1], 0.0).then_inc(shift_out, 1)
                    if q >= 6:
                        shift(p, s, lambda m: KRV[:, 2 * MT + 4 * (q - 6) + m, :],
                              lambda m: prmc("mu", 2 * MT + 4 * (q - 6) + m))
                    p += 1
            count_reg = dve.alloc_register("count")
            for b in range(2):
                base = S_GB + 48 * b
                with dve.Fori(0, 4) as i:
                    steps.enter(i, IN_SQUARE)

                    def rank(value, per=1):
                        return lin(per * 4 * b + value, per, i)

                    def pair(x, k0):
                        return x[:, bass.ds(k0 + 4 * b + i, 1), :].rearrange("p a b -> p (a b)")

                    def masked_wait(s, count):
                        dve.reg_mov(count_reg, count)
                        dve.wait_ge(masks_set, 1)
                        dve.wait_ge(s, count_reg)

                    for k in range(12):
                        if k == 0:
                            masked_wait(bgram, rank(1))
                            for c in range(NC):
                                g = BK[c][:, :].rearrange("p (e x t) -> p e x t", e=2, x=2)
                                u = slice(2 * c, 2 * c + 2)
                                v.copy_predicated(XT[:, u, :], mask(0, 2), g[:, :, 0, :])
                                v.copy_predicated(ZM[:, u, :], mask(2, 2), g[:, :, 0, :])
                                ins = v.copy_predicated(GRB[:, u, :], mask(1, 2), g[:, :, 1, :])
                            ins.then_inc(bgram_read, 1)
                            dve.wait_ge(bgram_read, rank(1))
                            v.transpose(TM[:, :, :], ZM[:, :, :]).then_inc(t_start, 1)
                        if 2 <= k < 8:
                            lv = k - 1
                            masked_wait(delta_mm, rank(lv, LEVELS - 1))
                            if lv == IN_SQUARE + 1:
                                v.copy_predicated(half(TM[:, :, :], lv, 0), half_mask(9, lv, 0), packed(BK[2], lv))
                            z = v.copy_predicated(half(ZM[:, :, :], lv, 1), half_mask(2 + lv, lv, 1),
                                                  packed(BK[3], lv))
                            if lv <= IN_SQUARE:
                                link(z)
                                z = v.transpose(TM[:, :, :], ZM[:, :, :])
                            z.then_inc(t_grown, 1)
                        if k == 9:
                            dve.wait_ge(s_mm, rank(1))
                            for e in range(2):
                                w = slice(64 * e, 64 * e + 64)
                                ins = v.tensor_scalar(SB[w, w], BK[2][w, w], ES[w, bass.ds(4 * b + i, 1)], None,
                                                      ALU.mult)
                            ins.then_inc(s_read, 1)
                        tick(base + k, 12, i)
                        if k == 0:
                            masked_wait(kgram, rank(1))
                            for c in range(NC):
                                g = BK[2 + c][:, :].rearrange("p (e x t) -> p e x t", e=2, x=2)
                                u = slice(2 * c, 2 * c + 2)
                                v.copy_predicated(LAK[:, u, :], mask(0, 2), g[:, :, 0, :])
                                ins = v.copy_predicated(GRK[:, u, :], mask(1, 2), g[:, :, 1, :])
                            ins.then_inc(kgram_read, 1)
                        if k == 11:
                            dve.wait_ge(mean_mm, rank(2))
                            v.scalar_tensor_tensor(out=pair(KRV, MT), in0=BK[0][:, 0:T], scalar=-1.0 / 64,
                                                   in1=YS[:, :], op0=ALU.mult, op1=ALU.add).then_inc(centred, 1)
                            v.tensor_tensor(pair(KRV, 2 * MT), BK[1][:, 0:T], pair(KRV, 2 * MT), ALU.mult)\
                                .then_inc(bonus_done, 1)
                            s = (p + 1) % 2
                            dve.wait_ge(chunk_done, lin(base + 12, 12, i))
                            mg = MG[:, bass.ds(4 * i, 4), :]
                            if b == 0:
                                v.tensor_tensor(mg, DP[s][:, :, :], mg, ALU.mult).then_inc(set_free[s], 1)
                            else:
                                v.tensor_tensor(GT1[:, :, :], DP[s][:, :, :], GT1[:, :, :], ALU.mult)\
                                    .then_inc(set_free[s], 1)
                                dve.wait_ge(set_free[s], lin((p + 1) // 2 + 2, 1, i))
                                v.tensor_tensor(mg, mg, GT1[:, :, :], ALU.add).then_inc(merged, 1)
                steps.leave(4)
                p += 8
            y = KRV[:, MT:2 * MT, :]
            for q in range(4):
                for c in range(8):
                    tick(S_RW + 8 * q + c)
                    if q == 0 and c < 4:
                        dve.wait_ge(gn_root, 1)
                        link(v.reciprocal(RT8[:, 2 * c:2 * c + 2, :], RT8[:, 2 * c:2 * c + 2, :]))
                    elif (q, c) == (0, 4):
                        link(v.tensor_tensor(y, y, RT8[:, :, :], ALU.mult))
                    elif q == 0 and c in (5, 6):
                        for t in range(4 * (c - 5), 4 * (c - 4)):
                            ins = v.tensor_scalar(KRV[:, MT + t, :], KRV[:, MT + t, :], prmc("ln_w", t),
                                                  prmc("ln_b", t), ALU.mult, ALU.add)
                        link(ins)
                    elif (q, c) == (0, 7):
                        link(v.tensor_tensor(y, y, KRV[:, 2 * MT:3 * MT, :], ALU.add))
                    elif (q, c) == (1, 0):
                        dve.wait_ge(g_read, 8)
                        v.tensor_tensor(y, y, GG[:, :, :], ALU.mult).then_inc(orw, 1)
                    elif (q, c) == (1, 4):
                        dve.wait_ge(orw, 2)
                        v.tensor_tensor(OPR[1][:, :, :], y, OPR[0][:, :, :].bitcast(F32), ALU.subtract)\
                            .then_inc(orw_lo, 1)
                p += 1
            for q in range(4):
                t = slice(4 * q, 4 * q + 4)
                for c in range(4):
                    tick(S_RW + 32 + 4 * q + c)
                dve.wait_ge(chunk_done, S_RW + 32 + 4 * q + 4)
                v.tensor_tensor(GTM[:, :, :], DP[p % 2][:, :, :], GB[:, t, :], ALU.mult).then_inc(set_free[p % 2], 1)
                dve.wait_ge(set_free[p % 2], p // 2 + 2)
                v.tensor_tensor(MG[:, t, :], MG[:, t, :], GTM[:, :, :], ALU.add).then_inc(merged, 1)
                dve.wait_ge(mg_hi, q + 1)
                v.tensor_tensor(HL[:, t, :], MG[:, t, :], HH[:, t, :].bitcast(F32), ALU.subtract).then_inc(mg_lo, 1)
                p += 1
            dve.wait_ge(x_again, 16)
            for q in range(4):
                for c in range(8):
                    tick(S_O + 8 * q + c)
                    if q == 3 and c in (2, 4, 6):
                        h_lo(c // 2 - 1, 1, SQ)
                dve.wait_ge(chunk_done, S_O + 8 * q + 8)
                residual(p, q, "ffn")
                p += 1

            def conv(w, i, pc, n, step):
                tiles = 1 if w == 21 else 2

                def par(name, m):
                    return PRM[:, bass.ds((0 if i is None else 4 * i) + 2 * w + m + COL[name][0], 1)]

                dve.wait_ge(chunk_done, lin(n + 1, step, i))
                link(v.tensor_tensor(ZB[:, 0:tiles, 2:], DP[pc % 2][:, 0:tiles, :], rs_n(tiles), ALU.mult))
                for m in range(tiles):
                    ins = v.tensor_scalar(CV[:, m, :], ZB[:, m, 2:T + 2], par("cw2", m), par("cb", m), ALU.mult,
                                          ALU.add)
                link(ins)
                for j in (1, 0):
                    for m in range(tiles):
                        ins = v.scalar_tensor_tensor(out=CV[:, m, :], in0=ZB[:, m, j:T + j], scalar=par(f"cw{j}", m),
                                                     in1=CV[:, m, :], op0=ALU.mult, op1=ALU.add)
                    if j == 1:
                        link(ins)
                ins.then_inc(conv_done, 1)

            def rs_n(n):
                return RS[:, :].unsqueeze(1).to_broadcast([P, n, T])

            def act_product(w, i, pc):
                tiles = 1 if w == 21 else 2
                dve.wait_ge(gelu_done, lin(w + 1, 2, i))
                link(v.tensor_tensor(GE[:, 0:tiles, :], GE[:, 0:tiles, :], rs_n(tiles), ALU.mult))
                v.tensor_tensor(AV[:, 0:tiles, :], DP[pc % 2][:, tiles:2 * tiles, :], GE[:, 0:tiles, :], ALU.mult)\
                    .then_inc(set_free[pc % 2], 1)

            def act_low(w, i):
                tiles = 1 if w == 21 else 2
                dve.wait_ge(act_hi, lin(w + 1, 2, i))
                tile = 2 * w if i is None else 2 * w + 4 * i
                v.tensor_tensor(AL[:, bass.ds(tile, tiles), :], AV[:, 0:tiles, :],
                                AH[:, bass.ds(tile, tiles), :].bitcast(F32), ALU.subtract).then_inc(act_lo, 1)

            for c in range(8):
                tick(S_UP + c)
                if c == 0:
                    h_lo(3, 1, SQ)
            reciprocal_root(1, RS)
            link(v.memset(ZB[:, :, 0:2], 0.0))
            with dve.Fori(0, 10) as i:
                steps.enter(i, 8)
                for q in range(2):
                    for c in range(8):
                        tick(S_UP + 8 + 8 * q + c, 16, i)
                        if c == 0:
                            conv(q, i, p + q, S_UP + 8 * q + 7, 16)
                        elif c == 2:
                            act_product(q, i, p + q)
                        elif c == 4:
                            act_low(q, i)
            steps.leave(10)
            p += 20
            for c in range(4):
                tick(S_UP + 168 + c)
                if c == 0:
                    conv(20, None, p, S_UP + 167, 0)
                elif c == 2:
                    act_product(20, None, p)
            p += 1
            for q in range(4):
                for c in range(22):
                    tick(S_DOWN + 22 * q + c)
                    if (q, c) == (0, 0):
                        act_low(20, None)
                    elif (q, c) == (0, 1):
                        conv(21, None, p, S_UP + 171, 0)
                    elif (q, c) == (0, 3):
                        act_product(21, None, p)
                    elif (q, c) == (0, 5):
                        act_low(21, None)
                    elif (q, c) == (0, 15):
                        dve.wait_ge(p_hi, 1)
                        v.tensor_tensor(PXL[:, :, :], PX[:, :, :], PXH[:, :, :].bitcast(F32), ALU.subtract)\
                            .then_inc(p_lo, 1)
                    elif q and c == 3:
                        h_lo(q - 1, 2, SQ)
                dve.wait_ge(chunk_done, S_DOWN + 22 * q + 22)
                residual(p + 1 + q, q, "ple")
            p += 5
            for q in range(4):
                tick(S_PLE + q)
                if q == 1:
                    h_lo(3, 2, SQ)
                p += 1

            def ple_norm(q, pc):
                dve.wait_ge(chunk_done, S_PLE + 12 + 8 * q)
                v.tensor_tensor(GP[:, :, :], DP[pc % 2][:, :, :], rs_n(4), ALU.mult).then_inc(set_free[pc % 2], 1)

            def ple_add(q):
                t = slice(4 * q, 4 * q + 4)
                dve.wait_ge(ple_sig, q + 1)
                link(v.tensor_tensor(GP[:, :, :], GP[:, :, :], PG[:, t, :], ALU.mult))
                v.tensor_tensor(XR[:, t, :], XR[:, t, :], GP[:, :, :], ALU.add).then_inc(ple_used, 1)

            for q in range(4):
                for c in range(8):
                    tick(S_PLE + 4 + 8 * q + c)
                    if q and c == 0:
                        ple_norm(q - 1, p - 1)
                    elif q and c == 3:
                        ple_add(q - 1)
                if q == 0:
                    reciprocal_root(2, RS)
                p += 1
            ple_norm(3, p - 1)
            ple_add(3)
            normalise(3, XR, SQ, RS, "fin")

        @block.gpsimd
        def _(pool):
            g = nc.gpsimd
            pool.dma_start(CST[:, :, :], const).then_inc(prm_loaded[1], 16)
            pool.dma_start(PRM[:, :], prm).then_inc(prm_loaded[0], 16)
            pool.dma_start(MSKI[:, :, :], masks).then_inc(prm_loaded[2], 16)
            pool.wait_ge(prm_loaded[2], 16)
            g.tensor_copy(MSK[:, :, :], MSKI[:, :, :]).then_inc(masks_set, 1)
            pool.wait_ge(hl_ready, 4)
            pool.dma_start(LORA[:, 0:3, :], lora[:, 0:3, :]).then_inc(lora_loaded, 16)
            pool.dma_start(PI32[:, :], pos).then_inc(pos_loaded, 16)
            pool.wait_ge(rw_prep, 1)
            pool.dma_start(DM[:, :, :], dmask).then_inc(dm_loaded, 16)
            pool.wait_ge(op_lo, 2)
            for x, s in ((XT, zeroed), (LAK, zeroed), (GRB, zeroed), (GRK, zeroed),
                         (UP, zeroed), (VP, zeroed), (SB, zeroed), (P1S, zeroed), (BS, vt_mm), (AR, y_mm), (PR, mean_mm),
                         (YS, bonus_done), (SQS, var_read), (RH, merged)):
                g.memset(x[tuple(slice(None) for _ in x.shape)], 0.0).then_inc(s, 1)
            pool.wait_ge(zeroed, 8)
            pool.wait_ge(rw_prep, 2)
            for b in range(2):
                pool.wait_ge(shift_out, 7 + b)
                with pool.Fori(0, 4) as i:
                    def rank(value, per=1):
                        return lin(per * 4 * b + value, per, i)

                    def pair(x, k0, rows=slice(None), cols=slice(None)):
                        return x[rows, bass.ds(k0 + 4 * b + i, 1), cols].rearrange("p a b -> p (a b)")

                    pool.wait_ge(vt_mm, rank(1))
                    g.tensor_copy(BS[:, :], pair(RWB, 0)).then_inc(staged, 1)
                    g.tensor_copy(KS[:, :], pair(KRV, 0)).then_inc(staged, 1)
                    g.tensor_copy(VS[:, :], pair(KRV, 2 * MT)).then_inc(staged, 1)
                    pool.wait_ge(staged, rank(3, STAGED))
                    own = BLK[:, 0:P:64].unsqueeze(2).to_broadcast([P, 2, T])
                    for x, src in ((BP, BS), (KP, KS)):
                        g.tensor_tensor(x[:, :, :], src[:, :].unsqueeze(1).to_broadcast([P, 2, T]), own, ALU.mult)\
                            .then_inc(staged, 1)
                    pool.wait_ge(y_mm, rank(1))
                    g.tensor_copy(AR[:, :, 0, :], pair(RWA, 0).rearrange("p (c t) -> p c t", c=NC)).then_inc(staged, 1)
                    g.tensor_copy(AR[:, :, 1, :], pair(KRV, MT).rearrange("p (c t) -> p c t", c=NC))\
                        .then_inc(staged, 1)
                    g.tensor_copy(ZM[:, :, :], IDENT.unsqueeze(1).to_broadcast([P, 4, P])).then_inc(staged, 1)
                    pool.wait_ge(mean_mm, rank(1))
                    g.tensor_copy(RKC, PRM[:, bass.ds(COL["r_k"][0] + 4 * b + i, 1)]).then_inc(rk_staged, 1)
                    pool.wait_ge(staged, rank(STAGED, STAGED))
                    g.tensor_tensor(PR[:, :].rearrange("p (c t) -> p c t", c=NC), AR[:, :, 1, :],
                                    KS[:, :].rearrange("p (c t) -> p c t", c=NC), ALU.mult).then_inc(rk_staged, 1)
                    pool.wait_ge(rk_staged, rank(2, 3))
                    g.tensor_tensor(PR[:, :], PR[:, :], RKC.to_broadcast([P, T]), ALU.mult).then_inc(rk_staged, 1)
            pool.wait_ge(chunk_done, S_GB + 48)
            pool.dma_start(G2[:, :, :], lora[:, 3:5, :]).then_inc(g2_loaded, 16)
            pool.wait_ge(gn_root, 1)
            pool.dma_start(XR[:, :, :], xT).then_inc(x_again, 16)
            pool.wait_ge(act_lo, 22)
            pool.dma_start(PX[:, :, :], pT).then_inc(p_loaded, 16)
            for k in range(4):
                pool.wait_ge(h_ready, 12 + k + 1)
                pool.dma_start(outT[:, 4 * k:4 * k + 4, :], SQ[:, 4 * k:4 * k + 4, :]).then_inc(out_stored, 16)
            pool.wait_ge(out_stored, 64)


def _layout(inputs):
    f = lambda k: np.asarray(inputs[k])[0]

    def rows(w, cols):
        w = w[:, cols]
        kt = -(-w.shape[0] // (2 * P)) * 2
        full = np.zeros((kt * P, 512), np.float32)
        full[:w.shape[0], :w.shape[1]] = w
        return full.reshape(kt // 2, 2, P, 512).transpose(0, 2, 1, 3).reshape(kt // 2, P, CH)

    def sl(a, n):
        return slice(a, a + n)

    w = f("w_in")
    up, down, wo = f("w_up"), f("w_down"), f("w_o")
    parts = [rows(np.concatenate([w[:, sl(RWKV0 + 3 * MW, 288)], w[:, sl(RWKV0 - GLA_LORA, GLA_LORA)]], 1),
                  slice(None))]
    for base in (RWKV0 + MW, RWKV0):
        parts += [rows(w, sl(base + 512 * j, 512)) for j in range(2)]
    for base in (RET0, GLA0):
        parts += [rows(w, sl(base + 512 * j, 512)) for j in range(6)]
    parts += [rows(w, sl(RWKV0 + 2 * MW + 512 * j, 512)) for j in range(2)]
    for gate, br in ((2, "w_br_ret"), (0, "w_br_gla")):
        for j in range(4):
            parts += [rows(w, sl(GATE0 + gate * D + 512 * j, 512)), rows(f(br), sl(512 * j, 512))]
    parts += [rows(w, sl(GATE0 + D + 512 * j, 512)) for j in range(4)]
    parts += [rows(f("w_br_rwkv"), sl(512 * j, 512)) for j in range(4)]
    parts += [rows(wo, sl(512 * j, 512)) for j in range(4)]
    for j in range(21):
        parts.append(rows(np.concatenate([up[:, sl(256 * j, 256)], up[:, sl(DFF + 256 * j, 256)]], 1), slice(None)))
    last = np.concatenate([up[:, sl(256 * 21, P)], up[:, sl(DFF + 256 * 21, P)]], 1)
    parts.append(last.reshape(4, 4, P, 256).transpose(0, 2, 1, 3).reshape(4, P, CH))
    parts += [rows(down, sl(512 * j, 512)) for j in range(4)]
    parts += [rows(f("w_ple_proj"), sl(512 * j, 512)) for j in range(4)]
    parts += [rows(f("w_ple_gate"), sl(512 * j, 512)) for j in range(4)]
    stream = np.concatenate(parts, 0)

    def col(x, n):
        x = np.asarray(x).reshape(-1)
        full = np.zeros(n * P, np.float32)
        full[:x.size] = x
        return full.reshape(n, P).T

    mu = f("rwkv_mu")
    mu = np.concatenate([mu[MW:2 * MW], mu[:MW], mu[2 * MW:]])
    invf = (np.float32(10000.0) ** (-np.arange(0, DK, 2, dtype=np.float32) / np.float32(DK))).astype(np.float32)
    cw = f("conv_w")
    cols = dict(mix=f("mix_norm"), ffn=f("ffn_norm"), ple=f("ple_norm"), fin=inputs["final_norm"], mu=mu,
                w0=f("rwkv_w0"), a0=f("rwkv_a0"), k_k=f("rwkv_k_k"), k_a=f("rwkv_k_a"), r_k=f("rwkv_r_k"),
                ln_w=f("rwkv_ln_w"), ln_b=f("rwkv_ln_b"), bdec=f("gla_b_decay"), gnorm=f("gla_norm"), cw0=cw[0],
                cw1=cw[1], cw2=cw[2], cb=f("conv_b"), invf=np.concatenate([invf, invf]), pad=np.zeros(1, np.float32))
    prm = np.concatenate([col(cols[n], k) for n, k in _COLS], 1)

    lora = np.zeros((P, 5, MW), np.float32)
    lora[0:64, 0] = f("rwkv_w2")
    lora[64:128, 1] = f("rwkv_a2")
    lora[32:48, 2, 0:512] = f("gla_w_decay")
    g2 = f("rwkv_g2")
    lora[:, 3] = g2[0:P]
    lora[0:32, 4] = g2[P:]

    a, b = np.arange(P)[:, None], np.arange(P)[None, :]
    const = np.zeros((P, 4, P), np.float32)
    const[:, 0] = a == b
    const[:, 1] = a // 64 == b // 64
    const[:, 2] = 1.0
    const[:, 3] = np.where(a == (b + 64) % P, np.where(b < 64, -1.0, 1.0), 0.0)
    masks = np.zeros((P, 10, P), np.int32)
    masks[:, 0] = a < b
    masks[:, 1] = a <= b
    for lv in range(LEVELS):
        m = 2 ** lv
        same = a // (2 * m) == b // (2 * m)
        masks[:, 2 + lv] = same & (a % (2 * m) < m) & (b % (2 * m) >= m)
        if lv == IN_SQUARE + 1:
            masks[:, 9] = masks[:, 2 + lv].T
    gamma = 1.0 - 2.0 ** (-5.0 - np.arange(HEADS))
    diff = np.arange(T)[None, :] - a
    dm = np.stack([np.where(diff >= 0, gm ** np.maximum(diff, 0), 0.0) * DK ** -0.5 for gm in gamma], 1)
    dmask = np.concatenate([dm, dm[:, :, 0:P]], 2).astype(np.float32)

    def chan(x, n):
        return np.asarray(x).T.reshape(n, P, T).transpose(1, 0, 2)

    return dict(stream=stream, xT=chan(inputs["x"][0], DT), prm=prm, const=const, masks=masks, dmask=dmask,
                pos=np.broadcast_to(np.asarray(inputs["positions"]).reshape(1, T), (P, T)), lora=lora,
                pT=chan(f("p")[0], 2))


def kernel(**inputs):
    import concourse.bacc as bacc
    from concourse.bass_utils import run_bass_kernel_spmd

    nc = bacc.Bacc("TRN2", target_bir_lowering=False, num_devices=1)
    arrays, args = {}, []
    for name, x in _layout(inputs).items():
        x = np.ascontiguousarray(x)
        arrays[f"in_{name}"] = x
        args.append(nc.dram_tensor(f"in_{name}", x.shape, mybir.dt.from_np(x.dtype), kind="ExternalInput").ap())
    out = nc.dram_tensor("out", (P, DT, T), F32, kind="ExternalOutput").ap()
    bass_hybrid_block(nc, *args, out)
    got = run_bass_kernel_spmd(nc, [arrays], core_ids=[0]).results[0]["out"]
    return np.ascontiguousarray(got.transpose(2, 1, 0).reshape(1, T, D))
```

```python
import math
from contextlib import ExitStack

import numpy as np

import concourse.bass as bass
from concourse import mybir

F32 = mybir.dt.float32
F32R = mybir.dt.float32r
I32 = mybir.dt.int32
U8 = mybir.dt.uint8
ALU = mybir.AluOpType
ACT = mybir.ActivationFunctionType

P = 128
T = 256
D = 2048
MW = 1024
DFF = 5504
PLE = 256
DT, MT, FT = D // P, MW // P, DFF // P
HEADS = 4
DK = 128
DV = 256
GLA_LORA = 16
RCOLS = 3 * MW + 64 + 64 + 160
GLA0, RWKV0 = 0, 2 * 512 + 2 * MW + GLA_LORA
RET0 = RWKV0 + RCOLS
GATE0 = RET0 + 2 * 512 + 2 * MW
EPS = 1e-6
GN_EPS = 64e-5
C_DECAY = math.exp(-0.5)
CL = 128
NC = T // CL

CH = 1024
RING = 4

_COLS = [("mix", 16), ("ffn", 16), ("ple", 16), ("fin", 16), ("mu", 27), ("w0", 8), ("a0", 8), ("k_k", 8),
         ("k_a", 8), ("r_k", 8), ("ln_w", 8), ("ln_b", 8), ("bdec", 4), ("gnorm", 2), ("cw0", FT), ("cw1", FT),
         ("cw2", FT), ("cb", FT), ("invf", 1), ("pad", 1)]
COL = {}
for _n, _k in _COLS:
    COL[_n] = sum(COL[m][1] for m in COL), _k
NPRM = sum(k for _, k in _COLS)

S_MISC = 0
S_KR = S_MISC + 8
S_QKVG = S_KR + 32
S_V = S_QKVG + 96
S_GB = S_V + 16
S_RW = S_GB + 96
S_O = S_RW + 48
S_UP = S_O + 32
S_DOWN = S_UP + 172
S_PLE = S_DOWN + 88
N_CHUNK = S_PLE + 36

LEVELS = 7
IN_SQUARE = 4
STAGED = 8


def bass_hybrid_block(nc, stream, xT, prm, const, masks, dmask, pos, lora, pT, outT):
    FIX = 16512
    KB = 1024

    ctx = ExitStack()
    with ctx:
        def at(name, shape, off, dt=F32):
            return nc.alloc_sbuf_tensor_at(name, shape, dt, offset=off)

        def sem(name):
            return ctx.enter_context(nc.semaphore(name))

        o = FIX
        RAW = at("raw", [P, RING, CH], o); o += 16 * KB
        WH = at("w_hi", [P, RING, CH], o, F32R); o += 16 * KB
        WL = at("w_lo", [P, RING, CH], o, F32R); o += 16 * KB
        HH = at("h_hi", [P, DT, T], o, F32R); o += 16 * KB
        HL = at("h_lo", [P, DT, T], o, F32R); o += 16 * KB
        PRM = at("prm", [P, NPRM], o); o += (NPRM * 4 + 31) // 32 * 32
        CST = at("const", [P, 4, P], o); o += 2048
        MSK_AT = o
        MSK = at("masks", [P, 7, P], o, U8); o += 8 * P
        MISC = at("misc", [P, 3, T], o); o += 3072
        ES = at("state_scale", [P, MT + 3], o); o += 64
        o = (o + 31) // 32 * 32
        U = o
        assert U + 119 * KB <= 229344, U

        def un(name, shape, kb, dt=F32):
            return at(name, shape, U + int(kb * KB), dt)

        EPSC, GNEPSC, RKC = ES[:, MT:MT + 1], ES[:, MT + 1:MT + 2], ES[:, MT + 2:MT + 3]
        IDENT, BLK, ONES, PERM = CST[:, 0, :], CST[:, 1, :], CST[:, 2, :], CST[:, 3, :]

        def prmc(name, k):
            return PRM[:, COL[name][0] + k:COL[name][0] + k + 1]

        RWA = un("rw_a", [P, MT, T], 0)
        RWB = un("rw_b", [P, MT, T], 8)
        KRV = un("rw_krv", [P, 3 * MT, T], 16)
        MSKI = un("masks_int", [P, 7, P], 0, I32)
        X0 = un("x_in", [P, DT, T], 88)
        SQ0 = un("sq_in", [P, DT, T], 64)
        RSTD = un("rstd_in", [P, T], 60)
        UBUF = un("shift_u", [P, 4, T + 1], 112)
        DBUF = un("shift_d", [P, 4, T], 107)
        LORA = un("lora", [P, 3, MW], 64)
        LG = un("log_a", [P, HEADS, T], 88)
        LT1 = un("log_t1", [P, HEADS, T], 80)
        LT2 = un("log_t2", [P, HEADS, T], 84)
        BR = un("branch", [P, 2, 24, T], 40)
        MD = un("mid_diff", [P, 4], 117)
        T1 = un("t1", [P, 4, T], 96)
        T2 = un("t2", [P, 4, T], 100)
        T3 = un("t3", [P, 4, T], 104)
        T4 = un("t4", [P, 4, T], 108)
        SG = un("sig", [P, 4, T], 112)
        ROW1 = un("one_row", [P, T], 118)
        COS = un("cos", [P, T], 76)
        SIN = un("sin", [P, T], 77)
        RT = un("rope_t", [P, 2, T], 94)
        PI32 = un("pos", [P, T], 104, I32)
        RA = un("angle", [P, T], 105)
        RB = un("angle_b", [P, T], 106)
        RC = un("angle_c", [P, T], 107)
        DM = un("dmask", [P, HEADS, 384], 96)
        SR = un("scores", [P, 2, 384], 102)
        RS4 = un("att_rs", [P, HEADS, T], 92)
        GI = un("gla_inc", [P, HEADS, T], 92)
        GD = un("gla_dec", [P, HEADS, T], 96)
        GSC = un("gla_sc", [P, 2, NC, CL], 100)
        GKT = un("gla_kt", [P, 2, CL], 102)
        GS = un("gla_s", [P, 2, DV], 103)
        GES = un("gla_es", [P, HEADS], 105)
        GMD = un("gla_md", [P, HEADS], 106)
        OP = [un(f"o_parts{b}", [P, 2, MT, T], 48 + 24 * b, F32R) for b in range(2)]
        AR = un("st_ar", [P, NC, 2, CL], 40)
        BP = un("st_b", [P, 2, T], 42)
        KP = un("st_k", [P, 2, T], 44)
        BS = un("st_b_all", [P, T], 46)
        KS = MISC[:, 0, :]
        VS = un("st_v", [P, T], 47)
        XT = un("x_t", [P, 4, CL], 64)
        LAK = un("l_ak", [P, 4, CL], 66)
        GRB = un("g_rb", [P, 4, CL], 68)
        GRK = un("g_rk", [P, 4, CL], 70)
        TM = un("t_inv", [P, 4, CL], 88)
        ZM = un("t_inv_t", [P, 4, CL], 90)
        P1S = un("p1", [P, 4, CL], 92)
        UP = un("u_pad", [P, NC, 4, 64], 94)
        VP = un("v_pad", [P, NC, 4, 64], 96)
        BKT = un("bk_tok", [P, 2, P], 98)
        SB = un("s_blk", [P, P], 99)
        RH = un("rhs", [P, P], 99.5)
        YS = un("y_s", [P, T], 100)
        PR = un("rk_prod", [P, T], 101)
        SQS = un("sq_s", [P, T], 102)
        MG = un("merged", [P, DT, T], 103)
        GT1 = un("gate_gla", [P, 4, T], 48)
        GB = un("gate_rwkv", [P, DT, T], 48)
        G2 = un("g2", [P, 2, MW], 56)
        GG = un("g_rwkv", [P, MT, T], 16)
        OPR = [un("o_rw_hi", [P, MT, T], 80, F32R), un("o_rw_lo", [P, MT, T], 64, F32R)]
        RT8 = un("rw_rstd", [P, MT, T], 88)
        GTM = un("gate_times", [P, 4, T], 96)
        XR = un("x_res", [P, DT, T], 0)
        SQ = un("sq", [P, DT, T], 103)
        RS = un("rstd", [P, T], 102)
        AH = un("act_hi", [P, FT, T], 16, F32R)
        AL = un("act_lo", [P, FT, T], 59, F32R)
        ZB = un("z", [P, 2, T + 2], 103)
        CV = un("conv", [P, 2, T], 106)
        GE = un("gelu", [P, 2, T], 108)
        AV = un("act", [P, 2, T], 110)
        PG = un("p_proj", [P, DT, T], 16)
        PX = un("p_in", [P, 2, T], 103)
        PXH = at("p_hi", [P, 2, T], MSK_AT, F32R)
        PXL = at("p_lo", [P, 2, T], MSK_AT + 2 * KB, F32R)
        GP = un("ple_gate", [P, 4, T], 38)

        DP = [ctx.enter_context(nc.psum_tensor(f"dense{s}", [P, 4, T], F32)) for s in range(2)]
        BK = [ctx.enter_context(nc.psum_tensor(f"side{s}", [P, 512], F32)) for s in range(4)]

        raw_loaded = [sem(f"raw_loaded{s}") for s in range(RING)]
        hi_ready = sem("hi_ready")
        lo_ready = sem("lo_ready")
        chunk_done = sem("chunk_done")
        set_free = [sem(f"set_free{s}") for s in range(2)]
        x_loaded = [sem(f"x_loaded{g}") for g in range(4)]
        masks_set = sem("masks_set")
        prm_loaded = [sem(f"prm_loaded{k}") for k in range(3)]
        sq_ready = sem("sq_ready")
        sq_pairs = sem("sq_pairs")
        sq_added = sem("sq_added")
        on_added = sem("on_added")
        ssq_done = sem("ssq_done")
        rs_root = sem("rs_root")
        h_ready = sem("h_ready")
        hh_ready = sem("hh_ready")
        hl_ready = sem("hl_ready")
        dve_step = sem("dve_step")
        act_step = sem("act_step")
        shift_out = sem("shift_out")
        lora_loaded = sem("lora_loaded")
        misc_act = sem("misc_act")
        lora_mm = sem("lora_mm")
        lora_read = sem("lora_read")
        log_sp = sem("log_sp")
        g_sig = sem("g_sig")
        kk_sq = sem("kk_sq")
        kk_ssq = sem("kk_ssq")
        kk_root = sem("kk_root")
        dec_in = sem("dec_in")
        dec_exp = sem("dec_exp")
        rw_prep = sem("rw_prep")
        pos_loaded = sem("pos_loaded")
        dm_loaded = sem("dm_loaded")
        trig_in = sem("trig_in")
        trig_out = sem("trig_out")
        rope_mm = sem("rope_mm")
        rope_read = sem("rope_read")
        rope_done = sem("rope_done")
        sc_mm = sem("sc_mm")
        sc_read = sem("sc_read")
        ov_mm = sem("ov_mm")
        ov_read = sem("ov_read")
        on_sq = sem("on_sq")
        on_ssq = sem("on_ssq")
        on_root = sem("on_root")
        o_final = sem("o_final")
        op_hi = sem("op_hi")
        op_lo = sem("op_lo")
        gdec_in = sem("gdec_in")
        gdec_exp = sem("gdec_exp")
        gqk = sem("gqk")
        gkt_mm = sem("gkt_mm")
        gkt_read = sem("gkt_read")
        gs_mm = sem("gs_mm")
        gs_read = sem("gs_read")
        zeroed = sem("zeroed")
        staged = sem("staged")
        rk_staged = sem("rk_staged")
        bgram = sem("bgram")
        kgram = sem("kgram")
        bgram_read = sem("bgram_read")
        kgram_read = sem("kgram_read")
        t_start = sem("t_start")
        vt_mm = sem("vt_mm")
        vt_read = sem("vt_read")
        p1_mm = sem("p1_mm")
        p1_read = sem("p1_read")
        delta_mm = sem("delta_mm")
        t_grown = sem("t_grown")
        rhs_mm = sem("rhs_mm")
        rhs_read = sem("rhs_read")
        u_mm = sem("u_mm")
        u_read = sem("u_read")
        s_mm = sem("s_mm")
        s_read = sem("s_read")
        y_mm = sem("y_mm")
        y_read = sem("y_read")
        mean_mm = sem("mean_mm")
        centred = sem("centred")
        var_sq = sem("var_sq")
        var_mm = sem("var_mm")
        var_read = sem("var_read")
        bonus_done = sem("bonus_done")
        merged = sem("merged")
        g2_loaded = sem("g2_loaded")
        g_mm = sem("g_mm")
        g_read = sem("g_read")
        gn_root = sem("gn_root")
        orw = sem("orw")
        orw_lo = sem("orw_lo")
        mg_hi = sem("mg_hi")
        mg_lo = sem("mg_lo")
        x_again = sem("x_again")
        conv_done = sem("conv_done")
        gelu_done = sem("gelu_done")
        act_hi = sem("act_hi")
        act_lo = sem("act_lo")
        p_loaded = sem("p_loaded")
        p_hi = sem("p_hi")
        p_lo = sem("p_lo")
        ple_sig = sem("ple_sig")
        ple_used = sem("ple_used")
        out_ready = [sem(f"out_ready{g}") for g in range(4)]
        rs_last = sem("rs_last")
        out_stored = sem("out_stored")

        block = ctx.enter_context(nc.Block())

        def lin(value, step, i):
            return value if i is None else value + step * i

        def bcast(ap, n):
            return ap.unsqueeze(2).to_broadcast([ap.shape[0], ap.shape[1], n])

        def mask(k, n):
            return MSK[:, k, :].unsqueeze(1).to_broadcast([P, n, P])

        def half(x, lv, h):
            names = "u " if len(x.shape) == 3 else ""
            v = x.rearrange(f"p {names}(g h m) -> p {names}g h m", h=2, m=2 ** lv)
            return v[:, :, :, h, :] if names else v[:, :, h, :]

        def sides(j):
            return slice(64 * j, 64 * j + 32), slice(64 * j + 32, 64 * j + 64)

        def packed(bank, lv, u=None):
            if u is None:
                return bank[:, 0:2 * P].rearrange("p (u g m) -> p u g m", u=4, m=2 ** lv)
            return bank[:, u * 64:(u + 1) * 64].rearrange("p (g m) -> p g m", m=2 ** lv)

        def half_mask(k, lv, h):
            x = half(MSK[:, k, :], lv, h)
            return x.unsqueeze(1).to_broadcast([P, 4, x.shape[1], x.shape[2]])

        def panel_read(eng, p):
            eng.wait_ge(set_free[p % 2], p // 2 + 2)

        class Steps:

            def __init__(self, eng, s):
                self.eng, self.sem, self.n, self.i, self.per, self.at0 = eng, s, 0, None, 0, 0

            def link(self, ins):
                self.n += 1
                ins.then_inc(self.sem, 1)
                self.eng.wait_ge(self.sem, lin(self.n, self.per, self.i))

            def enter(self, i, per):
                self.i, self.per, self.at0 = i, per, self.n

            def leave(self, turns):
                assert self.n - self.at0 == self.per, (self.sem, self.n - self.at0)
                self.n, self.i = self.at0 + turns * self.per, None

        @block.sync
        def _(sp):
            def load(n, i=None):
                slot = n % RING
                if n >= RING:
                    sp.wait_ge(lo_ready, lin(n - RING + 1, RING, i))
                row = n if i is None else n + RING * i
                sp.dma_start(RAW[:, slot, :], stream[bass.ds(row, 1)].rearrange("a p c -> p (a c)"))\
                    .then_inc(raw_loaded[slot], 16)

            sp.dma_start(PRM[:, :], prm).then_inc(prm_loaded[0], 16)
            for g in range(4):
                sp.dma_start(X0[:, 4 * g:4 * g + 4, :], xT[:, 4 * g:4 * g + 4, :]).then_inc(x_loaded[g], 16)
                load(g)
            with sp.Fori(0, N_CHUNK // RING - 1) as i:
                for s in range(RING):
                    load(RING + s, i)
            for g in (0, 2, 1, 3):
                t = slice(4 * g, 4 * g + 4)
                sp.wait_ge(out_ready[g], 1)
                sp.dma_start(outT[:, t, :], XR[:, t, :]).then_inc(out_stored, 16)
            sp.wait_ge(out_stored, 64)

        @block.tensor
        def _(pe):
            mm = nc.tensor.matmul

            def begin(p, step=0, i=None):
                pe.wait_ge(set_free[p % 2], lin(p // 2 + 1, step // 2, i))

            def split(out, whi, wlo, xhi, xlo, start, stop):
                mm(out, whi, xhi, start=start, stop=False, skip_group_check=True)
                mm(out, whi, xlo, start=False, stop=False, skip_group_check=True)
                return mm(out, wlo, xhi, start=False, stop=stop, skip_group_check=True)

            def rows(slot, col, tiles, s, xhi, xlo, first, last, between=None):
                for m in range(tiles):
                    if m == 1 and between is not None:
                        between()
                    w = slice(col + m * P, col + (m + 1) * P)
                    ins = split(DP[s][:, m, :], WH[:, slot, w], WL[:, slot, w], xhi, xlo,
                                first and m % 2 == 0, last and (m % 2 == 1 or m == tiles - 1))
                return ins

            def chunk(n, step, i, kt, s, xs, last_kt, tiles=4, hop=None):
                pe.wait_ge(lo_ready, lin(n + 1, step, i))
                width = 2 if tiles > 2 else 4
                for r in range(width):
                    k = kt + r
                    if k > last_kt:
                        break
                    ins = rows(n % RING, r * CH // width, tiles, s, *xs(k), k == 0, k == last_kt,
                               between=(lambda: hop(0)) if hop is not None and r == 1 else None)
                    if r == width - 1 or k == last_kt:
                        ins.then_inc(chunk_done, 1)
                    if hop is not None and r == 1:
                        hop(1)

            def h(k):
                return HH[:, k, :], HL[:, k, :]

            def chunk_v(n, step, i, kt, s):
                pe.wait_ge(lo_ready, lin(n + 1, step, i))
                slot = n % RING
                for r in range(2):
                    k = kt + r
                    w = slice(r * 512, (r + 1) * 512)
                    for t in range(2):
                        tok = slice(t * P, (t + 1) * P)
                        out = DP[s][:, 2 * t:2 * t + 2, :].rearrange("p a b -> p (a b)")
                        mm(out, HH[:, k, tok], WH[:, slot, w], start=(k == 0), stop=False, skip_group_check=True)
                        mm(out, HL[:, k, tok], WH[:, slot, w], start=False, stop=False, skip_group_check=True)
                        ins = mm(out, HH[:, k, tok], WL[:, slot, w], start=False, stop=(k == DT - 1),
                                 skip_group_check=True)
                ins.then_inc(chunk_done, 1)

            def norm_sum(k, g, sq):
                pe.wait_ge(sq_added, 4 * k + g + 1)
                ins = mm(BK[3][:, 0:T], ONES, sq[:, 4 * g, :], start=(g == 0), stop=(g == 3))
                if g == 3:
                    ins.then_inc(ssq_done, 1)

            def group(parts_ready, k, c):
                if c % 2 == 0:
                    pe.wait_ge(parts_ready, 4 * k + c // 2 + 1)

            pe.wait_ge(prm_loaded[1], 16)
            p = 0
            begin(p)
            for c in range(8):
                group(hl_ready, 0, c)
                chunk(S_MISC + c, 0, None, 2 * c, 0, h, DT - 1, tiles=3)
                if c >= 4:
                    norm_sum(0, c - 4, SQ0)
            p = 1
            with pe.Fori(0, 2) as i:
                for q in range(2):
                    begin(p + q, 2, i)
                    for c in range(8):
                        chunk(S_KR + 8 * q + c, 16, i, 2 * c, (p + q) % 2, h, DT - 1)
            p += 4

            def lora_products(c):
                if c == 0:
                    pe.wait_ge(lora_loaded, 16)
                    pe.wait_ge(misc_act, 3)
                else:
                    pe.wait_ge(lora_read, 4 * c)
                for m in range(4 * c, 4 * c + 4):
                    if m < 16:
                        w, x = LORA[:, m % 2, (m // 2) * P:(m // 2 + 1) * P], MISC[:, 0, :]
                    else:
                        w, x = LORA[:, 2, (m - 16) * P:(m - 15) * P], MISC[:, 2, :]
                    mm(BK[m % 4][:, 0:T], w, x, start=True, stop=True).then_inc(lora_mm, 1)

            def key_norms(b):
                pe.wait_ge(kk_sq, b + 1)
                for j in range(4):
                    ins = mm(BK[j // 2][:, (j % 2) * T:(j % 2 + 1) * T], BLK, T2[:, j, :], start=True, stop=True)
                ins.then_inc(kk_ssq, 1)

            def rope(m):
                if m >= 2:
                    pe.wait_ge(rope_read, m - 1)
                mm(BK[m % 2][:, :], PERM, BR[:, 0, 2 * m:2 * m + 2, :], start=True, stop=True).then_inc(rope_mm, 1)

            vt = [BR[:, b, 8:16, :].rearrange("p (t a) c -> p t (a c)", t=2) for b in range(2)]

            def ret_scores(hd):
                if hd >= 2:
                    pe.wait_ge(sc_read, hd - 1)
                q, k = BR[:, 0, hd, :], BR[:, 0, 4 + hd, :]
                mm(BK[hd % 2][:, 0:T], k[:, 0:P], q, start=True, stop=True, skip_group_check=True)
                mm(BK[hd % 2][:, T:T + P], k[:, P:T], q[:, P:T], start=False, stop=True,
                   skip_group_check=True).then_inc(sc_mm, 1)

            def ret_out(hd):
                pe.wait_ge(sc_read, hd + 1)
                if hd >= 2:
                    pe.wait_ge(ov_read, hd - 1)
                for b in range(2):
                    v = slice(hd * DV + b * P, hd * DV + (b + 1) * P)
                    o = BK[2 + hd % 2]
                    mm(o[:, b * T:(b + 1) * T], vt[0][:, 0, v], SR[:, hd % 2, 0:T], start=(b == 0), stop=False,
                       skip_group_check=True)
                    ins = mm(o[:, b * T + P:(b + 1) * T], vt[0][:, 1, v], SR[:, hd % 2, T:T + P], start=False,
                             stop=(b == 1), skip_group_check=True)
                ins.then_inc(ov_mm, 1)

            def head_norm_sum(b):
                pe.wait_ge(on_added, b + 1)
                for hd in range(HEADS):
                    ins = mm(BK[hd // 2][:, (hd % 2) * T:(hd % 2 + 1) * T], ONES, BR[:, b, 8 + hd, :],
                             start=(hd % 2 == 0), stop=True, skip_group_check=True)
                ins.then_inc(on_ssq, 1)

            def gla_scores(hd):
                if hd >= 1:
                    pe.wait_ge(sc_read, 4 + hd)
                    pe.wait_ge(gkt_read, hd)
                q, k = BR[:, 1, hd, :], BR[:, 1, 4 + hd, :]
                for c in range(NC):
                    t = slice(c * CL, (c + 1) * CL)
                    ins = mm(BK[0][:, t], k[:, t], q[:, t], start=(c == 0), stop=(c == 1), skip_group_check=True)
                ins.then_inc(sc_mm, 1)
                nc.tensor.transpose(BK[1][:, 0:P], k[:, 0:P], IDENT).then_inc(gkt_mm, 1)

            def gla_state(hd):
                pe.wait_ge(gkt_read, hd + 1)
                mm(BK[2][:, 0:DV], GKT[:, hd % 2, :], vt[1][:, 0, hd * DV:(hd + 1) * DV], start=True, stop=True)\
                    .then_inc(gs_mm, 1)

            def gla_out(hd):
                pe.wait_ge(sc_read, 4 + hd + 1)
                pe.wait_ge(gs_read, hd + 1)
                pe.wait_ge(ov_read, 4 + hd)
                for b in range(2):
                    v = slice(hd * DV + b * P, hd * DV + (b + 1) * P)
                    o = BK[3][:, b * T:(b + 1) * T]
                    mm(o[:, 0:P], vt[1][:, 0, v], GSC[:, hd % 2, 0, :], start=(b == 0), stop=False,
                       skip_group_check=True)
                    mm(o[:, P:T], vt[1][:, 1, v], GSC[:, hd % 2, 1, :], start=False, stop=False,
                       skip_group_check=True)
                    ins = mm(o[:, P:T], GS[:, hd % 2, b * P:(b + 1) * P], BR[:, 1, hd, P:T], start=False,
                             stop=(b == 1), skip_group_check=True)
                ins.then_inc(ov_mm, 1)

            def side(b, q, c):
                if b == 0:
                    if q == 0 and c < 5:
                        lora_products(c)
                    elif (q, c) == (0, 6):
                        pe.wait_ge(lora_read, 20)
                        key_norms(0)
                    elif q == 2 and c > 4:
                        if c == 5:
                            panel_read(pe, p - 2)
                            panel_read(pe, p - 1)
                            pe.wait_ge(kk_root, 2)
                        rope(c - 5)
                    elif (q, c) == (3, 0):
                        rope(3)
                    elif (q, c) in ((3, 2), (3, 4)):
                        pe.wait_ge(rope_done, 4)
                        ret_scores((c - 2) // 2)
                    elif q == 4 and c % 2:
                        if c == 1:
                            panel_read(pe, p - 2)
                            panel_read(pe, p - 1)
                        ret_out(c // 2)
                        if c < 4:
                            ret_scores(2 + c // 2)
                    elif (q, c) == (5, 3):
                        head_norm_sum(0)
                else:
                    if (q, c) == (0, 5):
                        pe.wait_ge(on_root, 2)
                        key_norms(1)
                    elif q == 4 and c % 2 == 0:
                        if c == 0:
                            pe.wait_ge(gqk, 1)
                            pe.wait_ge(kk_root, 4)
                            pe.wait_ge(ov_read, 4)
                            panel_read(pe, p - 2)
                            panel_read(pe, p - 1)
                        else:
                            gla_out(c // 2 - 1)
                        gla_scores(c // 2)
                    elif q == 4:
                        gla_state(c // 2)
                    elif (q, c) == (5, 0):
                        gla_out(HEADS - 1)
                    elif (q, c) == (5, 3):
                        head_norm_sum(1)

            for b in range(2):
                for q in range(6 + 2 * b):
                    begin(p)
                    for c in range(8):
                        n = S_QKVG + 48 * b + 8 * q + c
                        if q in (2, 3):
                            chunk_v(n, 0, None, 2 * c, p % 2)
                        else:
                            if (b, q) == (0, 0):
                                group(hl_ready, 1, c)
                            chunk(n, 0, None, 2 * c, p % 2, h, DT - 1)
                        side(b, q, c)
                    p += 1

            count_reg = pe.alloc_register("count")
            for b in range(2):
                pe.wait_ge(op_lo, b + 1)
                if b == 0:
                    pe.wait_ge(op_lo, 2)
                    pe.wait_ge(zeroed, 8)
                base = S_GB + 48 * b
                with pe.Fori(0, 4) as i:
                    def rank(value, per=1):
                        return lin(per * 4 * b + value, per, i)

                    def grams(which):
                        x, done, banks = ((BP, bgram, (0, 1)), (KP, kgram, (2, 3)))[which]
                        pe.wait_ge(staged, rank(STAGED, STAGED))
                        pe.wait_ge((bonus_done, var_read)[which], rank(1))
                        for c in range(NC):
                            for e in range(2):
                                ins = mm(BK[banks[c]][:, e * 2 * CL:(e + 1) * 2 * CL],
                                         x[:, e, c * CL:(c + 1) * CL], AR[:, c, :, :], start=(e == 0),
                                         stop=(e == 1), skip_group_check=True)
                        ins.then_inc(done, 1)

                    def tokens():
                        pe.wait_ge(kgram_read, rank(1))
                        for c in range(NC):
                            nc.tensor.transpose(BK[2][:, c * P:(c + 1) * P], VS[:, c * CL:(c + 1) * CL], IDENT)
                        nc.tensor.transpose(BK[2][:, 2 * P:3 * P], BS[:, 0:CL], IDENT)
                        nc.tensor.transpose(BK[2][:, 3 * P:4 * P], KS[:, 0:CL], IDENT).then_inc(vt_mm, 1)

                    def zeroed_wait(s, count):
                        pe.reg_mov(count_reg, count)
                        pe.wait_ge(zeroed, 8)
                        pe.wait_ge(s, count_reg)

                    def grow_a(lv):
                        if lv == 1:
                            pe.wait_ge(t_start, rank(1))
                        else:
                            zeroed_wait(t_grown, rank(lv - 1, LEVELS - 1))
                        for u in range(4):
                            if lv == LEVELS - 1:
                                ins = mm(BK[1][64:P, u * 64:(u + 1) * 64], XT[0:64, u, 64:P], TM[0:64, u, 0:64],
                                         start=(u == 0), stop=(u == 3), skip_group_check=True)
                            elif lv > IN_SQUARE:
                                for j in range(2):
                                    early, late = sides(j)
                                    ins = mm(BK[1][late, 32 * u:32 * u + 32], XT[:, u, late], TM[:, u, early],
                                             start=(u == 0), stop=(u == 3), skip_group_check=True)
                            else:
                                ins = mm(packed(BK[1], lv, u), XT[:, u, :], half(TM[:, u, :], lv, 0), start=(u == 0),
                                         stop=(u == 3), skip_group_check=True)
                        ins.then_inc(p1_mm, 1)

                    def grow_b(lv):
                        if lv == 1:
                            pe.wait_ge(vt_read, rank(1))
                        zeroed_wait(p1_read, rank(lv, LEVELS - 1))
                        if lv == IN_SQUARE + 1:
                            for u in range(4):
                                for j in range(2):
                                    early, late = sides(j)
                                    mm(BK[2][late, 32 * u:32 * u + 32], ZM[:, u, late], P1S[:, u, early],
                                       start=(u == 0), stop=(u == 3), skip_group_check=True)
                        for u in range(4):
                            if lv == LEVELS - 1:
                                ins = mm(BK[3][0:64, u * 64:(u + 1) * 64], P1S[64:P, u, 0:64], ZM[64:P, u, 64:P],
                                         start=(u == 0), stop=(u == 3), skip_group_check=True)
                            elif lv > IN_SQUARE:
                                for j in range(2):
                                    early, late = sides(j)
                                    ins = mm(BK[3][early, 32 * u:32 * u + 32], P1S[:, u, early], ZM[:, u, late],
                                             start=(u == 0), stop=(u == 3), skip_group_check=True)
                            else:
                                ins = mm(packed(BK[3], lv, u), P1S[:, u, :], half(ZM[:, u, :], lv, 1), start=(u == 0),
                                         stop=(u == 3), skip_group_check=True)
                        ins.then_inc(delta_mm, 1)

                    def vh(c, e):
                        return VP[:, c, 3 * e, :]

                    def rhs(c):
                        if c == 0:
                            pe.wait_ge(vt_read, rank(1))
                            pe.wait_ge(kgram_read, rank(1))
                        else:
                            pe.wait_ge(s_read, rank(1))
                            mm(BK[0][:, 0:P], AR[:, 1, 0, :], SB[:, :], start=True, stop=False,
                               skip_group_check=True)
                        for e in range(2):
                            ins = mm(BK[0][:, e * 64:(e + 1) * 64], LAK[:, 2 * c + e, :], vh(c, e),
                                     start=(c == 0 and e == 0), stop=(e == 1), skip_group_check=True)
                        ins.then_inc(rhs_mm, 1)

                    def solve(c):
                        pe.wait_ge(rhs_read, rank(c + 1, 2))
                        pe.wait_ge(t_grown, rank(LEVELS - 1, LEVELS - 1))
                        for e in range(2):
                            ins = mm(BK[1][:, e * 64:(e + 1) * 64], ZM[:, 2 * c + e, :], RH[:, e * 64:(e + 1) * 64],
                                     start=(e == 0), stop=(e == 1), skip_group_check=True)
                        ins.then_inc(u_mm, 1)

                    def state():
                        pe.wait_ge(u_read, rank(1, 2))
                        mm(BK[2][:, 0:P], BKT[:, 0, :], UP[:, 0, 0:4:3, :], start=True, stop=False)
                        mm(BK[2][:, 0:P], BKT[:, 1, :], VP[:, 0, 0:4:3, :], start=False, stop=True).then_inc(s_mm, 1)

                    def outputs(c):
                        pe.wait_ge(u_read, rank(c + 1, 2))
                        t = slice(c * CL, (c + 1) * CL)
                        if c == 1:
                            mm(BK[3][:, t], SB[:, :], AR[:, 1, 1, :], start=False, stop=False,
                               skip_group_check=True)
                        for e in range(2):
                            mm(BK[3][:, t], UP[:, c, 2 * e:2 * e + 2, :], GRB[:, 2 * c + e, :],
                               start=(c == 0 and e == 0), stop=False, skip_group_check=True)
                            ins = mm(BK[3][:, t], VP[:, c, 2 * e:2 * e + 2, :], GRK[:, 2 * c + e, :], start=False,
                                     stop=(e == 1), skip_group_check=True)
                        if c == 1:
                            ins.then_inc(y_mm, 1)

                    def means():
                        pe.wait_ge(y_read, rank(1))
                        pe.wait_ge(rk_staged, rank(3, 3))
                        mm(BK[0][:, 0:T], BLK, YS[:, :], start=True, stop=True)
                        mm(BK[1][:, 0:T], BLK, PR[:, :], start=True, stop=True).then_inc(mean_mm, 1)

                    def variances():
                        pe.wait_ge(var_sq, rank(1))
                        mm(BK[2][:, 0:T], BLK, SQS[:, :], start=True, stop=True).then_inc(var_mm, 1)

                    def hop(s):
                        if s == 0:
                            grams(0)
                        elif s == 1:
                            grams(1)
                        elif s == 3:
                            tokens()
                        elif 4 <= s < 16:
                            (grow_a, grow_b)[s % 2]((s - 4) // 2 + 1)
                            if s == 5:
                                rhs(0)
                        elif s == 16:
                            solve(0)
                        elif s == 17:
                            state()
                            outputs(0)
                        elif s == 18:
                            rhs(1)
                        elif s == 19:
                            solve(1)
                        elif s == 20:
                            outputs(1)
                        elif s == 21:
                            means()
                        elif s == 23:
                            variances()

                    begin(p, 2, i)
                    for c in range(8):
                        chunk(base + c, 12, i, 2 * c, p % 2, h, DT - 1, hop=lambda r: hop(2 * c + r))
                    begin(p + 1, 2, i)
                    for c in range(4):
                        chunk(base + 8 + c, 12, i, 2 * c, (p + 1) % 2,
                              lambda k: [OP[b][:, j, k // 2 + 4 * (k % 2), :] for j in range(2)], MT - 1,
                              hop=lambda r: hop(16 + 2 * c + r))
                p += 8

            pe.wait_ge(g2_loaded, 16)
            pe.wait_ge(var_read, 9)
            pe.wait_ge(bonus_done, 9)
            for q in range(4):
                begin(p)
                for c in range(8):
                    chunk(S_RW + 8 * q + c, 0, None, 2 * c, p % 2, h, DT - 1)
                    if q == 0:
                        if c >= 4:
                            pe.wait_ge(g_read, c - 3)
                        w = slice(c * P, (c + 1) * P)
                        mm(BK[c % 4][:, 0:T], G2[:, 0, w], MISC[:, 1, :], start=True, stop=False)
                        mm(BK[c % 4][:, 0:T], G2[:, 1, w], MISC[:, 2, :], start=False, stop=True).then_inc(g_mm, 1)
                p += 1
            pe.wait_ge(orw_lo, 1)
            with pe.Fori(0, 2) as i:
                for q in range(2):
                    begin(p + q, 2, i)
                    for c in range(4):
                        chunk(S_RW + 32 + 4 * q + c, 8, i, 2 * c, (p + q) % 2,
                              lambda k: (OPR[0][:, k, :], OPR[1][:, k, :]), MT - 1)
            p += 4
            with pe.Fori(0, 2) as i:
                for q in range(2):
                    begin(p + q, 2, i)
                    for c in range(8):
                        group(mg_lo, 0, c)
                        chunk(S_O + 8 * q + c, 16, i, 2 * c, (p + q) % 2, h, DT - 1)
            p += 4
            begin(p)
            for c in range(8):
                group(hl_ready, 2, c)
                chunk(S_UP + c, 0, None, 2 * c, p % 2, h, DT - 1)
                if 1 <= c < 4 or c == 7:
                    norm_sum(1, min(c - 1, 3), SQ)
            p += 1
            with pe.Fori(0, 10) as i:
                for q in range(2):
                    begin(p + q, 2, i)
                    for c in range(8):
                        chunk(S_UP + 8 + 8 * q + c, 16, i, 2 * c, (p + q) % 2, h, DT - 1)
            p += 20
            begin(p)
            for c in range(4):
                chunk(S_UP + 168 + c, 0, None, 4 * c, p % 2, h, DT - 1, tiles=2)
            p += 1
            with pe.Fori(0, 2) as i:
                for q in range(2):
                    begin(p + q, 2, i)
                    for c in range(22):
                        pe.wait_ge(act_lo, c + 1)
                        chunk(S_DOWN + 22 * q + c, 44, i, 2 * c, (p + q) % 2,
                              lambda k: (AH[:, k, :], AL[:, k, :]), FT - 1)
            p += 4
            pe.wait_ge(p_lo, 1)
            for q in range(4):
                begin(p)
                chunk(S_PLE + q, 0, None, 0, p % 2, lambda k: (PXH[:, k, :], PXL[:, k, :]), 1)
                if q < 3:
                    norm_sum(2, q, SQ)
                p += 1
            for q in range(4):
                begin(p)
                for c in range(8):
                    if q == 0:
                        group(hl_ready, 3, c)
                    chunk(S_PLE + 4 + 8 * q + c, 0, None, 2 * c, p % 2, h, DT - 1)
                    if (q, c) == (0, 7):
                        norm_sum(2, 3, SQ)
                    elif q and c == 6:
                        pe.wait_ge(rs_root, 3)
                        norm_sum(3, q - 1, SQ)
                p += 1
            norm_sum(3, 3, SQ)

        @block.scalar
        def _(act):
            a = nc.scalar.activation
            steps = Steps(act, act_step)

            def hi(n, step=0, i=None):
                slot = n % RING
                act.wait_ge(raw_loaded[slot], lin(16 * (n // RING + 1), 16 * step // RING, i))
                if n >= RING:
                    act.wait_ge(chunk_done, lin(n - RING + 1, step, i))
                a(WH[:, slot, :], RAW[:, slot, :], ACT.Copy).then_inc(hi_ready, 1)

            def tick(n, step=0, i=None):
                if n + 3 < N_CHUNK:
                    hi(n + 3, step, i)

            def panel_end(n, step=0, i=None):
                act.wait_ge(chunk_done, lin(n + 1, step, i))

            def root(k, rs):
                act.wait_ge(ssq_done, k + 1)
                a(rs[:, :], BK[3][:, 0:T], ACT.Sqrt, scale=1.0 / D, bias=EPSC).then_inc(rs_root, 1)

            def h_hi(k, g, sq):
                act.wait_ge(h_ready, 4 * k + g + 1)
                a(HH[:, 4 * g:4 * g + 4, :], sq[:, 4 * g:4 * g + 4, :], ACT.Copy).then_inc(hh_ready, 1)

            def squares(x, sq, g):
                a(sq[:, 4 * g:4 * g + 4, :], x[:, 4 * g:4 * g + 4, :], ACT.Square).then_inc(sq_ready, 1)

            for g in range(4):
                h_hi(0, g, SQ0)
                if g < 3:
                    hi(g)
            p = 0
            for c in range(8):
                tick(S_MISC + c)
                if c < 4:
                    act.wait_ge(hl_ready, c + 1)
                    squares(X0, SQ0, c)
            act.wait_ge(set_free[1], 1)
            root(0, RSTD)
            act.wait_ge(trig_in, 2)
            a(SIN[:, :], RA[:, :], ACT.Sin).then_inc(trig_out, 1)
            a(COS[:, :], RB[:, :], ACT.Sin).then_inc(trig_out, 1)
            p = 1
            for q in range(4):
                for c in range(8):
                    tick(S_KR + 8 * q + c)
                    if (q, c) == (0, 4):
                        act.wait_ge(shift_out, 1)
                        a(MISC[0:64, 0, :], MISC[0:64, 0, :], ACT.Tanh).then_inc(misc_act, 1)
                    elif (q, c) == (0, 5):
                        a(MISC[:, 1, :], MISC[:, 1, :], ACT.Sigmoid).then_inc(misc_act, 1)
                        a(MISC[0:32, 2, :], MISC[0:32, 2, :], ACT.Sigmoid).then_inc(misc_act, 1)
                    elif q == 3 and c in (2, 4, 6):
                        act.wait_ge(chunk_done, S_KR + 24 + c)
                        h_hi(1, c // 2 - 1, X0)
            p += 4

            def lora_out(c):
                if c == 0:
                    act.wait_ge(masks_set, 1)
                for m in range(4 * c, 4 * c + 4):
                    act.wait_ge(lora_mm, m + 1)
                    t = m // 2
                    if m < 16:
                        a((RWA, RWB)[m % 2][:, t, :], BK[m % 4][:, 0:T], ACT.Sigmoid,
                          bias=prmc(("w0", "a0")[m % 2], t)).then_inc(lora_read, 1)
                    else:
                        a(LG[:, m - 16, :], BK[m % 4][:, 0:T], ACT.Identity, bias=prmc("bdec", m - 16))\
                            .then_inc(lora_read, 1)

            def log_sigmoid(part):
                if part == 0:
                    act.wait_ge(lora_read, 20)
                    steps.link(a(LT1[:, :, :], LG[:, :, :], ACT.Abs))
                elif part == 1:
                    steps.link(a(LT1[:, :, :], LT1[:, :, :], ACT.Exp, scale=-1.0))
                else:
                    a(LT1[:, :, :], LT1[:, :, :], ACT.Ln, bias=1.0).then_inc(log_sp, 1)

            def key_roots(b):
                act.wait_ge(kk_ssq, b + 1)
                for j in range(2):
                    a(T2[:, 2 * j:2 * j + 2, :].rearrange("p a b -> p (a b)"), BK[j][:, :], ACT.Sqrt)\
                        .then_inc(kk_root, 1)

            def decays(b, part):
                t = slice(4 * b, 4 * b + 4)
                if part == 0:
                    act.wait_ge(dec_in, b + 1)
                    a(T4[:, :, :], T4[:, :, :], ACT.Exp, scale=-C_DECAY).then_inc(dec_exp, 1)
                    a(RWA[:, t, :], T3[:, :, :], ACT.Exp, scale=-C_DECAY).then_inc(dec_exp, 1)
                else:
                    act.wait_ge(dec_exp, 4 * b + 2)
                    a(T3[:, :, :], T3[:, :, :], ACT.Exp, scale=C_DECAY).then_inc(dec_exp, 1)
                    a(ES[:, t], MD[:, :], ACT.Exp, scale=-C_DECAY).then_inc(dec_exp, 1)

            def o_read(b, hd):
                act.wait_ge(ov_mm, 4 * b + hd + 1)
                bank = BK[3] if b else BK[2 + hd % 2]
                a(BR[:, b, hd:8:4, :], bank[:, :].rearrange("p (e t) -> p e t", e=2), ACT.Copy).then_inc(ov_read, 1)

            def head_squares(b):
                act.wait_ge(ov_read, 4 * b + 4)
                a(BR[:, b, 8:16, :], BR[:, b, 0:8, :], ACT.Square).then_inc(on_sq, 1)

            def head_roots(b):
                act.wait_ge(on_ssq, b + 1)
                for j in range(2):
                    a(RS4[:, 2 * j:2 * j + 2, :].rearrange("p a b -> p (a b)"), BK[j][:, :], ACT.Sqrt,
                      scale=1.0 / DV, bias=EPSC).then_inc(on_root, 1)

            def output_hi(b):
                act.wait_ge(o_final, b + 1)
                a(OP[b][:, 0, :, :], BR[:, b, 0:8, :], ACT.Copy).then_inc(op_hi, 1)

            def side(b, q, c):
                if b == 0:
                    if q == 0 and c < 5:
                        if c == 0:
                            act.wait_ge(chunk_done, S_QKVG)
                            h_hi(1, 3, X0)
                        elif c == 4:
                            act.wait_ge(hl_ready, 8)
                        lora_out(c)
                    elif (q, c) == (0, 7):
                        key_roots(0)
                    elif q == 1 and c < 2:
                        decays(0, c)
                    elif q == 1 and 4 <= c < 7:
                        log_sigmoid(c - 4)
                    elif q == 4 and c in (2, 4, 6):
                        o_read(0, c // 2 - 1)
                    elif (q, c) == (5, 0):
                        o_read(0, 3)
                    elif (q, c) == (5, 1):
                        head_squares(0)
                    elif (q, c) == (5, 4):
                        head_roots(0)
                else:
                    if (q, c) == (0, 6):
                        key_roots(1)
                    elif q == 1 and 1 <= c < 3:
                        decays(1, c - 1)
                    elif (q, c) == (1, 6):
                        output_hi(0)
                    elif (q, c) == (2, 7):
                        act.wait_ge(gdec_in, 1)
                        a(GI[:, :, :], GD[:, :, :], ACT.Exp, scale=1.0 / 16).then_inc(gdec_exp, 1)
                        a(GD[:, :, :], GD[:, :, :], ACT.Exp, scale=-1.0 / 16).then_inc(gdec_exp, 1)
                        a(GES[:, :], GMD[:, :], ACT.Exp, scale=1.0 / 16).then_inc(gdec_exp, 1)
                    elif q == 4 and c % 2 == 0:
                        hd = c // 2
                        act.wait_ge(gkt_mm, hd + 1)
                        a(GKT[:, hd % 2, :], BK[1][:, 0:P], ACT.Copy).then_inc(gkt_read, 1)
                        if hd:
                            o_read(1, hd - 1)
                    elif q == 4:
                        hd = c // 2
                        act.wait_ge(gs_mm, hd + 1)
                        act.wait_ge(gdec_exp, 3)
                        a(GS[:, hd % 2, :], BK[2][:, 0:DV], ACT.Copy, scale=GES[:, hd:hd + 1]).then_inc(gs_read, 1)
                    elif (q, c) == (5, 0):
                        o_read(1, 3)
                        head_squares(1)
                    elif (q, c) == (5, 3):
                        head_roots(1)
                    elif (q, c) == (6, 3):
                        output_hi(1)

            for b in range(2):
                for q in range(6 + 2 * b):
                    s = p % 2
                    for c in range(8):
                        tick(S_QKVG + 48 * b + 8 * q + c)
                        side(b, q, c)
                    panel_end(S_QKVG + 48 * b + 8 * q + 7)
                    if q < 2:
                        a(BR[:, b, 4 * q:4 * q + 4, :], DP[s][:, :, :], ACT.Copy).then_inc(set_free[s], 1)
                    elif q < 4:
                        for t in range(2):
                            lo_t = 8 + 4 * t + 2 * (q - 2)
                            ins = a(BR[:, b, lo_t:lo_t + 2, :], DP[s][:, 2 * t:2 * t + 2, :], ACT.Copy)
                        ins.then_inc(set_free[s], 1)
                    elif q < 6:
                        if q == 4:
                            act.wait_ge(shift_out, 5)
                        else:
                            panel_read(act, p - 1)
                        a(SG[:, :, :], DP[s][:, :, :], ACT.Sigmoid).then_inc(g_sig, 1)
                    else:
                        act.wait_ge(shift_out, q)
                        a(UBUF[:, :, 1:T + 1], DP[s][:, :, :], ACT.Copy).then_inc(set_free[s], 1)
                    p += 1
            act.wait_ge(shift_out, 8)
            for b in range(2):
                base = S_GB + 48 * b
                with act.Fori(0, 4) as i:
                    def rank(value, per=1):
                        return lin(per * 4 * b + value, per, i)

                    for k in range(12):
                        tick(base + k, 12, i)
                        if k == 1:
                            act.wait_ge(vt_mm, rank(2))
                            a(VP[:, :, 0:4:3, :], BK[2][:, 0:2 * P].rearrange("p (c e q) -> p c e q", c=2, e=2),
                              ACT.Copy)
                            a(BKT[:, :, :].rearrange("p a b -> p (a b)"), BK[2][:, 2 * P:], ACT.Copy)\
                                .then_inc(vt_read, 1)
                        elif 2 <= k < 8:
                            act.wait_ge(p1_mm, rank(k - 1, LEVELS - 1))
                            if k == LEVELS:
                                a(P1S[64:P, :, 0:64], BK[1][64:P, 0:2 * P].rearrange("p (u t) -> p u t", u=4),
                                  ACT.Copy).then_inc(p1_read, 1)
                            elif k > IN_SQUARE + 1:
                                for j in range(2):
                                    early, late = sides(j)
                                    ins = a(P1S[late, :, early],
                                            BK[1][late, 0:P].rearrange("p (u t) -> p u t", u=4), ACT.Copy)
                                ins.then_inc(p1_read, 1)
                            else:
                                a(half(P1S[:, :, :], k - 1, 0), packed(BK[1], k - 1), ACT.Copy).then_inc(p1_read, 1)
                        if k in (2, 9):
                            act.wait_ge(rhs_mm, rank(1 + k // 9, 2))
                            a(RH[:, :], BK[0][:, 0:P], ACT.Copy).then_inc(rhs_read, 1)
                        if k in (8, 9):
                            c = k - 8
                            act.wait_ge(u_mm, rank(c + 1, 2))
                            a(UP[:, c, 0:4:3, :], BK[1][:, 0:P].rearrange("p (e q) -> p e q", e=2), ACT.Copy)\
                                .then_inc(u_read, 1)
                        if k == 10:
                            act.wait_ge(y_mm, rank(2))
                            a(YS[:, :], BK[3][:, 0:T], ACT.Copy).then_inc(y_read, 1)
                        if k == 11:
                            act.wait_ge(centred, rank(1))
                            a(SQS[:, :], KRV[:, bass.ds(MT + 4 * b + i, 1), :].rearrange("p a b -> p (a b)"),
                              ACT.Square).then_inc(var_sq, 1)
                            act.wait_ge(var_mm, rank(1))
                            a(RWA[:, bass.ds(4 * b + i, 1), :].rearrange("p a b -> p (a b)"), BK[2][:, 0:T],
                              ACT.Copy).then_inc(var_read, 1)
                        if k == 7:
                            panel_end(base + 7, 12, i)
                            if b == 0:
                                a(MG[:, bass.ds(4 * i, 4), :], DP[p % 2][:, :, :], ACT.Sigmoid)\
                                    .then_inc(set_free[p % 2], 1)
                            else:
                                act.wait_ge(merged, lin(1, 1, i))
                                a(GT1[:, :, :], DP[p % 2][:, :, :], ACT.Sigmoid).then_inc(set_free[p % 2], 1)
                p += 8
            act.wait_ge(var_read, 9)
            a(RT8[:, :, :], RWA[:, :, :], ACT.Sqrt, scale=1.0 / 64, bias=GNEPSC).then_inc(gn_root, 1)
            act.wait_ge(merged, 5)
            for q in range(4):
                for c in range(8):
                    tick(S_RW + 8 * q + c)
                    if q == 0:
                        act.wait_ge(g_mm, c + 1)
                        a(GG[:, c, :], BK[c % 4][:, 0:T], ACT.Copy).then_inc(g_read, 1)
                    elif (q, c) == (1, 2):
                        act.wait_ge(orw, 1)
                        a(OPR[0][:, :, :], KRV[:, MT:2 * MT, :], ACT.Copy).then_inc(orw, 1)
                panel_end(S_RW + 8 * q + 7)
                a(GB[:, 4 * q:4 * q + 4, :], DP[p % 2][:, :, :], ACT.Sigmoid).then_inc(set_free[p % 2], 1)
                p += 1
            for q in range(4):
                for c in range(4):
                    tick(S_RW + 32 + 4 * q + c)
                act.wait_ge(merged, 6 + q)
                a(HH[:, 4 * q:4 * q + 4, :], MG[:, 4 * q:4 * q + 4, :], ACT.Copy).then_inc(mg_hi, 1)
                p += 1
            for q in range(4):
                for c in range(8):
                    tick(S_O + 8 * q + c)
                    if q == 3 and c in (2, 4, 6):
                        act.wait_ge(chunk_done, S_O + 24 + c)
                        h_hi(2, c // 2 - 1, SQ)
                    elif q == 3 and c in (3, 5, 7):
                        act.wait_ge(hl_ready, 8 + c // 2)
                        squares(XR, SQ, c // 2 - 1)
                p += 1

            def gelu(w, i):
                act.wait_ge(conv_done, lin(w + 1, 2, i))
                tiles = 1 if w == 21 else 2
                a(GE[:, 0:tiles, :], CV[:, 0:tiles, :], ACT.Gelu_apprx_tanh).then_inc(gelu_done, 1)

            def act_high(w, i, pc):
                tiles = 1 if w == 21 else 2
                act.wait_ge(set_free[pc % 2], lin(pc // 2 + 2, 1, i))
                tile = 2 * w if i is None else 2 * w + 4 * i
                a(AH[:, bass.ds(tile, tiles), :], AV[:, 0:tiles, :], ACT.Copy).then_inc(act_hi, 1)

            for c in range(8):
                tick(S_UP + c)
                if c == 0:
                    act.wait_ge(chunk_done, S_UP)
                    h_hi(2, 3, SQ)
                elif c == 2:
                    act.wait_ge(hl_ready, 12)
                    squares(XR, SQ, 3)
            root(1, RS)
            with act.Fori(0, 10) as i:
                for q in range(2):
                    for c in range(8):
                        tick(S_UP + 8 + 8 * q + c, 16, i)
                        if c == 1:
                            gelu(q, i)
                        elif c == 3:
                            act_high(q, i, p + q)
            p += 20
            for c in range(4):
                tick(S_UP + 168 + c)
                if c == 1:
                    gelu(20, None)
                elif c == 3:
                    act_high(20, None, p)
            p += 1
            for q in range(4):
                for c in range(22):
                    tick(S_DOWN + 22 * q + c)
                    if (q, c) == (0, 2):
                        gelu(21, None)
                    elif (q, c) == (0, 4):
                        act_high(21, None, p)
                    elif (q, c) == (0, 14):
                        act.wait_ge(p_loaded, 16)
                        a(PXH[:, :, :], PX[:, :, :], ACT.Copy).then_inc(p_hi, 1)
                    elif q and c == 2:
                        h_hi(3, q - 1, SQ)
                    elif q and c == 4:
                        act.wait_ge(hl_ready, 12 + q)
                        squares(XR, SQ, q - 1)
            p += 5
            for q in range(4):
                tick(S_PLE + q)
                if q == 0:
                    h_hi(3, 3, SQ)
                elif q == 2:
                    act.wait_ge(hl_ready, 16)
                    squares(XR, SQ, 3)
                panel_end(S_PLE + q)
                a(PG[:, 4 * q:4 * q + 4, :], DP[p % 2][:, :, :], ACT.Copy).then_inc(set_free[p % 2], 1)
                p += 1

            def ple_sigmoid(pc):
                panel_read(act, pc)
                a(GP[:, :, :], GP[:, :, :], ACT.Sigmoid).then_inc(ple_sig, 1)

            for q in range(4):
                for c in range(8):
                    tick(S_PLE + 4 + 8 * q + c)
                    if q and c == 1:
                        ple_sigmoid(p - 1)
                    elif q and c == 4:
                        act.wait_ge(ple_used, q)
                        squares(XR, SQ, q - 1)
                if q == 0:
                    root(2, RS)
                p += 1
            ple_sigmoid(p - 1)
            act.wait_ge(ple_used, 4)
            squares(XR, SQ, 3)
            root(3, RS)

        @block.vector
        def _(dve):
            v = nc.vector
            steps = Steps(dve, dve_step)
            link = steps.link

            def lo(n, step=0, i=None):
                slot = n % RING
                dve.wait_ge(hi_ready, lin(n + 1, step, i))
                v.tensor_tensor(WL[:, slot, :], RAW[:, slot, :], WH[:, slot, :].bitcast(F32), ALU.subtract)\
                    .then_inc(lo_ready, 1)

            def tick(n, step=0, i=None):
                if n + 3 < N_CHUNK:
                    lo(n + 3, step, i)

            def h_lo(g, k, sq):
                dve.wait_ge(hh_ready, 4 * k + g + 1)
                t = slice(4 * g, 4 * g + 4)
                v.tensor_tensor(HL[:, t, :], sq[:, t, :], HH[:, t, :].bitcast(F32), ALU.subtract)\
                    .then_inc(hl_ready, 1)

            def reciprocal_root(k, rs):
                dve.wait_ge(rs_root, k + 1)
                link(v.reciprocal(rs[:, :], rs[:, :]))

            def over_norm(x, out, rs, gain, g):
                for t in range(4 * g, 4 * g + 4):
                    ins = v.scalar_tensor_tensor(out=out[:, t, :], in0=x[:, t, :], scalar=prmc(gain, t),
                                                 in1=rs[:, :], op0=ALU.mult, op1=ALU.mult)
                ins.then_inc(h_ready, 1)

            def times_gain(x, out, gain, g):
                t = slice(4 * g, 4 * g + 4)
                at = COL[gain][0] + 4 * g
                v.tensor_tensor(out[:, t, :], x[:, t, :], bcast(PRM[:, at:at + 4], T), ALU.mult).then_inc(h_ready, 1)

            def norm_n(rs, n):
                return rs[:, :].unsqueeze(1).to_broadcast([P, n, T])

            def residual(p, q, gain):
                t = slice(4 * q, 4 * q + 4)
                v.tensor_tensor(XR[:, t, :], DP[p % 2][:, :, :], XR[:, t, :], ALU.add).then_inc(set_free[p % 2], 1)
                panel_read(dve, p)
                times_gain(XR, SQ, gain, q)

            v.memset(EPSC, EPS)
            v.memset(GNEPSC, GN_EPS)
            link(v.memset(ROW1[:, :], 1.0))
            v.memset(UBUF[:, :, 0:1], 0.0).then_inc(set_free[0], 1)
            v.memset(DBUF[:, :, 0:1], 0.0).then_inc(set_free[1], 1)
            dve.wait_ge(prm_loaded[0], 16)
            for g in range(5):
                if g < 4:
                    dve.wait_ge(x_loaded[g], 16)
                    times_gain(X0, SQ0, "mix", g)
                if g:
                    h_lo(g - 1, 0, SQ0)
                if 1 <= g < 4:
                    lo(g - 1)
            p = 0

            def shift(p, dest, mu, tiles=4, end=None):
                if end is not None:
                    dve.wait_ge(chunk_done, end)
                    v.tensor_tensor(UBUF[:, 0:tiles, 1:T + 1], DP[p % 2][:, 0:tiles, :], norm_n(RSTD, tiles),
                                    ALU.mult)\
                        .then_inc(set_free[p % 2], 1)
                panel_read(dve, p)
                link(v.tensor_tensor(DBUF[:, 0:tiles, :], UBUF[:, 0:tiles, 0:T], UBUF[:, 0:tiles, 1:T + 1],
                                     ALU.subtract))
                for m in range(tiles):
                    ins = v.scalar_tensor_tensor(out=dest(m), in0=DBUF[:, m, :], scalar=mu(m),
                                                 in1=UBUF[:, m, 1:T + 1], op0=ALU.mult, op1=ALU.add)
                ins.then_inc(shift_out, 1)

            two_pi = 2 * math.pi
            magic = 1.5 * 2 ** 23
            c1 = 6.28125
            c2 = float(np.float32(two_pi - c1) - np.float32(two_pi - c1) % np.float32(2.0 ** -19))
            c3 = two_pi - c1 - c2
            lim = 3.1415925

            def trig(part):
                if part == 0:
                    dve.wait_ge(pos_loaded, 16)
                    link(v.tensor_copy(RA[:, :], PI32[:, :]))
                    link(v.tensor_scalar(RA[:, :], RA[:, :], prmc("invf", 0), None, ALU.mult))
                elif part == 1:
                    link(v.tensor_scalar(RB[:, :], RA[:, :], 1 / two_pi, magic, ALU.mult, ALU.add))
                    link(v.tensor_scalar(RB[:, :], RB[:, :], -magic, None, ALU.add))
                elif part == 2:
                    for ck in (c1, c2, c3):
                        link(v.scalar_tensor_tensor(out=RA[:, :], in0=RB[:, :], scalar=-ck, in1=RA[:, :],
                                                    op0=ALU.mult, op1=ALU.add))
                elif part == 3:
                    link(v.tensor_scalar(RB[:, :], RA[:, :], math.pi / 2, None, ALU.add))
                    v.tensor_scalar(RA[:, :], RA[:, :], lim, -lim, ALU.min, ALU.max).then_inc(trig_in, 1)
                    link(v.tensor_scalar(RC[:, :], RB[:, :], math.pi, -two_pi, ALU.is_gt, ALU.mult))
                elif part == 4:
                    link(v.tensor_tensor(RB[:, :], RB[:, :], RC[:, :], ALU.add))
                    v.tensor_scalar(RB[:, :], RB[:, :], lim, -lim, ALU.min, ALU.max).then_inc(trig_in, 1)

            for c in range(8):
                tick(S_MISC + c)
                if c:
                    trig(c - 1)
            reciprocal_root(0, RSTD)
            dve.wait_ge(trig_in, 2)
            shift(0, lambda m: MISC[:, m, :], lambda m: prmc("mu", 24 + m), tiles=3, end=S_KR)
            p = 1
            for q in range(4):
                for c in range(8):
                    tick(S_KR + 8 * q + c)
                    if q == 0 and c % 2:
                        over_norm(X0, X0, RSTD, "mix", c // 2)
                    elif q == 3 and c in (2, 4, 6):
                        h_lo(c // 2 - 1, 1, X0)
                shift(p, lambda m: KRV[:, 4 * q + m, :], lambda m: prmc("mu", 4 * q + m), end=S_KR + 8 * q + 8)
                p += 1

            def prepare(b, step):
                t = slice(4 * b, 4 * b + 4)
                kx, rx, ax, bx = KRV[:, t, :], KRV[:, MT + 4 * b:MT + 4 * b + 4, :], RWA[:, t, :], RWB[:, t, :]

                def chan(name):
                    at = COL[name][0] + 4 * b
                    return bcast(PRM[:, at:at + 4], T)

                if step == 0:
                    dve.wait_ge(shift_out, 5)
                    dve.wait_ge(hl_ready, 8)
                    link(v.tensor_tensor(T1[:, :, :], kx, chan("k_k"), ALU.mult))
                elif step == 1:
                    v.tensor_tensor(T2[:, :, :], T1[:, :, :], T1[:, :, :], ALU.mult).then_inc(kk_sq, 1)
                elif step == 2:
                    dve.wait_ge(lora_read, 8 * b + 8)
                    for m in range(4):
                        for c in range(NC):
                            t = slice(c * CL, (c + 1) * CL)
                            ins = v.tensor_tensor_scan(T4[:, m, t], ROW1[:, t], RWA[:, 4 * b + m, t], 0.0, ALU.mult,
                                                       ALU.add)
                    link(ins)
                elif step == 3:
                    t4 = T4[:, :, :].rearrange("p m (c t) -> p (m c) t", c=NC)
                    link(v.tensor_tensor(T3[:, :, :].rearrange("p m (c t) -> p (m c) t", c=NC), t4,
                                         t4[:, :, 63:64].to_broadcast([P, 4 * NC, CL]), ALU.subtract))
                    link(v.tensor_tensor(MD[:, :], T3[:, :, 127:128].rearrange("p a b -> p (a b)"),
                                         T4[:, :, 191:192].rearrange("p a b -> p (a b)"), ALU.add))
                elif step == 4:
                    v.tensor_tensor(T4[:, :, :], T3[:, :, :], ax, ALU.subtract).then_inc(dec_in, 1)
                elif step < 9:
                    m = step - 5
                    dve.wait_ge(kk_root, 2 * b + 2)
                    link(v.tensor_scalar(T2[:, m, :], T2[:, m, :], 1e-12, None, ALU.max))
                    link(v.reciprocal(T2[:, m, :], T2[:, m, :]))
                elif step == 9:
                    link(v.tensor_tensor(T1[:, :, :], T1[:, :, :], T2[:, :, :], ALU.mult))
                elif step == 10:
                    dve.wait_ge(lora_read, 20)
                    link(v.scalar_tensor_tensor(out=T2[:, :, :], in0=bx, scalar=-1.0, in1=chan("k_a"),
                                                op0=ALU.add, op1=ALU.mult))
                elif step == 11:
                    link(v.scalar_tensor_tensor(out=kx, in0=T2[:, :, :], scalar=1.0, in1=kx,
                                                op0=ALU.add, op1=ALU.mult))
                elif step == 12:
                    link(v.scalar_tensor_tensor(out=T2[:, :, :], in0=T1[:, :, :], scalar=-1.0, in1=bx,
                                                op0=ALU.mult, op1=ALU.mult))
                elif step == 13:
                    dve.wait_ge(dec_exp, 4 * b + 4)
                    link(v.tensor_tensor(rx, rx, ax, ALU.mult))
                elif step == 14:
                    link(v.tensor_tensor(ax, T1[:, :, :], T4[:, :, :], ALU.mult))
                elif step == 15:
                    link(v.tensor_tensor(kx, kx, T3[:, :, :], ALU.mult))
                else:
                    v.tensor_tensor(bx, T2[:, :, :], T3[:, :, :], ALU.mult).then_inc(rw_prep, 1)

            sin2 = SIN[:, :].unsqueeze(1).to_broadcast([P, 2, T])
            cos2 = COS[:, :].unsqueeze(1).to_broadcast([P, 2, T])

            def rope(m):
                x = BR[:, 0, 2 * m:2 * m + 2, :]
                dve.wait_ge(trig_out, 2)
                dve.wait_ge(rope_mm, m + 1)
                v.tensor_tensor(RT[:, :, :], BK[m % 2][:, :].rearrange("p (a b) -> p a b", a=2), sin2, ALU.mult)\
                    .then_inc(rope_read, 1)
                link(v.tensor_tensor(x, x, cos2, ALU.mult))
                dve.wait_ge(rope_read, m + 1)
                v.tensor_tensor(x, x, RT[:, :, :], ALU.add).then_inc(rope_done, 1)
                dve.wait_ge(rope_done, m + 1)

            def ret_weigh(hd):
                dve.wait_ge(dm_loaded, 16)
                dve.wait_ge(sc_mm, hd + 1)
                if hd >= 2:
                    dve.wait_ge(ov_mm, hd - 1)
                v.tensor_tensor(SR[:, hd % 2, :], BK[hd % 2][:, 0:384], DM[:, hd, :], ALU.mult).then_inc(sc_read, 1)

            def gla_mask(hd):
                dve.wait_ge(masks_set, 1)
                dve.wait_ge(sc_mm, 4 + hd + 1)
                if hd >= 2:
                    dve.wait_ge(ov_mm, 4 + hd - 1)
                v.copy_predicated(GSC[:, hd % 2, :, :], mask(1, 2), BK[0][:, 0:T].rearrange("p (c t) -> p c t", c=2))\
                    .then_inc(sc_read, 1)

            def head_recip(b, hd):
                dve.wait_ge(on_root, 2 * b + 2)
                link(v.reciprocal(RS4[:, hd, :], RS4[:, hd, :]))

            def head_scale(b, part):
                if part < 2:
                    o = BR[:, b, 4 * part:4 * part + 4, :]
                    if b == 0:
                        link(v.tensor_tensor(o, o, RS4[:, :, :], ALU.mult))
                    else:
                        link(v.scalar_tensor_tensor(out=o, in0=o, scalar=prmc("gnorm", part), in1=RS4[:, :, :],
                                                    op0=ALU.mult, op1=ALU.mult))
                else:
                    o = BR[:, b, 0:8, :].rearrange("p (e h) t -> p e h t", e=2)
                    v.tensor_tensor(o, o, BR[:, b, 16:24, :].rearrange("p (h e) t -> p e h t", e=2), ALU.mult)\
                        .then_inc(o_final, 1)

            def output_lo(b):
                dve.wait_ge(op_hi, b + 1)
                v.tensor_tensor(OP[b][:, 1, :, :], BR[:, b, 0:8, :], OP[b][:, 0, :, :].bitcast(F32), ALU.subtract)\
                    .then_inc(op_lo, 1)

            slots = ((1, 2, 4, 5, 6, 8, 9, 10, 11, 12, 13, 14, 15, 16, 17, 18, 19),
                     (3, 4, 5, 6, 7, 8, 9, 10, 11, 12, 13, 14, 15, 16, 17, 18, 19))

            def side(b, q, c):
                if 8 * q + c in slots[b]:
                    prepare(b, slots[b].index(8 * q + c))
                elif b == 0:
                    if (q, c) == (0, 0):
                        h_lo(3, 1, X0)
                    elif (q, c) == (2, 4):
                        link(v.tensor_scalar(LT2[:, :, :], LG[:, :, :], 0.0, None, ALU.min))
                        dve.wait_ge(log_sp, 1)
                        link(v.tensor_tensor(LG[:, :, :], LT2[:, :, :], LT1[:, :, :], ALU.subtract))
                    elif q == 2:
                        rope(c - 5)
                    elif (q, c) == (3, 0):
                        rope(3)
                    elif (q, c) in ((3, 2), (3, 4)):
                        ret_weigh((c - 2) // 2)
                    elif (q, c) in ((4, 1), (4, 3)):
                        ret_weigh(2 + c // 2)
                    elif q == 5 and c >= 4:
                        head_recip(0, c - 4)
                else:
                    if q == 0 and c < 3:
                        head_scale(0, c)
                    elif (q, c) == (2, 4):
                        output_lo(0)
                    elif (q, c) == (2, 5):
                        for hd in range(HEADS):
                            ins = v.tensor_tensor_scan(GI[:, hd, :], ROW1[:, :], LG[:, hd, :], 0.0, ALU.mult, ALU.add)
                        link(ins)
                    elif (q, c) == (2, 6):
                        gi = GI[:, :, :].rearrange("p m (c t) -> p (m c) t", c=NC)
                        v.tensor_tensor(GD[:, :, :].rearrange("p m (c t) -> p (m c) t", c=NC), gi,
                                        gi[:, :, 63:64].to_broadcast([P, HEADS * NC, CL]), ALU.subtract)
                        v.tensor_tensor(GMD[:, :], GI[:, :, 191:192].rearrange("p a b -> p (a b)"),
                                        GI[:, :, 63:64].rearrange("p a b -> p (a b)"), ALU.subtract)\
                            .then_inc(gdec_in, 1)
                    elif (q, c) == (3, 1):
                        dve.wait_ge(gdec_exp, 3)
                        v.scalar_tensor_tensor(out=BR[:, 1, 0:4, :], in0=BR[:, 1, 0:4, :], scalar=DK ** -0.5,
                                               in1=GI[:, :, :], op0=ALU.mult, op1=ALU.mult)
                    elif (q, c) == (3, 2):
                        v.tensor_tensor(BR[:, 1, 4:8, :], BR[:, 1, 4:8, :], GD[:, :, :], ALU.mult).then_inc(gqk, 1)
                    elif (q, c) == (3, 3):
                        link(v.memset(GSC[:, :, :, :], 0.0))
                    elif q == 4 and c % 2 == 0:
                        gla_mask(c // 2)
                    elif q == 5 and c >= 4:
                        head_recip(1, c - 4)
                    elif q == 6 and c < 3:
                        head_scale(1, c)
                    elif (q, c) == (6, 5):
                        output_lo(1)

            for b in range(2):
                for q in range(6 + 2 * b):
                    s = p % 2
                    for c in range(8):
                        tick(S_QKVG + 48 * b + 8 * q + c)
                        side(b, q, c)
                    if q in (4, 5):
                        dve.wait_ge(g_sig, 2 * b + q - 3)
                        v.tensor_tensor(BR[:, b, 4 * q:4 * q + 4, :], DP[s][:, :, :], SG[:, :, :], ALU.mult)\
                            .then_inc(set_free[s], 1)
                    if (b, q) == (1, 5):
                        panel_read(dve, p)
                        v.memset(UBUF[:, :, 0:1], 0.0).then_inc(shift_out, 1)
                    if q >= 6:
                        shift(p, lambda m: KRV[:, 2 * MT + 4 * (q - 6) + m, :],
                              lambda m: prmc("mu", 2 * MT + 4 * (q - 6) + m))
                    p += 1
            count_reg = dve.alloc_register("count")
            for b in range(2):
                base = S_GB + 48 * b
                with dve.Fori(0, 4) as i:
                    steps.enter(i, IN_SQUARE)

                    def rank(value, per=1):
                        return lin(per * 4 * b + value, per, i)

                    def pair(x, k0):
                        return x[:, bass.ds(k0 + 4 * b + i, 1), :].rearrange("p a b -> p (a b)")

                    def masked_wait(s, count):
                        dve.reg_mov(count_reg, count)
                        dve.wait_ge(masks_set, 1)
                        dve.wait_ge(s, count_reg)

                    for k in range(12):
                        if k == 0:
                            masked_wait(bgram, rank(1))
                            for c in range(NC):
                                g = BK[c][:, :].rearrange("p (e x t) -> p e x t", e=2, x=2)
                                u = slice(2 * c, 2 * c + 2)
                                v.copy_predicated(XT[:, u, :], mask(0, 2), g[:, :, 0, :])
                                v.copy_predicated(ZM[:, u, :], mask(2, 2), g[:, :, 0, :])
                                ins = v.copy_predicated(GRB[:, u, :], mask(1, 2), g[:, :, 1, :])
                            ins.then_inc(bgram_read, 1)
                            dve.wait_ge(bgram_read, rank(1))
                            v.transpose(TM[:, :, :], ZM[:, :, :]).then_inc(t_start, 1)
                        if 2 <= k < 8:
                            lv = k - 1
                            if lv == LEVELS - 1:
                                dve.wait_ge(delta_mm, rank(lv, LEVELS - 1))
                                v.tensor_copy(ZM[0:64, :, 64:P], BK[3][0:64, 0:2 * P]
                                              .rearrange("p (u t) -> p u t", u=4)).then_inc(t_grown, 1)
                                tick(base + k, 12, i)
                                continue
                            if lv > IN_SQUARE:
                                dve.wait_ge(delta_mm, rank(lv, LEVELS - 1))
                                for j in range(2):
                                    early, late = sides(j)
                                    v.tensor_copy(TM[late, :, early],
                                                  BK[2][late, 0:P].rearrange("p (u t) -> p u t", u=4))
                                    z = v.tensor_copy(ZM[early, :, late],
                                                      BK[3][early, 0:P].rearrange("p (u t) -> p u t", u=4))
                                z.then_inc(t_grown, 1)
                                tick(base + k, 12, i)
                                continue
                            masked_wait(delta_mm, rank(lv, LEVELS - 1))
                            z = v.copy_predicated(half(ZM[:, :, :], lv, 1), half_mask(2 + lv, lv, 1),
                                                  packed(BK[3], lv))
                            link(z)
                            v.transpose(TM[:, :, :], ZM[:, :, :]).then_inc(t_grown, 1)
                        if k == 9:
                            dve.wait_ge(s_mm, rank(1))
                            for e in range(2):
                                w = slice(64 * e, 64 * e + 64)
                                ins = v.tensor_scalar(SB[w, w], BK[2][w, w], ES[w, bass.ds(4 * b + i, 1)], None,
                                                      ALU.mult)
                            ins.then_inc(s_read, 1)
                        tick(base + k, 12, i)
                        if k == 0:
                            masked_wait(kgram, rank(1))
                            for c in range(NC):
                                g = BK[2 + c][:, :].rearrange("p (e x t) -> p e x t", e=2, x=2)
                                u = slice(2 * c, 2 * c + 2)
                                v.copy_predicated(LAK[:, u, :], mask(0, 2), g[:, :, 0, :])
                                ins = v.copy_predicated(GRK[:, u, :], mask(1, 2), g[:, :, 1, :])
                            ins.then_inc(kgram_read, 1)
                        if k == 10:
                            dve.wait_ge(mean_mm, rank(2))
                            v.scalar_tensor_tensor(out=pair(KRV, MT), in0=BK[0][:, 0:T], scalar=-1.0 / 64,
                                                   in1=YS[:, :], op0=ALU.mult, op1=ALU.add).then_inc(centred, 1)
                            v.tensor_tensor(pair(KRV, 2 * MT), BK[1][:, 0:T], pair(KRV, 2 * MT), ALU.mult)\
                                .then_inc(bonus_done, 1)
                        if k == 11:
                            s = (p + 1) % 2
                            dve.wait_ge(chunk_done, lin(base + 12, 12, i))
                            mg = MG[:, bass.ds(4 * i, 4), :]
                            if b == 0:
                                v.tensor_tensor(mg, DP[s][:, :, :], mg, ALU.mult).then_inc(set_free[s], 1)
                            else:
                                v.tensor_tensor(GT1[:, :, :], DP[s][:, :, :], GT1[:, :, :], ALU.mult)\
                                    .then_inc(set_free[s], 1)
                                dve.wait_ge(set_free[s], lin((p + 1) // 2 + 2, 1, i))
                                v.tensor_tensor(mg, mg, GT1[:, :, :], ALU.add).then_inc(merged, 1)
                steps.leave(4)
                p += 8
            y = KRV[:, MT:2 * MT, :]
            for q in range(4):
                for c in range(8):
                    tick(S_RW + 8 * q + c)
                    if q == 0 and c < 4:
                        dve.wait_ge(gn_root, 1)
                        link(v.reciprocal(RT8[:, 2 * c:2 * c + 2, :], RT8[:, 2 * c:2 * c + 2, :]))
                    elif (q, c) == (0, 4):
                        link(v.tensor_tensor(y, y, RT8[:, :, :], ALU.mult))
                    elif q == 0 and c in (5, 6):
                        for t in range(4 * (c - 5), 4 * (c - 4)):
                            ins = v.tensor_scalar(KRV[:, MT + t, :], KRV[:, MT + t, :], prmc("ln_w", t),
                                                  prmc("ln_b", t), ALU.mult, ALU.add)
                        link(ins)
                    elif (q, c) == (0, 7):
                        link(v.tensor_tensor(y, y, KRV[:, 2 * MT:3 * MT, :], ALU.add))
                    elif (q, c) == (1, 0):
                        dve.wait_ge(g_read, 8)
                        v.tensor_tensor(y, y, GG[:, :, :], ALU.mult).then_inc(orw, 1)
                    elif (q, c) == (1, 4):
                        dve.wait_ge(orw, 2)
                        v.tensor_tensor(OPR[1][:, :, :], y, OPR[0][:, :, :].bitcast(F32), ALU.subtract)\
                            .then_inc(orw_lo, 1)
                p += 1
            for q in range(4):
                t = slice(4 * q, 4 * q + 4)
                for c in range(4):
                    tick(S_RW + 32 + 4 * q + c)
                dve.wait_ge(chunk_done, S_RW + 32 + 4 * q + 4)
                v.tensor_tensor(GTM[:, :, :], DP[p % 2][:, :, :], GB[:, t, :], ALU.mult).then_inc(set_free[p % 2], 1)
                dve.wait_ge(set_free[p % 2], p // 2 + 2)
                v.tensor_tensor(MG[:, t, :], MG[:, t, :], GTM[:, :, :], ALU.add).then_inc(merged, 1)
                dve.wait_ge(mg_hi, q + 1)
                v.tensor_tensor(HL[:, t, :], MG[:, t, :], HH[:, t, :].bitcast(F32), ALU.subtract).then_inc(mg_lo, 1)
                p += 1
            dve.wait_ge(x_again, 16)
            for q in range(4):
                for c in range(8):
                    tick(S_O + 8 * q + c)
                    if q == 3 and c in (2, 4, 6):
                        h_lo(c // 2 - 1, 2, SQ)
                dve.wait_ge(chunk_done, S_O + 8 * q + 8)
                residual(p, q, "ffn")
                p += 1

            def conv(w, i, pc, n, step):
                tiles = 1 if w == 21 else 2

                def par(name, m):
                    return PRM[:, bass.ds((0 if i is None else 4 * i) + 2 * w + m + COL[name][0], 1)]

                dve.wait_ge(chunk_done, lin(n + 1, step, i))
                link(v.tensor_tensor(ZB[:, 0:tiles, 2:], DP[pc % 2][:, 0:tiles, :], norm_n(RS, tiles), ALU.mult))
                for m in range(tiles):
                    ins = v.tensor_scalar(CV[:, m, :], ZB[:, m, 2:T + 2], par("cw2", m), par("cb", m), ALU.mult,
                                          ALU.add)
                link(ins)
                for j in (1, 0):
                    for m in range(tiles):
                        ins = v.scalar_tensor_tensor(out=CV[:, m, :], in0=ZB[:, m, j:T + j], scalar=par(f"cw{j}", m),
                                                     in1=CV[:, m, :], op0=ALU.mult, op1=ALU.add)
                    if j == 1:
                        link(ins)
                ins.then_inc(conv_done, 1)

            def act_product(w, i, pc):
                tiles = 1 if w == 21 else 2
                dve.wait_ge(gelu_done, lin(w + 1, 2, i))
                link(v.tensor_tensor(GE[:, 0:tiles, :], GE[:, 0:tiles, :], norm_n(RS, tiles), ALU.mult))
                v.tensor_tensor(AV[:, 0:tiles, :], DP[pc % 2][:, tiles:2 * tiles, :], GE[:, 0:tiles, :], ALU.mult)\
                    .then_inc(set_free[pc % 2], 1)

            def act_low(w, i):
                tiles = 1 if w == 21 else 2
                dve.wait_ge(act_hi, lin(w + 1, 2, i))
                tile = 2 * w if i is None else 2 * w + 4 * i
                v.tensor_tensor(AL[:, bass.ds(tile, tiles), :], AV[:, 0:tiles, :],
                                AH[:, bass.ds(tile, tiles), :].bitcast(F32), ALU.subtract).then_inc(act_lo, 1)

            for c in range(8):
                tick(S_UP + c)
                if c == 0:
                    h_lo(3, 2, SQ)
            reciprocal_root(1, RS)
            link(v.memset(ZB[:, :, 0:2], 0.0))
            with dve.Fori(0, 10) as i:
                steps.enter(i, 8)
                for q in range(2):
                    for c in range(8):
                        tick(S_UP + 8 + 8 * q + c, 16, i)
                        if c == 0:
                            conv(q, i, p + q, S_UP + 8 * q + 7, 16)
                        elif c == 2:
                            act_product(q, i, p + q)
                        elif c == 4:
                            act_low(q, i)
            steps.leave(10)
            p += 20
            for c in range(4):
                tick(S_UP + 168 + c)
                if c == 0:
                    conv(20, None, p, S_UP + 167, 0)
                elif c == 2:
                    act_product(20, None, p)
            p += 1
            for q in range(4):
                for c in range(22):
                    tick(S_DOWN + 22 * q + c)
                    if (q, c) == (0, 0):
                        act_low(20, None)
                    elif (q, c) == (0, 1):
                        conv(21, None, p, S_UP + 171, 0)
                    elif (q, c) == (0, 3):
                        act_product(21, None, p)
                    elif (q, c) == (0, 5):
                        act_low(21, None)
                    elif (q, c) == (0, 15):
                        dve.wait_ge(p_hi, 1)
                        v.tensor_tensor(PXL[:, :, :], PX[:, :, :], PXH[:, :, :].bitcast(F32), ALU.subtract)\
                            .then_inc(p_lo, 1)
                    elif q and c == 3:
                        h_lo(q - 1, 3, SQ)
                dve.wait_ge(chunk_done, S_DOWN + 22 * q + 22)
                residual(p + 1 + q, q, "ple")
            p += 5
            for q in range(4):
                tick(S_PLE + q)
                if q == 1:
                    h_lo(3, 3, SQ)
                p += 1

            def ple_norm(q, pc):
                dve.wait_ge(chunk_done, S_PLE + 12 + 8 * q)
                v.tensor_tensor(GP[:, :, :], DP[pc % 2][:, :, :], norm_n(RS, 4), ALU.mult).then_inc(set_free[pc % 2], 1)

            def ple_add(q):
                t = slice(4 * q, 4 * q + 4)
                dve.wait_ge(ple_sig, q + 1)
                link(v.tensor_tensor(GP[:, :, :], GP[:, :, :], PG[:, t, :], ALU.mult))
                v.tensor_tensor(XR[:, t, :], XR[:, t, :], GP[:, :, :], ALU.add).then_inc(ple_used, 1)

            def final_gain(g):
                dve.wait_ge(sq_ready, 12 + g + 1)
                t = slice(4 * g, 4 * g + 4)
                at = COL["fin"][0] + 4 * g
                link(v.tensor_tensor(XR[:, t, :], XR[:, t, :], bcast(PRM[:, at:at + 4], T), ALU.mult))

            for q in range(4):
                for c in range(8):
                    tick(S_PLE + 4 + 8 * q + c)
                    if q and c == 0:
                        ple_norm(q - 1, p - 1)
                    elif q and c == 3:
                        ple_add(q - 1)
                    elif q and c == 6:
                        final_gain(q - 1)
                if q == 0:
                    reciprocal_root(2, RS)
                p += 1
            ple_norm(3, p - 1)
            ple_add(3)
            dve.wait_ge(sq_ready, 16)
            link(v.tensor_tensor(SQ[:, 12:14, :], SQ[:, 12:14, :], SQ[:, 14:16, :], ALU.add))
            v.tensor_tensor(SQ[:, 12, :], SQ[:, 12, :], SQ[:, 13, :], ALU.add).then_inc(sq_added, 1)
            final_gain(3)
            dve.wait_ge(rs_root, 4)
            v.reciprocal(RS[:, :], RS[:, :]).then_inc(rs_last, 1)
            dve.wait_ge(rs_last, 1)
            for g in (0, 2, 3):
                t = slice(4 * g, 4 * g + 4)
                v.tensor_tensor(XR[:, t, :], XR[:, t, :], norm_n(RS, 4), ALU.mult).then_inc(out_ready[g], 1)

        @block.gpsimd
        def _(pool):
            gp = nc.gpsimd
            pool.dma_start(CST[:, :, :], const).then_inc(prm_loaded[1], 16)
            pool.dma_start(MSKI[:, :, :], masks).then_inc(prm_loaded[2], 16)
            pool.dma_start(PI32[:, :], pos).then_inc(pos_loaded, 16)

            def add_squares(k, g, sq):
                t = 4 * g
                pool.wait_ge(sq_ready, 4 * k + g + 1)
                gp.tensor_tensor(sq[:, t:t + 2, :], sq[:, t:t + 2, :], sq[:, t + 2:t + 4, :], ALU.add)\
                    .then_inc(sq_pairs, 1)
                pool.wait_ge(sq_pairs, 4 * k + g + 1)
                gp.tensor_tensor(sq[:, t, :], sq[:, t, :], sq[:, t + 1, :], ALU.add).then_inc(sq_added, 1)

            def add_head_squares(b):
                pool.wait_ge(on_sq, b + 1)
                gp.tensor_tensor(BR[:, b, 8:12, :], BR[:, b, 8:12, :], BR[:, b, 12:16, :], ALU.add)\
                    .then_inc(on_added, 1)

            for k in range(4):
                add_squares(0, k, SQ0)
            pool.wait_ge(prm_loaded[2], 16)
            gp.tensor_copy(MSK[:, :, :], MSKI[:, :, :]).then_inc(masks_set, 1)
            pool.wait_ge(ssq_done, 1)
            pool.dma_start(LORA[:, 0:3, :], lora[:, 0:3, :]).then_inc(lora_loaded, 16)
            pool.wait_ge(rw_prep, 1)
            pool.dma_start(DM[:, :, :], dmask).then_inc(dm_loaded, 16)
            for b in range(2):
                add_head_squares(b)
            pool.wait_ge(op_lo, 2)
            for x, s in ((XT, zeroed), (LAK, zeroed), (GRB, zeroed), (GRK, zeroed),
                         (UP, zeroed), (VP, zeroed), (SB, zeroed), (P1S, zeroed), (BS, vt_mm), (AR, y_mm), (PR, mean_mm),
                         (YS, bonus_done), (SQS, var_read), (RH, merged)):
                gp.memset(x[tuple(slice(None) for _ in x.shape)], 0.0).then_inc(s, 1)
            pool.wait_ge(zeroed, 8)
            pool.wait_ge(rw_prep, 2)
            for b in range(2):
                pool.wait_ge(shift_out, 7 + b)
                with pool.Fori(0, 4) as i:
                    def rank(value, per=1):
                        return lin(per * 4 * b + value, per, i)

                    def pair(x, k0, rows=slice(None), cols=slice(None)):
                        return x[rows, bass.ds(k0 + 4 * b + i, 1), cols].rearrange("p a b -> p (a b)")

                    pool.wait_ge(vt_mm, rank(1))
                    gp.tensor_copy(BS[:, :], pair(RWB, 0)).then_inc(staged, 1)
                    gp.tensor_copy(KS[:, :], pair(KRV, 0)).then_inc(staged, 1)
                    gp.tensor_copy(VS[:, :], pair(KRV, 2 * MT)).then_inc(staged, 1)
                    pool.wait_ge(staged, rank(3, STAGED))
                    own = BLK[:, 0:P:64].unsqueeze(2).to_broadcast([P, 2, T])
                    for x, src in ((BP, BS), (KP, KS)):
                        gp.tensor_tensor(x[:, :, :], src[:, :].unsqueeze(1).to_broadcast([P, 2, T]), own, ALU.mult)\
                            .then_inc(staged, 1)
                    pool.wait_ge(y_mm, rank(1))
                    gp.tensor_copy(AR[:, :, 0, :], pair(RWA, 0).rearrange("p (c t) -> p c t", c=NC)).then_inc(staged, 1)
                    gp.tensor_copy(AR[:, :, 1, :], pair(KRV, MT).rearrange("p (c t) -> p c t", c=NC))\
                        .then_inc(staged, 1)
                    gp.tensor_copy(ZM[:, :, :], IDENT.unsqueeze(1).to_broadcast([P, 4, P])).then_inc(staged, 1)
                    pool.wait_ge(mean_mm, rank(1))
                    gp.tensor_copy(RKC, PRM[:, bass.ds(COL["r_k"][0] + 4 * b + i, 1)]).then_inc(rk_staged, 1)
                    pool.wait_ge(staged, rank(STAGED, STAGED))
                    gp.tensor_tensor(PR[:, :].rearrange("p (c t) -> p c t", c=NC), AR[:, :, 1, :],
                                    KS[:, :].rearrange("p (c t) -> p c t", c=NC), ALU.mult).then_inc(rk_staged, 1)
                    pool.wait_ge(rk_staged, rank(2, 3))
                    gp.tensor_tensor(PR[:, :], PR[:, :], RKC.to_broadcast([P, T]), ALU.mult).then_inc(rk_staged, 1)
            pool.wait_ge(chunk_done, S_GB + 48)
            pool.dma_start(G2[:, :, :], lora[:, 3:5, :]).then_inc(g2_loaded, 16)
            pool.wait_ge(gn_root, 1)
            pool.dma_start(XR[:, :, :], xT).then_inc(x_again, 16)
            for k in range(4):
                add_squares(1, k, SQ)
            pool.wait_ge(act_lo, 22)
            pool.dma_start(PX[:, :, :], pT).then_inc(p_loaded, 16)
            for k in range(4):
                add_squares(2, k, SQ)
            for k in range(3):
                add_squares(3, k, SQ)
            pool.wait_ge(rs_last, 1)
            gp.tensor_tensor(XR[:, 4:8, :], XR[:, 4:8, :], RS[:, :].unsqueeze(1).to_broadcast([P, 4, T]), ALU.mult)\
                .then_inc(out_ready[1], 1)


def _layout(inputs):
    f = lambda k: np.asarray(inputs[k])[0]

    def rows(w, cols):
        w = w[:, cols]
        kt = -(-w.shape[0] // (2 * P)) * 2
        full = np.zeros((kt * P, 512), np.float32)
        full[:w.shape[0], :w.shape[1]] = w
        return full.reshape(kt // 2, 2, P, 512).transpose(0, 2, 1, 3).reshape(kt // 2, P, CH)

    def sl(a, n):
        return slice(a, a + n)

    w = f("w_in")
    up, down, wo = f("w_up"), f("w_down"), f("w_o")
    parts = [rows(np.concatenate([w[:, sl(RWKV0 + 3 * MW, 288)], w[:, sl(RWKV0 - GLA_LORA, GLA_LORA)]], 1),
                  slice(None))]
    for base in (RWKV0 + MW, RWKV0):
        parts += [rows(w, sl(base + 512 * j, 512)) for j in range(2)]
    for base in (RET0, GLA0):
        parts += [rows(w, sl(base + 512 * j, 512)) for j in range(6)]
    parts += [rows(w, sl(RWKV0 + 2 * MW + 512 * j, 512)) for j in range(2)]
    for gate, br in ((2, "w_br_ret"), (0, "w_br_gla")):
        for j in range(4):
            parts += [rows(w, sl(GATE0 + gate * D + 512 * j, 512)), rows(f(br), sl(512 * j, 512))]
    parts += [rows(w, sl(GATE0 + D + 512 * j, 512)) for j in range(4)]
    parts += [rows(f("w_br_rwkv"), sl(512 * j, 512)) for j in range(4)]
    parts += [rows(wo, sl(512 * j, 512)) for j in range(4)]
    for j in range(21):
        parts.append(rows(np.concatenate([up[:, sl(256 * j, 256)], up[:, sl(DFF + 256 * j, 256)]], 1), slice(None)))
    last = np.concatenate([up[:, sl(256 * 21, P)], up[:, sl(DFF + 256 * 21, P)]], 1)
    parts.append(last.reshape(4, 4, P, 256).transpose(0, 2, 1, 3).reshape(4, P, CH))
    parts += [rows(down, sl(512 * j, 512)) for j in range(4)]
    parts += [rows(f("w_ple_proj"), sl(512 * j, 512)) for j in range(4)]
    parts += [rows(f("w_ple_gate"), sl(512 * j, 512)) for j in range(4)]
    stream = np.concatenate(parts, 0)

    def col(x, n):
        x = np.asarray(x).reshape(-1)
        full = np.zeros(n * P, np.float32)
        full[:x.size] = x
        return full.reshape(n, P).T

    mu = f("rwkv_mu")
    mu = np.concatenate([mu[MW:2 * MW], mu[:MW], mu[2 * MW:]])
    invf = (np.float32(10000.0) ** (-np.arange(0, DK, 2, dtype=np.float32) / np.float32(DK))).astype(np.float32)
    cw = f("conv_w")
    cols = dict(mix=f("mix_norm"), ffn=f("ffn_norm"), ple=f("ple_norm"), fin=inputs["final_norm"], mu=mu,
                w0=f("rwkv_w0"), a0=f("rwkv_a0"), k_k=f("rwkv_k_k"), k_a=f("rwkv_k_a"), r_k=f("rwkv_r_k"),
                ln_w=f("rwkv_ln_w"), ln_b=f("rwkv_ln_b"), bdec=f("gla_b_decay"), gnorm=f("gla_norm"), cw0=cw[0],
                cw1=cw[1], cw2=cw[2], cb=f("conv_b"), invf=np.concatenate([invf, invf]), pad=np.zeros(1, np.float32))
    prm = np.concatenate([col(cols[n], k) for n, k in _COLS], 1)

    lora = np.zeros((P, 5, MW), np.float32)
    lora[0:64, 0] = f("rwkv_w2")
    lora[64:128, 1] = f("rwkv_a2")
    lora[32:48, 2, 0:512] = f("gla_w_decay")
    g2 = f("rwkv_g2")
    lora[:, 3] = g2[0:P]
    lora[0:32, 4] = g2[P:]

    a, b = np.arange(P)[:, None], np.arange(P)[None, :]
    const = np.zeros((P, 4, P), np.float32)
    const[:, 0] = a == b
    const[:, 1] = a // 64 == b // 64
    const[:, 2] = 1.0
    const[:, 3] = np.where(a == (b + 64) % P, np.where(b < 64, -1.0, 1.0), 0.0)
    masks = np.zeros((P, 7, P), np.int32)
    masks[:, 0] = a < b
    masks[:, 1] = a <= b
    for lv in range(IN_SQUARE + 1):
        m = 2 ** lv
        same = a // (2 * m) == b // (2 * m)
        masks[:, 2 + lv] = same & (a % (2 * m) < m) & (b % (2 * m) >= m)
    gamma = 1.0 - 2.0 ** (-5.0 - np.arange(HEADS))
    diff = np.arange(T)[None, :] - a
    dm = np.stack([np.where(diff >= 0, gm ** np.maximum(diff, 0), 0.0) * DK ** -0.5 for gm in gamma], 1)
    dmask = np.concatenate([dm, dm[:, :, 0:P]], 2).astype(np.float32)

    def chan(x, n):
        return np.asarray(x).T.reshape(n, P, T).transpose(1, 0, 2)

    return dict(stream=stream, xT=chan(inputs["x"][0], DT), prm=prm, const=const, masks=masks, dmask=dmask,
                pos=np.broadcast_to(np.asarray(inputs["positions"]).reshape(1, T), (P, T)), lora=lora,
                pT=chan(f("p")[0], 2))


def kernel(**inputs):
    import concourse.bacc as bacc
    from concourse.bass_utils import run_bass_kernel_spmd

    nc = bacc.Bacc("TRN2", target_bir_lowering=False, num_devices=1)
    arrays, args = {}, []
    for name, x in _layout(inputs).items():
        x = np.ascontiguousarray(x)
        arrays[f"in_{name}"] = x
        args.append(nc.dram_tensor(f"in_{name}", x.shape, mybir.dt.from_np(x.dtype), kind="ExternalInput").ap())
    out = nc.dram_tensor("out", (P, DT, T), F32, kind="ExternalOutput").ap()
    bass_hybrid_block(nc, *args, out)
    got = run_bass_kernel_spmd(nc, [arrays], core_ids=[0]).results[0]["out"]
    return np.ascontiguousarray(got.transpose(2, 1, 0).reshape(1, T, D))
```
